# Optimizing a Trainium2 kernel written in Bass

```python
import jax, jax.numpy as jnp
from jax import lax
import numpy as np

D_MODEL = 1024
BATCH = 1
SEQ = 512
DEPTH = 1

GRID_W = 64
CTX_LEN = 256
D_CONV = 512
CONV_W = 3
D_RWKV = 512
HEAD_SIZE = 64
N_RWKV_HEADS = D_RWKV // HEAD_SIZE
D_MIX = D_CONV + D_RWKV
D_DECAY_LORA = 64
D_AAA_LORA = 64
D_GATE_LORA = 128
COL_SIZES = (D_CONV, D_CONV, D_CONV, D_RWKV, D_RWKV, D_RWKV, D_GATE_LORA, D_DECAY_LORA, D_DECAY_LORA, D_AAA_LORA, D_AAA_LORA)
COL_SPLITS = (512, 1024, 1536, 2048, 2560, 3072, 3200, 3264, 3328, 3392)
D_IN_PROJ = 3 * D_CONV + 3 * D_RWKV + D_GATE_LORA + 2 * D_DECAY_LORA + 2 * D_AAA_LORA
N_KEYS = 128
N_EXPERTS = N_KEYS * N_KEYS
PEER_HEADS = 8
PEER_TOPK = 16
D_QUERY = 256
D_HALF = D_QUERY // 2
PEER_CHUNK = 128
NORM_EPS = 1e-6
LNX_EPS = 64e-5

kernel_name = 'hybrid_conv_rwkv7_peer_dit_layer'

def _rmsnorm(x, g):
    xf = x.astype(jnp.float32)
    xf = xf * lax.rsqrt(jnp.mean(xf * xf, axis=-1, keepdims=True) + NORM_EPS)
    return xf.astype(x.dtype) * g

def _modulate(h, shift, scale):
    return h * (1 + scale) + shift

def _neighbours(z):
    pad = [(0, 0)] * (z.ndim - 2) + [(1, 1), (0, 0)]
    zp = jnp.pad(z, pad)
    return zp[..., :-2, :], zp[..., 2:, :]

def _conv3(z, w):
    prev, nxt = _neighbours(z)
    return w[0] * prev + w[1] * z + w[2] * nxt

def _token_shift(z, mu_prev, mu_next):
    prev, nxt = _neighbours(z)
    return z + mu_prev * (prev - z) + mu_next * (nxt - z)

def _wkv_scan(s0, r, w, k, v, kk, a, reverse):
    xs = tuple(jnp.moveaxis(z, 1, 0) for z in (r, w, k, v, kk, a))

    def step(s, inp):
        r_t, w_t, k_t, v_t, kk_t, a_t = inp
        sa = jnp.einsum('bhvk,bhk->bhv', s, kk_t)
        s = (s * w_t[:, :, None, :]
             - sa[..., :, None] * (kk_t * a_t)[:, :, None, :]
             + v_t[..., :, None] * k_t[:, :, None, :])
        return s, jnp.einsum('bhvk,bhk->bhv', s, r_t)

    s_fin, ys = lax.scan(step, s0, xs, reverse=reverse)
    return s_fin, jnp.moveaxis(ys, 0, 1)

def _token_mixer(h, s0_fwd, s0_bwd, on_grid, with_output, w_in, w_out, conv_w, tshift_mu,
                 decay_w0, decay_w2, iclr_a0, iclr_a2, gate_w2, k_k, k_a, r_k, lnx_g, lnx_b):
    bsz, length, _ = h.shape
    (xb, xc_gate, xc, r, k, v, g_lo, wf_lo, wb_lo, af_lo, ab_lo) = jnp.split(h @ w_in, COL_SPLITS, axis=-1)

    def heads(z):
        return z.astype(jnp.float32).reshape(bsz, length, N_RWKV_HEADS, HEAD_SIZE)

    r = _token_shift(r, tshift_mu[0, 0], tshift_mu[1, 0])
    k = _token_shift(k, tshift_mu[0, 1], tshift_mu[1, 1])
    v = _token_shift(v, tshift_mu[0, 2], tshift_mu[1, 2])
    r_h, k_h, v_h = heads(r), heads(k), heads(v)
    kk = k_h * k_k.astype(jnp.float32).reshape(N_RWKV_HEADS, HEAD_SIZE)
    kk = kk * lax.rsqrt(jnp.sum(kk * kk, axis=-1, keepdims=True) + 1e-12)
    k_a_h = k_a.astype(jnp.float32).reshape(N_RWKV_HEADS, HEAD_SIZE)
    finals, outs = [], []
    for d, (lo_w, lo_a, s0) in enumerate(((wf_lo, af_lo, s0_fwd), (wb_lo, ab_lo, s0_bwd))):
        logw = -jax.nn.softplus(-(decay_w0[d] + jnp.tanh(lo_w) @ decay_w2[d]).astype(jnp.float32)) - 0.5
        decay = heads(jnp.exp(-jnp.exp(logw)))
        a = heads(jax.nn.sigmoid(iclr_a0[d] + lo_a @ iclr_a2[d]))
        k_d = k_h * (1 + (a - 1) * k_a_h)
        s_fin, y_d = _wkv_scan(s0, r_h, decay, k_d, v_h, kk, a, reverse=(d == 1))
        finals.append(s_fin)
        outs.append(y_d)
    if not with_output:
        return None, finals[0], finals[1]
    y = outs[0] + outs[1]
    mu = jnp.mean(y, axis=-1, keepdims=True)
    var = jnp.mean(jnp.square(y - mu), axis=-1, keepdims=True)
    y = ((y - mu) * lax.rsqrt(var + LNX_EPS)).reshape(bsz, length, D_RWKV) * lnx_g + lnx_b
    bonus = jnp.sum(r_h * k_h * r_k.astype(jnp.float32), axis=-1, keepdims=True) * v_h
    y = (y + bonus.reshape(bsz, length, D_RWKV)).astype(h.dtype)
    y_rwkv = y * (jax.nn.sigmoid(g_lo) @ gate_w2)

    z = xc_gate * xc
    if on_grid:
        rows = length // GRID_W
        z = _conv3(z.reshape(bsz, rows, GRID_W, D_CONV), conv_w).reshape(bsz, length, D_CONV)
    else:
        z = _conv3(z, conv_w)
    y_conv = xb * z

    out = jnp.concatenate([y_conv, y_rwkv], axis=-1) @ w_out
    return out, finals[0], finals[1]

def _peer(h, wq, subkeys, u, v):
    bsz, length, dim = h.shape
    chunks = h.reshape(-1, PEER_CHUNK, dim)

    def chunk_fn(hc):
        q = (hc @ wq).reshape(PEER_CHUNK, PEER_HEADS, 2, D_HALF)
        s = jnp.einsum('chsd,hskd->chsk', q, subkeys)
        vals, idx = lax.top_k(s, PEER_TOPK)
        cand = vals[:, :, 0, :, None] + vals[:, :, 1, None, :]
        cand_idx = idx[:, :, 0, :, None] * N_KEYS + idx[:, :, 1, None, :]
        sc, pos = lax.top_k(cand.reshape(PEER_CHUNK, PEER_HEADS, PEER_TOPK * PEER_TOPK), PEER_TOPK)
        ex = jnp.take_along_axis(cand_idx.reshape(PEER_CHUNK, PEER_HEADS, PEER_TOPK * PEER_TOPK), pos, axis=-1)
        g = jax.nn.softmax(sc.astype(jnp.float32), axis=-1).astype(hc.dtype)
        act = jax.nn.gelu(jnp.einsum('chkd,cd->chk', u[ex], hc), approximate=False)
        return jnp.einsum('chk,chkd->cd', g * act, v[ex])

    return lax.map(chunk_fn, chunks).reshape(bsz, length, dim)

def setup_inputs(seed: int = 0) -> dict:
    key = jax.random.key(seed)
    ks = jax.random.split(key, 25)
    L, D = DEPTH, D_MODEL

    def nrm(k, shape, s):
        return jax.random.normal(k, shape, jnp.float32) * s

    return {
        'x': nrm(ks[0], (BATCH, SEQ, D), 1.0),
        'c': nrm(ks[1], (BATCH, D), 1.0),
        'ctx': nrm(ks[2], (BATCH, CTX_LEN, D), 1.0),
        'c_ctx': nrm(ks[3], (D,), 1.0),
        'w_mod': nrm(ks[4], (L, D, 6 * D), 0.5 * D ** -0.5),
        'b_mod': nrm(ks[5], (L, 6 * D), 0.01),
        'norm_gains': 1.0 + nrm(ks[6], (L, 4, D), 0.05),
        'w_in': nrm(ks[7], (L, D, D_IN_PROJ), D ** -0.5),
        'w_out': nrm(ks[8], (L, D_MIX, D), D_MIX ** -0.5),
        'conv_w': nrm(ks[9], (L, CONV_W, D_CONV), CONV_W ** -0.5),
        'tshift_mu': jax.random.uniform(ks[10], (L, 2, 3, D_RWKV), jnp.float32, 0.0, 0.5),
        'decay_w0': jax.random.uniform(ks[11], (L, 2, D_RWKV), jnp.float32, -6.0, 0.0),
        'decay_w2': nrm(ks[12], (L, 2, D_DECAY_LORA, D_RWKV), 0.5 * D_DECAY_LORA ** -0.5),
        'iclr_a0': nrm(ks[13], (L, 2, D_RWKV), 0.5),
        'iclr_a2': nrm(ks[14], (L, 2, D_AAA_LORA, D_RWKV), 0.5 * D_AAA_LORA ** -0.5),
        'gate_w2': nrm(ks[15], (L, D_GATE_LORA, D_RWKV), D_GATE_LORA ** -0.5),
        'k_k': 0.85 + nrm(ks[16], (L, D_RWKV), 0.05),
        'k_a': 1.0 + nrm(ks[17], (L, D_RWKV), 0.05),
        'r_k': nrm(ks[18], (L, N_RWKV_HEADS, HEAD_SIZE), 0.1),
        'lnx_g': 1.0 + nrm(ks[19], (L, D_RWKV), 0.05),
        'lnx_b': nrm(ks[20], (L, D_RWKV), 0.01),
        'peer_wq': nrm(ks[21], (L, D, PEER_HEADS * D_QUERY), D ** -0.5),
        'peer_subkeys': nrm(ks[22], (L, PEER_HEADS, 2, N_KEYS, D_HALF), D_HALF ** -0.5),
        'peer_u': nrm(ks[23], (L, N_EXPERTS, D), D ** -0.5),
        'peer_v': nrm(ks[24], (L, N_EXPERTS, D), D ** -0.5),
    }

def reference(x, c, ctx, c_ctx, w_mod, b_mod, norm_gains, w_in, w_out, conv_w, tshift_mu,
              decay_w0, decay_w2, iclr_a0, iclr_a2, gate_w2, k_k, k_a, r_k, lnx_g, lnx_b,
              peer_wq, peer_subkeys, peer_u, peer_v):
    bsz = x.shape[0]
    s_zero = jnp.zeros((bsz, N_RWKV_HEADS, HEAD_SIZE, HEAD_SIZE), jnp.float32)
    for l in range(DEPTH):
        last = l == DEPTH - 1
        mp = dict(w_in=w_in[l], w_out=w_out[l], conv_w=conv_w[l], tshift_mu=tshift_mu[l],
                  decay_w0=decay_w0[l], decay_w2=decay_w2[l], iclr_a0=iclr_a0[l], iclr_a2=iclr_a2[l],
                  gate_w2=gate_w2[l], k_k=k_k[l], k_a=k_a[l], r_k=r_k[l], lnx_g=lnx_g[l], lnx_b=lnx_b[l])
        ng = norm_gains[l]
        mod_lat = (jax.nn.silu(c) @ w_mod[l] + b_mod[l])[:, None, :]
        sh1, sc1, gt1, sh2, sc2, gt2 = jnp.split(mod_lat, 6, axis=-1)
        mod_ctx = jax.nn.silu(c_ctx) @ w_mod[l] + b_mod[l]
        csh1, csc1, cgt1, csh2, csc2, cgt2 = jnp.split(mod_ctx, 6, axis=-1)

        hc = _modulate(_rmsnorm(ctx, ng[0]), csh1, csc1)
        yc, st_fwd, st_bwd = _token_mixer(hc, s_zero, s_zero, False, not last, **mp)
        hx = _modulate(_rmsnorm(x, ng[0]), sh1, sc1)
        yx, _, _ = _token_mixer(hx, st_fwd, st_bwd, True, True, **mp)
        x = x + gt1 * _rmsnorm(yx, ng[1])
        if not last:
            ctx = ctx + cgt1 * _rmsnorm(yc, ng[1])

        hx = _modulate(_rmsnorm(x, ng[2]), sh2, sc2)
        x = x + gt2 * _rmsnorm(_peer(hx, peer_wq[l], peer_subkeys[l], peer_u[l], peer_v[l]), ng[3])
        if not last:
            hc = _modulate(_rmsnorm(ctx, ng[2]), csh2, csc2)
            ctx = ctx + cgt2 * _rmsnorm(_peer(hc, peer_wq[l], peer_subkeys[l], peer_u[l], peer_v[l]), ng[3])
    return x


_drawn_inputs = setup_inputs


def setup_inputs(seed=0):
    import zlib

    import numpy as np

    out = dict(_drawn_inputs(seed))
    spreads = {}
    factors = {'lnx_b': 5.396}
    for name, (base, spread) in spreads.items():
        noise = np.random.default_rng([zlib.crc32(name.encode()), seed]).standard_normal(out[name].shape)
        drawn = base * np.exp(spread * noise) if base else spread * noise
        out[name] = __import__('jax').numpy.asarray(drawn.astype(out[name].dtype))
    for name, factor in factors.items():
        out[name] = (out[name] * factor).astype(out[name].dtype)
    return out
```

```python
import concourse.bass as bass
from concourse import mybir
from contextlib import ExitStack

F32 = mybir.dt.float32
U32 = mybir.dt.uint32
ALU = mybir.AluOpType
ACT = mybir.ActivationFunctionType
AX = mybir.AxisListType

P = 128
D = 1024
KT = D // P
T = 512
TC = 256
TT = T + TC
NT = T // P
NTC = TC // P
GRID = 64
DH = 64
PAIRS = 4
C = 64
NCH = TT // C
NXC = T // C
NB = 4
D_IN = 3456
NORM_EPS = 1e-6
LNX_EPS = 64e-5
DECAY = 0.6065306597126334
HEADS = 8
KEYS = 128
TOPK = 16
DQ = 256
ROWS = [(0, 1, 16), (1, 1, 8), (2, 1, 5), (3, 1, 4), (4, 1, 3), (5, 3, 2), (8, 8, 1)]
PAIR_STEPS = 40
NCAND = sum(m * w for _, m, w in ROWS)

(MP_R, MP_K, MP_V, MN_R, MN_K, MN_V, W0_F, W0_B, A0_F, A0_B, K_K, K_A, R_K, LNX_G, LNX_B,
 CV0, CV1, CV2) = range(18)
NPAR = 18
(C0_R, C0_K, C0_V, OMKA) = range(18, 22)
NPP = 22

LINKS = 15
RING = 8


def layer(nc, x, c, ctx_in, c_ctx, w_mod, b_mod, norm_gains, w_in, w_out, conv_w, tshift_mu,
          decay_w0, decay_w2, iclr_a0, iclr_a2, gate_w2, k_k, k_a, r_k, lnx_g, lnx_b,
          peer_wq, peer_subkeys, peer_u, peer_v, out):
    with ExitStack() as stack:
        _layer(nc, stack, x, c, ctx_in, c_ctx, w_mod, b_mod, norm_gains, w_in, w_out, conv_w, tshift_mu,
               decay_w0, decay_w2, iclr_a0, iclr_a2, gate_w2, k_k, k_a, r_k, lnx_g, lnx_b,
               peer_wq, peer_subkeys, peer_u, peer_v, out)


def _layer(nc, stack, x, c, ctx_in, c_ctx, w_mod, b_mod, norm_gains, w_in, w_out, conv_w, tshift_mu,
           decay_w0, decay_w2, iclr_a0, iclr_a2, gate_w2, k_k, k_a, r_k, lnx_g, lnx_b,
           peer_wq, peer_subkeys, peer_u, peer_v, out):
    ARENA = 51200
    arena = stack.enter_context(nc.sbuf_tensor("arena", [P, ARENA], F32))
    psum = [stack.enter_context(nc.psum_tensor(f"bank{i}", [P, 512], F32)) for i in range(8)]

    class Cut:

        def __init__(self, at, end=ARENA):
            self.at, self.end = at, end

        def __call__(self, *shape):
            n = 1
            for s in shape:
                n *= s
            a = arena[:, self.at:self.at + n]
            self.at += n
            assert self.at <= self.end, (self.at, self.end)
            if len(shape) == 2:
                a = a.rearrange("p (a b) -> p a b", b=shape[1])
            elif len(shape) == 3:
                a = a.rearrange("p (a b c) -> p a b c", b=shape[1], c=shape[2])
            elif len(shape) == 4:
                a = a.rearrange("p (a b c d) -> p a b c d", b=shape[1], c=shape[2], d=shape[3])
            return a

    def sem(name):
        return stack.enter_context(nc.semaphore(name))

    keep = Cut(0)
    ident = keep(P)
    xn = keep(NT, D)
    head_ones = keep(P)
    mix_diag = keep(P)
    par = keep(PAIRS, NPAR)
    ybmod = keep(64)
    shsc = keep(16, 2)
    ng_col = keep(16)
    eps = keep(4)
    silu_col = keep(KT, 2)
    yconv = keep(PAIRS, T)
    bonus = keep(PAIRS, T)
    gate = keep(PAIRS, T)
    pc_all = keep(2 * PAIRS, NCH)
    KEEP_END = keep.at

    cut = Cut(KEEP_END)
    hT = cut(KT, TT)
    wring = cut(3, KT, P)
    s3 = cut.at
    ctxn = cut(NTC, D)
    wm = cut(KT, 2 * P)
    wm2 = cut(KT, 2 * P)
    wm3 = cut(KT, 2 * P)
    prow = cut(P)
    prow2 = cut(P)
    sq = cut(D)
    xs = cut(2, D)
    pcolA = cut(P)
    pcolB = cut(P)
    cc = cut(2, KT)
    ccs = cut(2, KT)
    ssq = cut(8)
    rstd = cut(8)
    mod1 = cut(16, 2)
    tab = cut(KT, 2)

    cut = Cut(s3)
    lo_w = cut(TT)
    lo_a = cut(TT)
    lo_g = cut(T)
    lora = cut(2, 2, P)
    gw = cut(P)
    kraw = cut(TT + 4)
    vraw = cut(TT + 4)
    rraw = cut(T + 2)
    kS = cut(TT)
    vS = cut(TT)
    rS = cut(T)
    kk = cut(TT)
    sqk = cut(TT)
    sg = cut(TT)
    aa = cut(TT)
    cs = cut(TT)
    ex = cut(TT)
    inc = cut(TT)
    e1 = cut(TT)
    e2 = cut(TT)
    e3 = cut(TT)
    t1 = cut(TT)
    t2 = cut(TT)
    rk = cut(T)
    pp = cut(NPP)
    scan_keep = cut(TT)
    BKb = cut(2, NCH, P)
    KRb = cut(2, NCH, P)
    VSb = cut(NCH, P)
    CO, XO = 1, TC + 3

    cut = Cut(KEEP_END)
    BKs = cut(2, NB, P)
    VSs = cut(2, NB, P)
    BKT = cut(2, NB, P)
    NBD = cut(2, NB, P)
    MBD = cut(2, NB, P)
    ZZ = cut(2, NB, P)
    XX = cut(2, NB, P)
    AA = cut(2, NB, P)
    ysum = cut(PAIRS, NXC, DH)
    LE = cut(3, 2, NB * P)
    LO = cut(3, 2, NB * P)
    QQ = cut(3, 2, NB * P)
    KVP = cut(3, 2, NB * P)
    SV = cut(3, 2, NB * P)
    RB = cut(2, P)
    TMPS = cut(2, P)
    Yb = cut(NXC, 2, 2, DH)
    cut = Cut(ARENA - 2048)
    msk_e = cut(2, P)
    msk_o = cut(2, P)
    lvl = cut(2, 6, P)

    cut = Cut(KEEP_END + 8192)
    H2N = cut(NT, D)
    SC = arena[:, KEEP_END:KEEP_END + (NT + 1) * 2048].rearrange("p (t h k) -> p t h k", h=2 * HEADS, k=KEYS)
    brow = arena[:, KEEP_END:KEEP_END + 7 * D]
    silb = arena[:, KEEP_END + 7 * D:KEEP_END + 8 * D].rearrange("p (k q) -> p k q", q=P)
    ysq = H2N.rearrange("p a b -> p (a b)")[:, 2048:4096].rearrange("p (a x v) -> p a x v", x=NXC, v=DH)
    assert cut.at == KEEP_END + 8192 + 4096
    h2T = cut(KT, T)
    YT = h2T.rearrange("p a b -> p (a b)").rearrange("p (i c) -> p i c", c=P)
    U = cut(RING, D)
    V = cut(RING, D)
    wo = U
    wmr = V.rearrange("p a b -> p (a b)").rearrange("p (s k n) -> p s k n", s=2, k=KT)
    late = cut.at
    yrw = cut(PAIRS, T)
    g1row = cut(D)
    a2row = cut(D)
    sh2row = cut(D)
    tmp5 = cut(D)
    g2row = cut(D)
    st5 = cut(96)
    sh5 = arena[:, KEEP_END:KEEP_END + D]
    cut = Cut(late, late + 2048 + 4 * D)
    h2cur = cut(D)
    ot = cut(D)
    diag = cut(4, P)
    SCs = cut(2, 2, KEYS)
    mr = cut(2, KEYS)
    oh = cut(TOPK, NCAND)
    v16 = cut(2, TOPK)
    i16 = cut(2, TOPK)
    i16f = cut(2, TOPK)
    cand = cut(64)
    cid = cut(64)
    cmr = cut(64)
    iot = cut(64)
    top = cut(TOPK)
    pos = cut(TOPK)
    posf = cut(TOPK)
    exf = cut(TOPK)
    idx = cut(4, TOPK)
    ntop = cut(2)
    prob = cut(TOPK)
    psum_ = cut(2)
    gsm = cut(2, TOPK)
    acts = cut(2, TOPK)
    gel = cut(2, TOPK)
    wts = cut(2, TOPK)
    fst = cut(8)
    fsq = gate.rearrange("p a b -> p (a b)")[:, 0:512]
    dump_ = gate.rearrange("p a b -> p (a b)")[:, 512:512 + D]
    wq2 = yconv.rearrange("p a b -> p (a b)").rearrange("p (s k n) -> p s k n", s=2, k=KT)
    skn = bonus.rearrange("p a b -> p (a b)")[:, 0:256].rearrange("p (s n) -> p s n", s=2)
    skT = bonus.rearrange("p a b -> p (a b)")[:, 256:512].rearrange("p (s n) -> p s n", s=2)
    qT = bonus.rearrange("p a b -> p (a b)")[:, 512:1536].rearrange("p (s n) -> p s n", s=2)

    def v3(a):
        return a.rearrange("p (i c) -> p i c", c=P)

    bk_dram = nc.dram_tensor("bk_scratch", [2 * PAIRS, P, NCH * P], F32, kind="Internal").ap()
    kr_dram = nc.dram_tensor("kr_scratch", [2 * PAIRS, P, NCH * P], F32, kind="Internal").ap()
    vs_dram = nc.dram_tensor("vs_scratch", [PAIRS, P, NCH * P], F32, kind="Internal").ap()

    s_c = sem("cond_loaded")
    s_prow = sem("param_rows_loaded")
    s_x = [sem(f"latents_loaded{i}") for i in range(NT)]
    s_ctx = sem("context_loaded")
    s_wm = [sem(f"wmod_loaded{i}") for i in range(3)]
    s_const = sem("constants_made")
    s_silu = sem("silu_made")
    s_ptr = sem("params_transposed")
    s_pcol = sem("param_columns_made")
    s_mod = sem("mod_products")
    s_modc = sem("mod_columns_made")
    s_ssq = sem("square_sums")
    s_rstd = sem("rstd_made")
    s_dv = sem("vector_steps")
    s_xs = sem("normed_rows")
    s_tr = sem("rows_transposed")
    s_hT = sem("hT_parts")
    s_w = [sem(f"win_loaded{i}") for i in range(3)]
    s_pj = sem("projections_made")
    s_pe = sem("projections_evacuated")
    s_lora = sem("lora_loaded")
    s_ax = sem("aux_products")
    s_ae = sem("aux_evacuated")
    s_sh = sem("shifted")
    s_kk = sem("kk_ready")
    s_cum = sem("decay_sums")
    s_e = sem("decay_factors")
    s_bk = sem("pair_dir_ready")
    s_vs = sem("vs_ready")
    s_spill = sem("spilled")
    s_vw = sem("v_halves")
    s_pz = sem("pads_zeroed")
    s_pp = sem("pair_params")
    s_bn = sem("bonus_product_in")
    s_cv = sem("conv_steps")
    s_bd = sem("bonus_made")
    s_done3 = sem("stage3_vector_done")
    s_mask = sem("masks_made")
    s_bkl = [sem(f"bk_loaded{d}") for d in range(2)]
    s_vsl = [sem(f"vs_loaded{d}") for d in range(2)]
    s_krl = [sem(f"kr_loaded{i}") for i in range(6)]
    s_nz = sem("n_zeroed")
    s_mk = [sem(f"chunk_products{d}") for d in range(2)]
    s_ac = [sem(f"chunk_scalar_moves{d}") for d in range(2)]
    s_vc = [sem(f"chunk_vector_moves{d}") for d in range(2)]
    s_zt = [sem(f"inverse_products{d}") for d in range(2)]
    s_pl = [sem(f"inverse_started{d}") for d in range(2)]
    s_c1 = [sem(f"state_read{d}") for d in range(2)]
    s_rb = [sem(f"state_read_split{d}") for d in range(2)]
    s_y1 = [sem(f"y_from_state{d}") for d in range(2)]
    s_c2 = [sem(f"chunk_applied{d}") for d in range(2)]
    s_tm = [sem(f"state_decayed{d}") for d in range(2)]
    s_st = [sem(f"state_written{d}") for d in range(2)]
    s_y2 = [sem(f"y_from_chunk{d}") for d in range(2)]
    s_ys = sem("y_summed")
    s_br = sem("rows_loaded")
    s_wo = sem("wout_loaded")
    s_wr = [sem(f"wmod_row_weights{i}") for i in range(2)]
    s_sb = sem("silu_spread")
    s_mr = sem("modulation_rows")
    s_me = sem("modulation_rows_moved")
    s_yz = sem("y_transpose_zeroed")
    s_m0 = sem("head_sums")
    s_hn = sem("head_norm_vector")
    s_ha = sem("head_norm_scalar")
    s_yt = sem("y_transposed")
    s_yv = sem("y_affine")
    s_yg = sem("y_gated")
    s_op = sem("mixer_output")
    s_n1 = sem("norm1_scalar")
    s_m1 = sem("norm1_vector")
    s_h2 = sem("h2_rows")
    s_h2t = sem("h2_transposed")
    s_h2e = sem("h2_columns")
    s_wq = [sem(f"wq_loaded{i}") for i in range(2)]
    s_sk = [sem(f"subkeys_loaded{i}") for i in range(2)]
    s_skt = sem("subkeys_transposed")
    s_ske = sem("subkeys_moved")
    s_q = sem("queries")
    s_qe = sem("queries_moved")
    s_s = sem("scores")
    s_se = sem("scores_moved")
    s_io = sem("iota_made")
    s_scs = sem("scores_staged")
    s_lk = sem("topk_links")
    s_tk = sem("experts_chosen")
    s_ex = sem("probabilities_raised")
    s_gs = sem("probabilities")
    s_u = [sem(f"u_rows{i}") for i in range(RING)]
    s_v = [sem(f"v_rows{i}") for i in range(RING)]
    s_dot = sem("dots")
    s_ge = sem("gelus")
    s_wt = sem("expert_weights")
    s_dg = sem("weight_diagonals")
    s_mm = sem("experts_added")
    s_hc = sem("h2_current")
    s_fa = sem("final_scalar")
    s_fv = sem("final_vector")
    s_out = sem("output_stored")
    s_pass_sp, s_pass_dve, s_pass_pool = sem("sync_passed"), sem("vector_passed"), sem("pool_passed")

    block = stack.enter_context(nc.Block())

    x_v = x[0].rearrange("(t p) d -> t p d", p=P)
    ctx_v = ctx_in[0].rearrange("(t p) d -> t p d", p=P)
    wmod_v = w_mod[0].rearrange("(p k) n -> p k n", k=KT)
    win_v = w_in[0].rearrange("(k p) n -> p k n", p=P)

    def credit(engine, semaphore, n):
        engine.sem_inc(semaphore, n)

    def apart(engine, passed):
        engine.sem_inc(passed, 1)

    W1, W2 = [psum[0], psum[2]], [psum[1], psum[3]]
    C1, C2 = [psum[4], psum[6]], [psum[5], psum[7]]
    ORDER = [[0, 1, 2], [0, 2, 1]]
    ITEMS = [[0, 1, 2, 3], [3, 2, 1, 0]]
    LV = 5
    MK = {"bkT": 1, "vT": 2, "kv": 3, "ge": 4, "go": 5, "nT": 6}
    for l in range(LV):
        MK["a", l] = 7 + 3 * l
        if l < LV - 1:
            MK["z", l] = 8 + 3 * l
            MK["x", l] = 9 + 3 * l
    MK["x", LV - 1] = 8 + 3 * (LV - 1)
    MK["q"] = 9 + 3 * (LV - 1)
    NMK = MK["q"]
    AC = {"bkT": 1, "vT": 2, "m": 3, "q": 4}
    NAC = 4
    VC = {"kv": 1, "ge": 2, "go": 3}
    for l in range(LV):
        VC["a", l] = 4 + 3 * l
        if l < LV - 1:
            VC["z", l] = 5 + 3 * l
            VC["x", l] = 6 + 3 * l
    VC["x", LV - 1] = 5 + 3 * (LV - 1)
    NVC = VC["x", LV - 1]
    NPL = 2

    def bcast(m, rows, cols):
        w = cols.stop - cols.start
        return m[rows, cols].unsqueeze(1).broadcast_to([rows.stop - rows.start, NB, w])

    LOW, HIGH, ALL = slice(0, DH), slice(DH, P), slice(0, P)

    def steps4(engine, do, tail):
        do(0, 0, None, True)
        do(0, 1, (0, 0), True)
        do(0, 2, (0, 1), True)
        with engine.Fori(1, PAIRS) as p:
            do(p, 0, (p - 1, 2), False)
            do(p, 1, (p, 0), False)
            do(p, 2, (p, 1), False)
        tail()

    def sync4(sp):
        sp.wait_ge(s_done3, PAIRS + 1)

        def do(p, b, chain, first):
            n = 3 * p + b
            for d in range(2):
                src = slice(ORDER[d][b] * NB * P, (ORDER[d][b] + 1) * NB * P)
                if not (first and b == 0):
                    sp.wait_ge(s_mk[d], NMK * (n - 1) + MK["go"])
                if not first:
                    apart(sp, s_pass_sp)
                    sp.wait_ge(s_c1[d], 12 * (p - 1) + 4 * b + 4)
                    apart(sp, s_pass_sp)
                sp.dma_start(BKs[:, d].rearrange("p a b -> p (a b)"), bk_dram[2 * p + d][:, src]).then_inc(s_bkl[d], 16)
                sp.dma_start(VSs[:, d].rearrange("p a b -> p (a b)"), vs_dram[p][:, src]).then_inc(s_vsl[d], 16)
                sp.dma_start(LE[LOW, b, d, :], kr_dram[2 * p + d][LOW, src]).then_inc(s_krl[2 * b + d], 16)
                sp.dma_start(LO[HIGH, b, d, :], kr_dram[2 * p + d][HIGH, src]).then_inc(s_krl[2 * b + d], 16)
        steps4(sp, do, lambda: None)

    def pool_masks(pool):
        n = [0]

        def put(i):
            n[0] += 1
            i.then_inc(s_mask, 1)
            pool.wait_ge(s_mask, n[0])

        for d in range(2):
            put(nc.gpsimd.memset(msk_e[:, d], 1.0))
            put(nc.gpsimd.memset(msk_o[:, d], 1.0))
            for l in range(6):
                s = 1 << l
                v = lvl[:, d, l].rearrange("p (n h s) -> p n h s", h=2, s=s)
                put(nc.gpsimd.memset(v[:, :, d], 0.0))
                put(nc.gpsimd.memset(v[:, :, 1 - d], 1.0))
        for d in range(2):
            sg_ = 1 - 2 * d
            for tile, ops in ((msk_e, (ALU.is_gt, ALU.is_ge)), (msk_o, (ALU.is_ge, ALU.is_gt))):
                for h in range(2):
                    for rows in (LOW, HIGH):
                        a = tile[rows, d, DH * h:DH * h + DH]
                        put(nc.gpsimd.affine_select(out=a, in_=a, compare_op=ops[h], fill=0.0, base=0,
                                                    pattern=[[sg_, DH]], channel_multiplier=-sg_))
            for l in range(6):
                s = 1 << l
                v = lvl[:, d, l].rearrange("p (n w) -> p n w", w=2 * s)
                put(nc.gpsimd.affine_select(out=v, in_=v, compare_op=ALU.is_ge, fill=0.0, base=-d * s,
                                            pattern=[[-2 * s, P // (2 * s)], [0, 2 * s]], channel_multiplier=1))
        for d in range(2):
            for l in range(6):
                s = 1 << l
                v = lvl[:, d, l].rearrange("p (n w) -> p n w", w=2 * s)
                put(nc.gpsimd.affine_select(out=v, in_=v, compare_op=ALU.is_ge, fill=0.0, base=s - 1 + d * s,
                                            pattern=[[2 * s, P // (2 * s)], [0, 2 * s]], channel_multiplier=-1))
        return n[0]

    def pool4(pool):
        pool.wait_ge(s_done3, PAIRS + 1)
        for d in range(2):
            nc.gpsimd.memset(NBD[:, d], 0.0).then_inc(s_nz, 1)

        def do(p, b, chain, first):
            n = 3 * p + b
            for d in range(2):
                pool.wait_ge(s_vc[d], NVC * n + VC["go"])
                nc.gpsimd.tensor_tensor(ZZ[:, d], NBD[:, d], bcast(lvl[:, d, 0], ALL, ALL), ALU.mult).then_inc(s_zt[d], 1)
                pool.wait_ge(s_zt[d], 2 * n + 1)
                nc.gpsimd.tensor_tensor(ZZ[:, d], ZZ[:, d], bcast(ident, ALL, ALL), ALU.add).then_inc(s_pl[d], 1)
                pool.wait_ge(s_ac[d], NAC * n + AC["m"])
                nc.gpsimd.tensor_tensor(XX[:, d], MBD[:, d], bcast(lvl[:, 1 - d, 0], ALL, ALL), ALU.mult).then_inc(s_zt[d], 1)
                pool.wait_ge(s_zt[d], 2 * n + 2)
                nc.gpsimd.tensor_tensor(XX[:, d], XX[:, d], bcast(ident, ALL, ALL), ALU.add).then_inc(s_pl[d], 1)
        steps4(pool, do, lambda: None)

    def scalar4(act):
        def copies(cp, cb, i, which):
            for d in range(2):
                ci = ITEMS[d][i]
                xc = NB * ORDER[d][cb] + ci - TC // C
                src = [C1, C2][which][d]
                if which == 0:
                    act.wait_ge(s_rb[d], 12 * cp + 4 * cb + i + 1)
                elif (cb, i) == (2, 3):
                    act.wait_ge(s_c2[d], 12 * cp + 12)
                else:
                    act.wait_ge(s_st[d], 11 * cp + 4 * cb + i + 1)
                nc.scalar.activation(Yb[HIGH, xc, d, which, :], src[HIGH, 0:DH], ACT.Identity)
                nc.scalar.activation(Yb[LOW, xc, d, which, :], src[LOW, DH:P], ACT.Identity).then_inc([s_y1, s_y2][which][d], 1)

        def chain_part(chain, i, first):
            cp, cb = chain
            if cb == 0:
                return
            if i == 0 and cb == 1 and not first:
                act.wait_ge(s_ys, cp)
            copies(cp, cb, i, 0)
            copies(cp, cb, i, 1)

        def do(p, b, chain, first):
            n = 3 * p + b
            for d in range(2):
                act.wait_ge(s_mk[d], NMK * n + MK["bkT"])
                nc.scalar.activation(BKT[:, d], v3(W1[d][:, :]), ACT.Identity).then_inc(s_ac[d], 1)
            for d in range(2):
                act.wait_ge(s_mk[d], NMK * n + MK["vT"])
                if not first:
                    act.wait_ge(s_c1[d], 12 * (p - 1) + 4 * b + 4)
                    act.wait_ge(s_st[d], 11 * (p - 1) + min(4 * b + 4, 11))
                nc.scalar.activation(v3(SV[:, b, d]), v3(W2[d][:, :]), ACT.Identity).then_inc(s_ac[d], 1)
            for d in range(2):
                act.wait_ge(s_mk[d], NMK * n + MK["nT"])
                nc.scalar.activation(MBD[:, d], v3(W2[d][:, :]), ACT.Identity).then_inc(s_ac[d], 1)
            for i in range(NB):
                if chain:
                    chain_part(chain, i, first)
            for d in range(2):
                act.wait_ge(s_mk[d], NMK * n + MK["q"])
                if not first:
                    act.wait_ge(s_c2[d], 12 * (p - 1) + 4 * b + 4)
                nc.scalar.activation(v3(QQ[:, b, d]), v3(W2[d][:, :]), ACT.Identity).then_inc(s_ac[d], 1)

        def tail():
            for i in range(NB):
                chain_part((PAIRS - 1, 2), i, False)
        steps4(act, do, tail)

    def vector4(dve):
        def split(cp, cb, i):
            for d in range(2):
                dve.wait_ge(s_c1[d], 12 * cp + 4 * cb + i + 1)
                nc.vector.tensor_tensor(RB[:, d], C1[d][:, 0:P], mix_diag, ALU.mult).then_inc(s_rb[d], 1)
            if (cb, i) == (2, 3):
                return
            for d in range(2):
                ci = ITEMS[d][i]
                c = NB * ORDER[d][cb] + ci
                if not (cb == 0 and i == 0):
                    dve.wait_ge(s_st[d], 11 * cp + 4 * cb + i)
                nc.vector.scalar_tensor_tensor(TMPS[:, d], v3(SV[:, cb, d])[:, ci], pc_all[:, 2 * cp + d, c:c + 1],
                                               v3(KVP[:, cb, d])[:, ci], ALU.mult, ALU.add).then_inc(s_tm[d], 1)

        def advance(cp, cb, i):
            if (cb, i) == (2, 3):
                return
            nb, ni = (cb, i + 1) if i < 3 else (cb + 1, 0)
            for d in range(2):
                ci = ITEMS[d][i]
                c = NB * ORDER[d][cb] + ci
                dst = v3(SV[:, nb, d])[:, ITEMS[d][ni]]
                dve.wait_ge(s_c2[d], 12 * cp + 4 * cb + i + 1)
                dve.wait_ge(s_tm[d], 11 * cp + 4 * cb + i + 1)
                if ni == 0:
                    dve.wait_ge(s_vc[d], NVC * (3 * cp + nb) + VC["kv"])
                for rows, cols in ((LOW, slice(0, DH)), (HIGH, slice(DH, P))):
                    last = nc.vector.scalar_tensor_tensor(dst[rows, cols], C2[d][rows, cols],
                                                          pc_all[rows, 2 * cp + d, c:c + 1], TMPS[rows, d, cols],
                                                          ALU.mult, ALU.add)
                last.then_inc(s_st[d], 1)

        def total(cp):
            for d in range(2):
                dve.wait_ge(s_y1[d], 8 * cp + 8)
                dve.wait_ge(s_y2[d], 8 * cp + 8)
            nc.vector.tensor_reduce(ysum[:, cp], Yb.rearrange("p x d s v -> p x v d s"), AX.XY, ALU.add).then_inc(s_ys, 1)

        def do(p, b, chain, first):
            n = 3 * p + b
            if first and b == 0:
                dve.wait_ge(s_nz, 2)
                dve.wait_ge(s_mask, n_masks)
            for d in range(2):
                dve.wait_ge(s_mk[d], NMK * n + MK["kv"])
                pc = pc_all[:, 2 * p + d, NB * ORDER[d][b]:NB * ORDER[d][b] + NB]
                nc.vector.tensor_tensor(v3(KVP[:, b, d]), v3(W1[d][:, :]), pc.unsqueeze(2).broadcast_to([P, NB, P]),
                                        ALU.mult).then_inc(s_vc[d], 1)
            for d in range(2):
                g = v3(W2[d][:, :])
                dve.wait_ge(s_mk[d], NMK * n + MK["ge"])
                if not (first and b == 0):
                    dve.wait_ge(s_pl[d], NPL * n)
                nc.vector.tensor_tensor(NBD[LOW, d, :, 0:DH], g[LOW, :, 0:DH], bcast(msk_e[:, d], LOW, slice(0, DH)), ALU.mult)
                nc.vector.tensor_tensor(BKT[LOW, d, :, DH:P], g[LOW, :, DH:P], bcast(msk_e[:, d], LOW, slice(DH, P)), ALU.mult)
                nc.vector.tensor_tensor(v3(LE[:, b, d])[HIGH], g[HIGH], bcast(msk_e[:, d], HIGH, ALL), ALU.mult).then_inc(s_vc[d], 1)
            for d in range(2):
                g = v3(W1[d][:, :])
                dve.wait_ge(s_mk[d], NMK * n + MK["go"])
                nc.vector.tensor_tensor(v3(LO[:, b, d])[LOW], g[LOW], bcast(msk_o[:, d], LOW, ALL), ALU.mult)
                nc.vector.tensor_tensor(BKT[HIGH, d, :, 0:DH], g[HIGH, :, 0:DH], bcast(msk_o[:, d], HIGH, slice(0, DH)), ALU.mult)
                nc.vector.tensor_tensor(NBD[HIGH, d, :, DH:P], g[HIGH, :, DH:P], bcast(msk_o[:, d], HIGH, slice(DH, P)),
                                        ALU.mult).then_inc(s_vc[d], 1)
            for l in range(LV):
                for d in range(2):
                    dve.wait_ge(s_mk[d], NMK * n + MK["a", l])
                    nc.vector.tensor_tensor(AA[:, d], v3(W1[d][:, :]), bcast(lvl[:, d, l + 1], ALL, ALL), ALU.mult).then_inc(s_vc[d], 1)
                if chain and l < NB:
                    split(*chain, l)
                for d in range(2):
                    if l < LV - 1:
                        dve.wait_ge(s_mk[d], NMK * n + MK["z", l])
                        nc.vector.tensor_tensor(ZZ[:, d], v3(W2[d][:, :]), ZZ[:, d], ALU.add).then_inc(s_vc[d], 1)
                    dve.wait_ge(s_mk[d], NMK * n + MK["x", l])
                    nc.vector.tensor_tensor(XX[:, d], v3(W1[d][:, :]), XX[:, d], ALU.add).then_inc(s_vc[d], 1)
                if chain and l < NB:
                    advance(*chain, l)
            if chain and chain[1] == 2:
                total(chain[0])

        def tail():
            for i in range(NB):
                split(PAIRS - 1, 2, i)
                advance(PAIRS - 1, 2, i)
            total(PAIRS - 1)
        steps4(dve, do, tail)

    def tensor4(pe):
        def read_state(cp, cb, i, first):
            for d in range(2):
                ci = ITEMS[d][i]
                if not (cb == 0 and i == 0):
                    pe.wait_ge(s_st[d], 11 * cp + 4 * cb + i)
                yc = 8 * cp + max(4 * (cb - 1) + i, 0)
                if not (first and yc == 0):
                    pe.wait_ge(s_y1[d], yc)
                if not (first and cb == 0 and i == 0):
                    pe.wait_ge(s_rb[d], 12 * cp + 4 * cb + i)
                nc.tensor.matmul(C1[d][:, 0:DH], v3(LE[:, cb, d])[:, ci], v3(SV[:, cb, d])[:, ci, 0:DH], start=True, stop=True)
                nc.tensor.matmul(C1[d][:, DH:P], v3(LO[:, cb, d])[:, ci], v3(SV[:, cb, d])[:, ci, DH:P], start=True,
                                 stop=True).then_inc(s_c1[d], 1)

        def apply_chunk(cp, cb, i, first):
            for d in range(2):
                ci = ITEMS[d][i]
                pe.wait_ge(s_rb[d], 12 * cp + 4 * cb + i + 1)
                if i == 0:
                    pe.wait_ge(s_ac[d], NAC * (3 * cp + cb) + AC["q"])
                yc = 8 * cp + max(4 * (cb - 1) + i, 0)
                if not (first and yc == 0):
                    pe.wait_ge(s_y2[d], yc)
                nc.tensor.matmul(C2[d][:, 0:P], v3(QQ[:, cb, d])[:, ci], RB[:, d], start=True, stop=True).then_inc(s_c2[d], 1)

        def four(f, s):
            for i in range(NB):
                m = f(i)
            m.then_inc(s, 1)

        def do(p, b, chain, first):
            n = 3 * p + b
            start = first and b == 0
            for d in range(2):
                pe.wait_ge(s_bkl[d], 16 * n + 16)
                if not start:
                    pe.wait_ge(s_vc[d], NVC * n)
                    pe.wait_ge(s_ac[d], NAC * n)
                four(lambda i: nc.tensor.transpose(W1[d][:, P * i:P * i + P], BKs[:, d, i], ident), s_mk[d])
                pe.wait_ge(s_vsl[d], 16 * n + 16)
                four(lambda i: nc.tensor.transpose(W2[d][:, P * i:P * i + P], VSs[:, d, i], ident), s_mk[d])
            for d in range(2):
                pe.wait_ge(s_ac[d], NAC * n + AC["vT"])
                four(lambda i: nc.tensor.matmul(W1[d][:, P * i:P * i + P], BKT[:, d, i], v3(SV[:, b, d])[:, i],
                                                start=True, stop=True), s_mk[d])
                pe.wait_ge(s_krl[2 * b + d], 32 * p + 32)
                four(lambda i: nc.tensor.matmul(W2[d][:, P * i:P * i + P], BKs[LOW, d, i], v3(LE[:, b, d])[LOW, i],
                                                start=True, stop=True), s_mk[d])
            for d in range(2):
                pe.wait_ge(s_vc[d], NVC * n + VC["kv"])
                four(lambda i: nc.tensor.matmul(W1[d][:, P * i:P * i + P], BKs[HIGH, d, i], v3(LO[:, b, d])[HIGH, i],
                                                start=True, stop=True), s_mk[d])
            for d in range(2):
                pe.wait_ge(s_vc[d], NVC * n + VC["go"])
                four(lambda i: nc.tensor.transpose(W2[d][:, P * i:P * i + P], NBD[:, d, i], ident), s_mk[d])
            for l in range(LV):
                for d in range(2):
                    if l == 0:
                        pe.wait_ge(s_pl[d], NPL * n + 2)
                        pe.wait_ge(s_ac[d], NAC * n + AC["m"])
                    else:
                        pe.wait_ge(s_vc[d], NVC * n + VC["x", l - 1])
                    four(lambda i: nc.tensor.matmul(W1[d][:, P * i:P * i + P], MBD[:, d, i], ZZ[:, d, i],
                                                    start=True, stop=True), s_mk[d])
                if chain and l < NB:
                    read_state(*chain, l, first)
                for d in range(2):
                    pe.wait_ge(s_vc[d], NVC * n + VC["a", l])
                    if l < LV - 1:
                        four(lambda i: nc.tensor.matmul(W2[d][:, P * i:P * i + P], XX[:, d, i], AA[:, d, i],
                                                        start=True, stop=True), s_mk[d])
                    four(lambda i: nc.tensor.matmul(W1[d][:, P * i:P * i + P], AA[:, d, i], XX[:, d, i],
                                                    start=True, stop=True), s_mk[d])
                if chain and l < NB:
                    apply_chunk(*chain, l, first)
            for d in range(2):
                pe.wait_ge(s_vc[d], NVC * n + VC["x", LV - 1])
                four(lambda i: nc.tensor.matmul(W2[d][:, P * i:P * i + P], XX[:, d, i], BKT[:, d, i],
                                                start=True, stop=True), s_mk[d])

        def tail():
            for i in range(NB):
                read_state(PAIRS - 1, 2, i, False)
                apply_chunk(PAIRS - 1, 2, i, False)
        steps4(pe, do, tail)

    wout_v = w_out[0].rearrange("(k p) n -> p k n", p=P)
    wq_v = peer_wq[0].rearrange("(k p) n -> p k n", p=P)
    skey_v = peer_subkeys[0].rearrange("h s k d -> (h s) k d")
    HS = 2 * HEADS

    def sync5(sp):
        sp.wait_ge(s_ys, PAIRS)
        sp.dma_start(brow[:, 0:4 * D], b_mod[0, 2 * D:6 * D].unsqueeze(0).broadcast_to([P, 4 * D])).then_inc(s_br, 16)
        sp.dma_start(brow[:, 4 * D:7 * D], norm_gains[0, 1:4].rearrange("g d -> (g d)").unsqueeze(0)
                     .broadcast_to([P, 3 * D])).then_inc(s_br, 16)
        for u in range(8):
            if u >= 2:
                sp.wait_ge(s_mr, u - 1)
            sp.dma_start(wmr[:, u % 2], wmod_v[:, :, 2 * D + 512 * u:2 * D + 512 * u + 512]).then_inc(s_wr[u % 2], 16)
            if u == 1:
                sp.dma_start(wo, wout_v).then_inc(s_wo, 16)
        sp.wait_ge(s_op, NT)
        for a in range(2):
            sp.dma_start(wq2[:, a], wq_v[:, :, P * a:P * a + P]).then_inc(s_wq[a], 16)
            sp.dma_start(skn[:, a], skey_v[a]).then_inc(s_sk[a], 16)
        with sp.Fori(1, HEADS) as h:
            for a in range(2):
                sp.wait_ge(s_q, 2 * h - 1 + a)
                sp.wait_ge(s_skt, 2 * h - 1 + a)
                sp.dma_start(wq2[:, a], wq_v[:, :, bass.ds(h * (2 * P) + P * a, P)]).then_inc(s_wq[a], 16)
                sp.dma_start(skn[:, a], skey_v[2 * h + a]).then_inc(s_sk[a], 16)

    def pool5(pool):
        pool.wait_ge(s_ys, PAIRS)
        nc.gpsimd.memset(YT, 0.0).then_inc(s_yz, 1)

    def scalar5(act):
        y = ysum.rearrange("p a x v -> p (a x) v")
        act.wait_ge(s_hn, 2)
        nc.scalar.activation(ysq.rearrange("p a x v -> p (a x) v"), y, ACT.Square).then_inc(s_ha, 1)
        act.wait_ge(s_hn, 3)
        nc.scalar.activation(st5[:, 32:64], st5[:, 32:64], ACT.Sqrt, bias=eps[:, 2:3], scale=1.0 / DH).then_inc(s_ha, 1)
        for p in range(PAIRS):
            for b in range(2):
                act.wait_ge(s_yt, 2 * p + b + 1)
                bank = v3(psum[2 * p + b][:, :])
                for rows, cols in ((LOW, slice(DH, P)), (HIGH, slice(0, DH))):
                    o = yrw[rows, p, 256 * b:256 * b + 256].rearrange("p (i c) -> p i c", c=DH)
                    i = nc.scalar.activation(o, bank[rows, :, cols], ACT.Identity, bias=par[rows, p, LNX_B:LNX_B + 1],
                                             scale=par[rows, p, LNX_G:LNX_G + 1])
                i.then_inc(s_yv, 1)
        n = [0]

        def put(i):
            n[0] += 1
            i.then_inc(s_n1, 1)

        for t in range(NT):
            act.wait_ge(s_op, t + 1)
            for h in range(2):
                if n[0]:
                    act.wait_ge(s_n1, n[0])
                put(nc.scalar.activation(tmp5[:, 0:512], psum[2 * t + h][:, :], ACT.Square,
                                         accum_out=st5[:, 64 + 2 * t + h:65 + 2 * t + h]))
        for t in range(NT):
            act.wait_ge(s_m1, 5 * t + 1)
            put(nc.scalar.activation(st5[:, 80 + t:81 + t], st5[:, 76 + t:77 + t], ACT.Sqrt, bias=eps[:, 0:1], scale=1.0 / D))
            act.wait_ge(s_m1, 5 * t + 4)
            put(nc.scalar.activation(yrw.rearrange("p a b -> p (a b)")[:, 0:D], xn[:, t, :], ACT.Square,
                                     accum_out=st5[:, 84 + t:85 + t]))
            act.wait_ge(s_n1, n[0])
            put(nc.scalar.activation(st5[:, 88 + t:89 + t], st5[:, 84 + t:85 + t], ACT.Sqrt, bias=eps[:, 0:1], scale=1.0 / D))
        for t in range(NT):
            for h in range(2):
                act.wait_ge(s_h2t, 2 * t + h + 1)
                nc.scalar.activation(h2T[:, 4 * h:4 * h + 4, P * t:P * t + P], v3(psum[2 * t + h][:, :]),
                                     ACT.Identity).then_inc(s_h2e, 1)
        with act.Fori(0, HEADS) as h:
            for a in range(2):
                act.wait_ge(s_q, 2 * h + a + 1)
                nc.scalar.activation(qT[:, a], psum[a][:, :], ACT.Identity).then_inc(s_qe, 1)

    def vector5(dve):
        n = [0]

        def put(i):
            n[0] += 1
            i.then_inc(s_hn, 1)
            dve.wait_ge(s_hn, n[0])

        dve.wait_ge(s_ys, PAIRS)
        y = ysum.rearrange("p a x v -> p (a x) v")
        nc.vector.tensor_copy(silb, silu_col[:, :, 0:1].broadcast_to([P, KT, P])).then_inc(s_sb, 1)
        nc.vector.tensor_reduce(st5[:, 0:32], y, AX.X, ALU.add).then_inc(s_m0, 1)
        dve.wait_ge(s_m0, 1)
        put(nc.vector.tensor_scalar(st5[:, 0:32], st5[:, 0:32], 1.0 / DH, None, ALU.mult))
        put(nc.vector.tensor_tensor(y, y, st5[:, 0:32].unsqueeze(2).broadcast_to([P, 32, DH]), ALU.subtract))
        dve.wait_ge(s_ha, 1)
        put(nc.vector.tensor_reduce(st5[:, 32:64], ysq.rearrange("p a x v -> p (a x) v"), AX.X, ALU.add))
        dve.wait_ge(s_ha, 2)
        put(nc.vector.reciprocal(st5[:, 32:64], st5[:, 32:64]))
        dve.wait_ge(s_yz, 1)
        rs = st5[:, 32:64].unsqueeze(2).broadcast_to([P, 32, DH])
        nc.vector.tensor_tensor(YT[HIGH, :, 0:DH], y[HIGH], rs[HIGH], ALU.mult)
        put(nc.vector.tensor_tensor(YT[LOW, :, DH:P], y[LOW], rs[LOW], ALU.mult))
        dve.wait_ge(s_br, 32)
        m = [0]
        for u in range(8):
            kind, h = u // 2, u % 2
            row = [g1row, sh2row, a2row, g2row][kind][:, 512 * h:512 * h + 512]
            dve.wait_ge(s_mr, u + 1)
            m[0] += 1
            nc.vector.tensor_tensor(row, psum[u][:, :], brow[:, D * kind + 512 * h:D * kind + 512 * h + 512],
                                    ALU.add).then_inc(s_me, 1)
            if kind != 1:
                dve.wait_ge(s_me, m[0])
                g = {0: 4, 2: 5, 3: 6}[kind]
                m[0] += 1
                nc.vector.scalar_tensor_tensor(row, row, 1.0 if kind == 2 else 0.0,
                                               brow[:, D * g + 512 * h:D * g + 512 * h + 512], ALU.add, ALU.mult).then_inc(s_me, 1)
        for p in range(PAIRS):
            dve.wait_ge(s_yv, 2 * p + 2)
            nc.vector.tensor_tensor(yrw[:, p], yrw[:, p], bonus[:, p], ALU.add).then_inc(s_yg, 1)
            dve.wait_ge(s_yg, 2 * p + 1)
            nc.vector.tensor_tensor(yrw[:, p], yrw[:, p], gate[:, p], ALU.mult).then_inc(s_yg, 1)
        k = [0]

        def link(i):
            k[0] += 1
            i.then_inc(s_m1, 1)
            dve.wait_ge(s_m1, k[0])

        for t in range(NT):
            dve.wait_ge(s_n1, 2 * t + 2 if t == 0 else 8 + 3 * t)
            if t == 0:
                dve.wait_ge(s_n1, 8)
            link(nc.vector.tensor_tensor(st5[:, 76 + t:77 + t], st5[:, 64 + 2 * t:65 + 2 * t], st5[:, 65 + 2 * t:66 + 2 * t], ALU.add))
            dve.wait_ge(s_n1, 8 + 3 * t + 1)
            link(nc.vector.reciprocal(st5[:, 80 + t:81 + t], st5[:, 80 + t:81 + t]))
            for h in range(2):
                i = nc.vector.scalar_tensor_tensor(sh5[:, 512 * h:512 * h + 512], psum[2 * t + h][:, :],
                                                   st5[:, 80 + t:81 + t], g1row[:, 512 * h:512 * h + 512], ALU.mult, ALU.mult)
            link(i)
            link(nc.vector.tensor_tensor(xn[:, t, :], xn[:, t, :], sh5, ALU.add))
            dve.wait_ge(s_n1, 8 + 3 * t + 3)
            link(nc.vector.reciprocal(st5[:, 88 + t:89 + t], st5[:, 88 + t:89 + t]))
            nc.vector.scalar_tensor_tensor(H2N[:, t, :], xn[:, t, :], st5[:, 88 + t:89 + t], a2row, ALU.mult,
                                           ALU.mult).then_inc(s_h2, 1)
            dve.wait_ge(s_h2, 2 * t + 1)
            nc.vector.tensor_tensor(H2N[:, t, :], H2N[:, t, :], sh2row, ALU.add).then_inc(s_h2, 1)
        with dve.Fori(0, HEADS) as h:
            for a in range(2):
                dve.wait_ge(s_skt, 2 * h + a + 1)
                nc.vector.tensor_copy(skT[:, a], psum[2 + a][:, 0:P]).then_inc(s_ske, 1)
            for a in range(2):
                dve.wait_ge(s_s, 2 * h + a + 1)
                nc.vector.tensor_copy(SC[:, 0:NT, 2 * h + a, :], v3(psum[4 + a][:, :])).then_inc(s_se, 1)

    def tensor5(pe):
        pe.wait_ge(s_sb, 1)
        for u in range(8):
            pe.wait_ge(s_wr[u % 2], 16 * (u // 2 + 1))
            for k in range(KT):
                m = nc.tensor.matmul(psum[u][:, :], silb[:, k, :], wmr[:, u % 2, k, :], start=k == 0, stop=k == KT - 1)
            m.then_inc(s_mr, 1)
        pe.wait_ge(s_hn, 5)
        pe.wait_ge(s_me, 14)
        for b in range(8):
            for i in range(4):
                m = nc.tensor.transpose(psum[b][:, P * i:P * i + P], YT[:, 4 * b + i, :], ident)
            m.then_inc(s_yt, 1)
        pe.wait_ge(s_wo, 16)
        pe.wait_ge(s_yg, 2 * PAIRS)
        for t in range(NT):
            for k in range(KT):
                a = (yconv if k < PAIRS else yrw)[:, k % PAIRS, P * t:P * t + P]
                for h in range(2):
                    m = nc.tensor.matmul(psum[2 * t + h][:, :], a, wo[:, k, 512 * h:512 * h + 512],
                                         start=k == 0, stop=k == KT - 1)
            m.then_inc(s_op, 1)
        for t in range(NT):
            pe.wait_ge(s_h2, 2 * t + 2)
            for h in range(2):
                for k in range(4):
                    m = nc.tensor.transpose(psum[2 * t + h][:, P * k:P * k + P],
                                            H2N[:, t, P * (4 * h + k):P * (4 * h + k) + P], ident)
                m.then_inc(s_h2t, 1)
        pe.wait_ge(s_h2e, 2 * NT)
        for moved in (s_ske, s_qe, s_se):
            credit(pe, moved, 2)
        with pe.Fori(0, HEADS) as h:
            for a in range(2):
                pe.wait_ge(s_sk[a], 16 * h + 16)
                pe.wait_ge(s_ske, 2 * h + 2)
                nc.tensor.transpose(psum[2 + a][:, 0:P], skn[:, a], ident).then_inc(s_skt, 1)
                pe.wait_ge(s_wq[a], 16 * h + 16)
                pe.wait_ge(s_qe, 2 * h + 2)
                for k in range(KT):
                    m = nc.tensor.matmul(psum[a][:, :], wq2[:, a, k, :], h2T[:, k, :], start=k == 0, stop=k == KT - 1)
                m.then_inc(s_q, 1)
            for a in range(2):
                pe.wait_ge(s_ske, 2 * h + a + 3)
                pe.wait_ge(s_qe, 2 * h + a + 3)
                pe.wait_ge(s_se, 2 * h + 2)
                for t in range(NT):
                    m = nc.tensor.matmul(psum[4 + a][:, P * t:P * t + P], qT[:, a, P * t:P * t + P], skT[:, a],
                                         start=True, stop=True)
                m.then_inc(s_s, 1)

    PO = [psum[6], psum[7]]
    NSL = TOPK
    out_v = out[0].rearrange("(t p) d -> t p d", p=P)

    def tiles6(engine, body, tail):
        body(0, True)
        with engine.Fori(1, NT) as t:
            body(t, False)
        tail()

    def sync6(sp):
        with sp.Fori(0, NT) as t:
            sp.wait_ge(s_fv, 4 * t + 8)
            sp.dma_start(out_v[t], ot).then_inc(s_out, 16)
        sp.wait_ge(s_out, 16 * NT + 16)

    def pool6(pool):
        pool.wait_ge(s_se, HS + 2)
        nc.gpsimd.iota(iot[:, 0:NCAND], pattern=[[1, NCAND]], base=0, channel_multiplier=0,
                       allow_small_or_imprecise_dtypes=True).then_inc(s_io, 1)

        def gather(kind, g, hi, j, first):
            ring, table, sems, used = [(U, peer_u[0], s_u, s_dot), (V, peer_v[0], s_v, s_mm)][kind]
            if not (first and hi == 0 and j < RING):
                pool.wait_ge(used, NSL * g + j + 1 - RING)
            apart(pool, s_pass_pool)
            pool.indirect_dma_start(ring[:, j % RING, :], None, table,
                                    bass.IndirectOffsetOnAxis(ap=idx[:, hi % 4, j:j + 1].bitcast(U32), axis=0)
                                    ).then_inc(sems[j % RING], 16)

        def body(t, first):
            for h in range(HEADS):
                g = t * HEADS + h
                pool.wait_ge(s_tk, g + 1)
                for j in range(NSL):
                    gather(0, g, h, j, first)
                    if h:
                        gather(1, g - 1, h - 1, j, first)
                    elif not first:
                        gather(1, g - 1, HEADS - 1, j, False)

        def tail():
            for j in range(NSL):
                gather(1, NT * HEADS - 1, HEADS - 1, j, False)
        tiles6(pool, body, tail)

    def scalar6(act):
        act.wait_ge(s_se, HS + 2)

        def stage_scores(t, h):
            g = t * HEADS + h
            nc.scalar.activation(SCs[:, h % 2], SC[:, t, 2 * h:2 * h + 2, :], ACT.Identity).then_inc(s_scs, 1)

        def diags(g, hp):
            for j in range(NSL):
                if not (isinstance(g, int) and g == 0 and j < 4):
                    act.wait_ge(s_mm, NSL * g + j - 3)
                nc.scalar.activation(diag[:, j % 4], ident, ACT.Identity, scale=wts[:, hp % 2, j:j + 1]).then_inc(s_dg, 1)

        def exps(g):
            act.wait_ge(s_tk, g + 1)
            if not (isinstance(g, int) and g == 0):
                act.wait_ge(s_gs, 2 * g)
            nc.scalar.activation(prob, top, ACT.Exp, bias=ntop[:, 0:1], accum_out=psum_[:, 0:1]).then_inc(s_ex, 1)

        def finish(t):
            act.wait_ge(s_mm, NSL * HEADS * (t + 1))
            act.wait_ge(s_fv, 4 * t + 4)
            nc.scalar.activation(fsq[:, 0:512], PO[0][:, :], ACT.Square, accum_out=fst[:, 0:1]).then_inc(s_fa, 1)
            act.wait_ge(s_fa, 3 * t + 1)
            nc.scalar.activation(fsq[:, 0:512], PO[1][:, :], ACT.Square, accum_out=fst[:, 1:2]).then_inc(s_fa, 1)
            act.wait_ge(s_fv, 4 * t + 5)
            nc.scalar.activation(fst[:, 3:4], fst[:, 2:3], ACT.Sqrt, bias=eps[:, 0:1], scale=1.0 / D).then_inc(s_fa, 1)

        stage_scores(0, 0)
        stage_scores(0, 1)
        exps(0)

        def body(t, first):
            for h in range(HEADS):
                g = t * HEADS + h
                if h == 0:
                    if not first:
                        act.wait_ge(s_dot, NSL * g)
                    nc.scalar.activation(h2cur, H2N[:, t, :], ACT.Identity).then_inc(s_hc, 1)
                if h or not first:
                    act.wait_ge(s_wt, g)
                    diags(g - 1, (h - 1) % HEADS)
                act.wait_ge(s_tk, g + 1)
                if h < HEADS - 2:
                    stage_scores(t, h + 2)
                else:
                    stage_scores(t + 1, h + 2 - HEADS)
                exps(g + 1)
                act.wait_ge(s_dot, NSL * (g + 1))
                nc.scalar.activation(gel[:, h % 2], acts[:, h % 2], ACT.Gelu).then_inc(s_ge, 1)
                if h == 0 and not first:
                    finish(t - 1)

        def tail():
            g = NT * HEADS
            act.wait_ge(s_wt, g)
            diags(g - 1, HEADS - 1)
            finish(NT - 1)
        tiles6(act, body, tail)

    def vector6(dve):
        NL = LINKS

        def topk(g, hp, first):
            n = [0]

            def link(i):
                n[0] += 1
                i.then_inc(s_lk, 1)
                dve.wait_ge(s_lk, NL * g + n[0])
                apart(dve, s_pass_dve)

            dve.wait_ge(s_scs, g + 1)
            apart(dve, s_pass_dve)
            a = SCs[:, hp % 2]
            u16, p16 = i16.bitcast(U32), pos.bitcast(U32)
            for s in range(2):
                i = nc.vector.max(v16[:, s, 0:8], a[:, s])
            link(i)
            for s in range(2):
                nc.vector.max_index(u16[:, s, 0:8], v16[:, s, 0:8], a[:, s])
                i = nc.vector.match_replace(mr[:, s], v16[:, s, 0:8], a[:, s], -3.0e38)
            link(i)
            for s in range(2):
                i = nc.vector.max(v16[:, s, 8:16], mr[:, s])
            link(i)
            for s in range(2):
                i = nc.vector.max_index(u16[:, s, 8:16], v16[:, s, 8:16], mr[:, s])
            link(i)
            link(nc.vector.tensor_copy(i16f, u16))
            link(nc.vector.tensor_scalar(i16f[:, 0], i16f[:, 0], float(KEYS), None, ALU.mult))
            at = 0
            for r, m, w in ROWS:
                for src, dst, op in ((v16, cand, ALU.add), (i16f, cid, ALU.add)):
                    i = nc.vector.tensor_tensor(dst[:, at:at + m * w].rearrange("p (a b) -> p a b", b=w),
                                                src[:, 0, r:r + m].unsqueeze(2).broadcast_to([P, m, w]),
                                                src[:, 1, 0:w].unsqueeze(1).broadcast_to([P, m, w]), op)
                at += m * w
            link(i)
            if not first:
                dve.wait_ge(s_ex, g)
                apart(dve, s_pass_dve)
            link(nc.vector.max(top[:, 0:8], cand[:, 0:NCAND]))
            nc.vector.max_index(p16[:, 0:8], top[:, 0:8], cand[:, 0:NCAND])
            link(nc.vector.match_replace(cmr[:, 0:NCAND], top[:, 0:8], cand[:, 0:NCAND], -3.0e38))
            link(nc.vector.max(top[:, 8:16], cmr[:, 0:NCAND]))
            nc.vector.tensor_scalar(ntop[:, 0:1], top[:, 0:1], -1.0, None, ALU.mult)
            link(nc.vector.max_index(p16[:, 8:16], top[:, 8:16], cmr[:, 0:NCAND]))
            link(nc.vector.tensor_copy(posf, p16))
            link(nc.vector.tensor_tensor(oh, iot[:, 0:NCAND].unsqueeze(1).broadcast_to([P, TOPK, NCAND]),
                                         posf.unsqueeze(2).broadcast_to([P, TOPK, NCAND]), ALU.is_equal))
            link(nc.vector.tensor_tensor(oh, oh, cid[:, 0:NCAND].unsqueeze(1).broadcast_to([P, TOPK, NCAND]), ALU.mult))
            link(nc.vector.tensor_reduce(exf, oh, AX.X, ALU.add))
            assert n[0] == NL, n[0]
            nc.vector.tensor_copy(idx[:, hp % 4].bitcast(U32), exf).then_inc(s_tk, 1)

        def softmax(g, hp):
            dve.wait_ge(s_ex, g + 1)
            nc.vector.reciprocal(psum_[:, 1:2], psum_[:, 0:1]).then_inc(s_gs, 1)
            dve.wait_ge(s_gs, 2 * g + 1)
            nc.vector.tensor_scalar(gsm[:, hp % 2], prob, psum_[:, 1:2], None, ALU.mult).then_inc(s_gs, 1)

        def finish(t):
            dve.wait_ge(s_fa, 3 * t + 2)
            nc.vector.tensor_tensor(fst[:, 2:3], fst[:, 0:1], fst[:, 1:2], ALU.add).then_inc(s_fv, 1)
            dve.wait_ge(s_fa, 3 * t + 3)
            nc.vector.reciprocal(fst[:, 4:5], fst[:, 3:4]).then_inc(s_fv, 1)
            dve.wait_ge(s_fv, 4 * t + 6)
            dve.wait_ge(s_out, 16 * t + 16)
            for h in range(2):
                i = nc.vector.scalar_tensor_tensor(ot[:, 512 * h:512 * h + 512], PO[h][:, :], fst[:, 4:5],
                                                   g2row[:, 512 * h:512 * h + 512], ALU.mult, ALU.mult)
            i.then_inc(s_fv, 1)
            dve.wait_ge(s_fv, 4 * t + 7)
            nc.vector.tensor_tensor(ot, ot, xn[:, t, :], ALU.add).then_inc(s_fv, 1)

        credit(dve, s_fv, 4)
        credit(dve, s_out, 16)
        dve.wait_ge(s_io, 1)
        topk(0, 0, True)
        softmax(0, 0)

        def body(t, first):
            for h in range(HEADS):
                g = t * HEADS + h
                if h == 0:
                    dve.wait_ge(s_hc, t + 1)
                if h >= 3 or not first:
                    dve.wait_ge(s_mm, NSL * (g - 2))
                topk(g + 1, (h + 1) % HEADS, False)
                for j in range(NSL):
                    dve.wait_ge(s_u[j % RING], 32 * g + 16 * (j // RING) + 16)
                    nc.vector.tensor_tensor_reduce(U[:, j % RING, :], U[:, j % RING, :], h2cur, 1.0, 0.0, ALU.mult, ALU.add,
                                                   acts[:, h % 2, j:j + 1]).then_inc(s_dot, 1)
                softmax(g + 1, (h + 1) % HEADS)
                dve.wait_ge(s_ge, g + 1)
                if h >= 2 or not first:
                    dve.wait_ge(s_dg, NSL * (g - 1))
                nc.vector.tensor_tensor(wts[:, h % 2], gel[:, h % 2], gsm[:, h % 2], ALU.mult).then_inc(s_wt, 1)
                if h == 0 and not first:
                    finish(t - 1)

        tiles6(dve, body, lambda: finish(NT - 1))

    def tensor6(pe):
        def experts(g, hp, first):
            for j in range(NSL):
                pe.wait_ge(s_dg, NSL * g + j + 1)
                pe.wait_ge(s_v[j % RING], 32 * g + 16 * (j // RING) + 16)
                for h in range(2):
                    m = nc.tensor.matmul(PO[h][:, :], diag[:, j % 4], V[:, j % RING, 512 * h:512 * h + 512],
                                         start=hp == 0 and j == 0, stop=hp == HEADS - 1 and j == NSL - 1)
                m.then_inc(s_mm, 1)

        def body(t, first):
            for h in range(HEADS):
                g = t * HEADS + h
                if h:
                    if h == 1 and not first:
                        pe.wait_ge(s_fv, 4 * t + 4)
                    experts(g - 1, h - 1, first)
                elif not first:
                    experts(g - 1, HEADS - 1, False)
        tiles6(pe, body, lambda: experts(NT * HEADS - 1, HEADS - 1, False))


    n_masks = 4 + 4 * 6 + 16 + 12 + 12
    LATER = {'sync': (sync4, sync5, sync6), 'pool': (pool4, pool5, pool6), 'scalar': (scalar4, scalar5, scalar6),
             'vector': (vector4, vector5, vector6), 'tensor': (tensor4, tensor5, tensor6)}

    @block.sync
    def _(sp):
        sp.dma_start(cc[:, 0, :], c[0].rearrange("(p k) -> p k", k=KT)).then_inc(s_c, 16)
        sp.dma_start(cc[:, 1, :], c_ctx.rearrange("(p k) -> p k", k=KT)).then_inc(s_c, 16)
        sp.dma_start(prow[0:16, :], b_mod[0, 0:2048].rearrange("(r q) -> r q", q=P)).then_inc(s_prow, 16)
        sp.dma_start(prow[16:24, :], norm_gains[0, 0].rearrange("(r q) -> r q", q=P)).then_inc(s_prow, 16)
        rows = [tshift_mu[0, 0, 0], tshift_mu[0, 0, 1], tshift_mu[0, 0, 2],
                tshift_mu[0, 1, 0], tshift_mu[0, 1, 1], tshift_mu[0, 1, 2],
                decay_w0[0, 0], decay_w0[0, 1], iclr_a0[0, 0], iclr_a0[0, 1],
                k_k[0], k_a[0], r_k[0].rearrange("h n -> (h n)"), lnx_g[0], lnx_b[0],
                conv_w[0, 0], conv_w[0, 1], conv_w[0, 2]]
        for i, r in enumerate(rows):
            sp.dma_start(prow2[4 * i:4 * i + 4, :], r.rearrange("(r q) -> r q", q=P)).then_inc(s_prow, 16)
        for i in range(8):
            if i >= 3:
                sp.wait_ge(s_mod, i - 2)
            sp.dma_start([wm, wm2, wm3][i % 3], wmod_v[:, :, 256 * i:256 * i + 256]).then_inc(s_wm[i % 3], 16)
            if i == 0:
                for t in range(NT):
                    sp.dma_start(xn[:, t, :], x_v[t]).then_inc(s_x[t], 16)
                for t in range(NTC):
                    sp.dma_start(ctxn[:, t, :], ctx_v[t]).then_inc(s_ctx, 16)
        for j, col in enumerate([25 * P, 26 * P, 24 * P]):
            sp.dma_start(wring[:, j], win_v[:, :, col:col + P]).then_inc(s_w[j], 16)
        sp.wait_ge(s_hT, 12)

        def lora_loads(p):
            for d in range(2):
                sp.dma_start(lora[DH * d:DH * d + DH, 0, 0, :],
                             decay_w2[0, d, :, bass.ds(p * P, P)]).then_inc(s_lora, 16)
                sp.dma_start(lora[DH * d:DH * d + DH, 0, 1, :],
                             iclr_a2[0, d, :, bass.ds(p * P, P)]).then_inc(s_lora, 16)
            sp.dma_start(gw, gate_w2[0, :, bass.ds(p * P, P)]).then_inc(s_lora, 16)

        def pair_loads(p, first):
            for j, base in enumerate((16, 12, 20)):
                sp.wait_ge(s_pj, 3 * p + j + 1)
                sp.dma_start(wring[:, j], win_v[:, :, bass.ds(base * P + p * P, P)]).then_inc(s_w[j], 16)
            if not first:
                sp.wait_ge(s_ax, 7 * p)
                apart(sp, s_pass_sp)
            lora_loads(p)

        def spills(p):
            sp.wait_ge(s_vs, 2 * p + 2)
            sp.dma_start(vs_dram[p], VSb.rearrange("p a b -> p (a b)")).then_inc(s_spill, 16)
            for d in range(2):
                sp.wait_ge(s_bk, 2 * p + d + 1)
                sp.dma_start(bk_dram[2 * p + d], BKb[:, d].rearrange("p a b -> p (a b)")).then_inc(s_spill, 16)
                sp.dma_start(kr_dram[2 * p + d], KRb[:, d].rearrange("p a b -> p (a b)")).then_inc(s_spill, 16)

        pair_loads(0, True)
        with sp.Fori(1, PAIRS) as p:
            pair_loads(p, False)
            spills(p - 1)
        for j, base in enumerate((4, 8, 0)):
            sp.wait_ge(s_pj, 3 * PAIRS + j + 1)
            sp.dma_start(wring[:, j], win_v[:, :, base * P:base * P + P]).then_inc(s_w[j], 16)
        spills(PAIRS - 1)
        with sp.Fori(1, PAIRS) as q:
            for j, base in enumerate((4, 8, 0)):
                sp.wait_ge(s_pj, 3 * (q + PAIRS) + j + 1)
                apart(sp, s_pass_sp)
                sp.dma_start(wring[:, j], win_v[:, :, bass.ds(base * P + q * P, P)]).then_inc(s_w[j], 16)
        sp.wait_ge(s_spill, 16 * 5 * PAIRS)
        for stage in LATER["sync"]:
            stage(sp)

    @block.gpsimd
    def _(pool):
        n = [0]

        def put(i, done=s_const):
            n[0] += 1
            i.then_inc(done, 1)
            pool.wait_ge(done, n[0])

        put(nc.gpsimd.memset(ident, 0.0))
        put(nc.gpsimd.memset(head_ones, 0.0))
        put(nc.gpsimd.memset(eps[:, 0:1], NORM_EPS))
        put(nc.gpsimd.memset(eps[:, 1:2], 1e-12))
        put(nc.gpsimd.memset(eps[:, 2:3], LNX_EPS))
        put(nc.gpsimd.memset(eps[:, 3:4], 0.0))
        put(nc.gpsimd.affine_select(out=ident, in_=ident, compare_op=ALU.not_equal, fill=1.0, base=0,
                                    pattern=[[-1, P]], channel_multiplier=1))
        put(nc.gpsimd.memset(head_ones[0:DH, 0:DH], 1.0))
        put(nc.gpsimd.memset(head_ones[DH:P, DH:P], 1.0))
        assert pool_masks(pool) == n_masks
        pool.wait_ge(s_hT, 12)
        n[0] = 0
        for tile in (kraw, vraw, rraw, VSb, KRb):
            put(nc.gpsimd.memset(tile, 0.0), s_pz)
        put(nc.gpsimd.memset(scan_keep, 1.0), s_pz)
        put(nc.gpsimd.memset(scan_keep.rearrange("p (n c) -> p n c", c=C)[:, :, 0:1], 0.0), s_pz)
        for stage in LATER["pool"]:
            stage(pool)

    @block.scalar
    def _(act):
        act.wait_ge(s_c, 32)
        nc.scalar.activation(ccs, cc, ACT.Sigmoid).then_inc(s_silu, 1)
        act.wait_ge(s_const, 6)
        for i in range(NTC + NT):
            if i < NTC:
                act.wait_ge(s_ctx, 16 * NTC)
                src = ctxn[:, i, :]
            else:
                act.wait_ge(s_x[i - NTC], 16)
                src = xn[:, i - NTC, :]
            if i:
                act.wait_ge(s_ssq, i)
            nc.scalar.activation(sq, src, ACT.Square, accum_out=ssq[:, i:i + 1]).then_inc(s_ssq, 1)
        act.wait_ge(s_ssq, NTC + NT)
        nc.scalar.activation(rstd[:, 0:6], ssq[:, 0:6], ACT.Sqrt, bias=eps[:, 0:1], scale=1.0 / D).then_inc(s_ssq, 1)
        for t in range(NTC + NT):
            which = 1 if t < NTC else 0
            col = P * t
            for h in range(2):
                act.wait_ge(s_tr, 2 * t + h + 1)
                if t == 0 and h == 0:
                    act.wait_ge(s_modc, 3)
                for k in range(4 * h, 4 * h + 4):
                    i = nc.scalar.activation(hT[:, k, col:col + P], psum[2 * (t % 2) + h][:, P * (k % 4):P * (k % 4) + P],
                                             ACT.Identity, bias=shsc[:, k, which:which + 1],
                                             scale=tab[:, k, which:which + 1])
                i.then_inc(s_hT, 1)
        act.wait_ge(s_pj, 1)
        nc.scalar.activation(lo_w[:, TC:TT], psum[0][:, 0:T], ACT.Tanh)
        nc.scalar.activation(lo_w[:, 0:TC], psum[1][:, 0:TC], ACT.Tanh).then_inc(s_pe, 1)
        act.wait_ge(s_pj, 2)
        nc.scalar.activation(lo_a[:, TC:TT], psum[2][:, 0:T], ACT.Identity)
        nc.scalar.activation(lo_a[:, 0:TC], psum[3][:, 0:TC], ACT.Identity).then_inc(s_pe, 1)
        act.wait_ge(s_pj, 3)
        nc.scalar.activation(lo_g, psum[4][:, 0:T], ACT.Sigmoid).then_inc(s_pe, 1)

        def pair(p, first):
            def aux(d, which):
                act.wait_ge(s_ax, 7 * p + [[1, 2], [4, 6]][d][which])
                if d or not first:
                    act.wait_ge([s_cum, s_bk][which], 2 * p + d)
                dst, col = [sg, aa][which], [W0_F, A0_F][which] + d
                nc.scalar.activation(dst[:, TC:TT], psum[5][:, 0:T], ACT.Sigmoid, bias=pp[:, col:col + 1])
                nc.scalar.activation(dst[:, 0:TC], psum[6][:, 0:TC], ACT.Sigmoid,
                                     bias=pp[:, col:col + 1]).then_inc(s_ae, 1)

            def factors(d):
                act.wait_ge(s_cum, 2 * p + d + 1)
                if d or not first:
                    act.wait_ge(s_bk, 2 * p + d)
                nc.scalar.activation(e1, ex, ACT.Exp, scale=-DECAY)
                nc.scalar.activation(e3, inc, ACT.Exp, scale=DECAY)
                nc.scalar.activation(e2, inc, ACT.Exp, scale=-DECAY).then_inc(s_e, 1)

            act.wait_ge(s_pj, 3 * p + 4)
            if first:
                act.wait_ge(s_pz, 7)
            else:
                act.wait_ge(s_sh, 3 * p)
            nc.scalar.activation(kraw[:, XO:XO + T], psum[0][:, 0:T], ACT.Identity)
            nc.scalar.activation(kraw[:, CO:CO + TC], psum[1][:, 0:TC], ACT.Identity).then_inc(s_pe, 1)
            act.wait_ge(s_pp, 6 * p + 6)
            aux(0, 0)
            aux(0, 1)
            act.wait_ge(s_pj, 3 * p + 5)
            nc.scalar.activation(rraw[:, 1:1 + T], psum[2][:, 0:T], ACT.Identity).then_inc(s_pe, 1)
            act.wait_ge(s_sh, 3 * p + 1)
            nc.scalar.activation(sqk, kS, ACT.Square, scale=pp[:, K_K:K_K + 1]).then_inc(s_kk, 1)
            act.wait_ge(s_ax, 7 * p + 3)
            nc.scalar.activation(t2[:, TC:TT], psum[5][:, 0:T], ACT.Sqrt, bias=eps[:, 1:2])
            nc.scalar.activation(t2[:, 0:TC], psum[6][:, 0:TC], ACT.Sqrt, bias=eps[:, 1:2]).then_inc(s_ae, 1)
            act.wait_ge(s_pj, 3 * p + 6)
            nc.scalar.activation(vraw[:, XO:XO + T], psum[3][:, 0:T], ACT.Identity)
            nc.scalar.activation(vraw[:, CO:CO + TC], psum[4][:, 0:TC], ACT.Identity).then_inc(s_pe, 1)
            factors(0)
            aux(1, 0)
            act.wait_ge(s_sh, 3 * p + 3)
            if not first:
                act.wait_ge(s_spill, 16 * 5 * p)
            v_c = vS.rearrange("p (n c) -> p n c", c=C)
            nc.scalar.activation(VSb[0:DH, :, DH:P], v_c[0:DH], ACT.Identity).then_inc(s_vs, 1)
            nc.scalar.activation(VSb[DH:P, :, 0:DH], v_c[DH:P], ACT.Identity).then_inc(s_vs, 1)
            act.wait_ge(s_ax, 7 * p + 5)
            nc.scalar.activation(gate[:, p, :], psum[7][:, 0:T], ACT.Identity).then_inc(s_ae, 1)
            aux(1, 1)
            factors(1)

        pair(0, True)
        with act.Fori(1, PAIRS) as p:
            pair(p, False)
        act.wait_ge(s_bk, 2 * PAIRS)
        credit(act, s_cv, 4)
        with act.Fori(0, PAIRS) as q:
            act.wait_ge(s_pj, 3 * q + 3 * PAIRS + 4)
            act.wait_ge(s_cv, q * 4 + 4)
            nc.scalar.activation(t1[:, 0:T], psum[0][:, 0:T], ACT.Identity).then_inc(s_pe, 1)
        for stage in LATER["scalar"]:
            stage(act)

    @block.vector
    def _(dve):
        n_dv = [0]

        dve.wait_ge(s_silu, 1)
        nc.vector.tensor_tensor(silu_col.rearrange("p k v -> p v k"), cc, ccs, ALU.mult).then_inc(s_silu, 1)
        dve.wait_ge(s_ptr, 1)
        nc.vector.tensor_copy(pcolA[:, 0:24], psum[4][:, 0:24]).then_inc(s_pcol, 1)
        dve.wait_ge(s_ptr, 2)
        nc.vector.tensor_copy(par.rearrange("p r i -> p i r"),
                              psum[5][:, 0:4 * NPAR].rearrange("p (i r) -> p i r", r=PAIRS)).then_inc(s_pcol, 1)
        dve.wait_ge(s_const, 9)
        nc.vector.tensor_copy(mix_diag, head_ones).then_inc(s_pcol, 1)
        dve.wait_ge(s_ssq, NTC + NT + 1)
        nc.vector.reciprocal(rstd[:, 0:6], rstd[:, 0:6]).then_inc(s_rstd, 1)
        dve.wait_ge(s_rstd, 1)
        for t in range(NTC + NT):
            if t >= 2:
                dve.wait_ge(s_tr, 2 * (t - 1))
            src = ctxn[:, t, :] if t < NTC else xn[:, t - NTC, :]
            nc.vector.tensor_scalar(xs[:, t % 2, :], src, rstd[:, t:t + 1], None, ALU.mult).then_inc(s_xs, 1)
            if t == 1:
                dve.wait_ge(s_mod, 8)
                dve.wait_ge(s_pcol, 3)
                nc.vector.tensor_tensor(shsc, psum[6][:, 0:32].rearrange("p (a b) -> p a b", b=2),
                                        pcolA[:, 0:16].unsqueeze(2).broadcast_to([P, 16, 2]), ALU.add).then_inc(s_modc, 1)
                dve.wait_ge(s_modc, 1)
                nc.vector.tensor_scalar(tab, shsc[:, 8:16], 1.0, None, ALU.add).then_inc(s_modc, 1)
                dve.wait_ge(s_modc, 2)
                nc.vector.tensor_tensor(tab, tab, pcolA[:, 16:24].unsqueeze(2).broadcast_to([P, 8, 2]),
                                        ALU.mult).then_inc(s_modc, 1)
        dve.wait_ge(s_pz, 7)

        def chunks(a):
            return a.rearrange("p (n c) -> p n c", c=C)

        def pair(p, first):
            n_dv[0] = 0
            base = p * PAIR_STEPS

            def link(ins):
                n_dv[0] += 1
                ins.then_inc(s_dv, 1)
                dve.wait_ge(s_dv, base + n_dv[0])

            def shift(raw, off, cols, dst, dst0, c0, mp, mn):
                o = dst[:, dst0:dst0 + cols]
                link(nc.vector.tensor_scalar(o, raw[:, off:off + cols], pp[:, c0:c0 + 1], None, ALU.mult))
                link(nc.vector.scalar_tensor_tensor(o, raw[:, off - 1:off - 1 + cols], pp[:, mp:mp + 1], o, ALU.mult, ALU.add))
                return nc.vector.scalar_tensor_tensor(o, raw[:, off + 1:off + 1 + cols], pp[:, mn:mn + 1], o, ALU.mult, ALU.add)

            if not first:
                dve.wait_ge(s_ae, 6 * p)
            nc.vector.tensor_copy(pp[:, 0:NPAR], par[:, p, :]).then_inc(s_pp, 1)
            dve.wait_ge(s_pp, 6 * p + 1)
            nc.vector.tensor_scalar(pp[:, C0_R:C0_R + 3], pp[:, MP_R:MP_R + 3], -1.0, 1.0, ALU.mult, ALU.add).then_inc(s_pp, 1)
            nc.vector.tensor_scalar(pp[:, OMKA:OMKA + 1], pp[:, K_A:K_A + 1], -1.0, 1.0, ALU.mult, ALU.add).then_inc(s_pp, 1)
            dve.wait_ge(s_pp, 6 * p + 3)
            nc.vector.tensor_tensor(pp[:, C0_R:C0_R + 3], pp[:, C0_R:C0_R + 3], pp[:, MN_R:MN_R + 3], ALU.subtract).then_inc(s_pp, 3)
            dve.wait_ge(s_pp, 6 * p + 6)
            dve.wait_ge(s_pe, 3 * p + 4)
            link(shift(kraw, CO, TC, kS, 0, C0_K, MP_K, MN_K))
            shift(kraw, XO, T, kS, TC, C0_K, MP_K, MN_K).then_inc(s_sh, 1)

            def cumulate(d):
                dve.wait_ge(s_ae, 6 * p + [1, 4][d])
                if d or not first:
                    dve.wait_ge(s_e, 2 * p + d)
                link(nc.vector.tensor_tensor_scan(cs, scan_keep, sg, 0.0, ALU.mult, ALU.add))
                if d == 0:
                    link(nc.vector.tensor_copy(inc, cs))
                    nc.vector.tensor_tensor(ex, cs, sg, ALU.subtract).then_inc(s_cum, 1)
                else:
                    tot = chunks(cs)[:, :, C - 1:C].broadcast_to([P, NCH, C])
                    link(nc.vector.tensor_tensor(chunks(ex), tot, chunks(cs), ALU.subtract))
                    nc.vector.tensor_tensor(inc, ex, sg, ALU.add).then_inc(s_cum, 1)

            def products(d):
                dve.wait_ge(s_e, 2 * p + d + 1)
                dve.wait_ge(s_ae, 6 * p + [2, 6][d])
                if not first:
                    dve.wait_ge(s_spill, 16 * 5 * p)
                link(nc.vector.tensor_scalar(t1, aa, pp[:, K_A:K_A + 1], pp[:, OMKA:OMKA + 1], ALU.mult, ALU.add))
                link(nc.vector.tensor_tensor(t1, t1, kS, ALU.mult))
                k3 = chunks(t1)
                f1, f2, f3, kk3, r3 = chunks(e1), chunks(e2), chunks(e3), chunks(kk), chunks(rS)
                lo, hi = slice(0, DH), slice(DH, P)
                link(nc.vector.tensor_tensor(BKb[lo, d, :, DH:P], k3[lo], f3[lo], ALU.mult))
                link(nc.vector.tensor_tensor(BKb[hi, d, :, 0:DH], k3[hi], f3[hi], ALU.mult))
                link(nc.vector.scalar_tensor_tensor(t1, kk, -1.0, aa, ALU.mult, ALU.mult))
                link(nc.vector.tensor_tensor(BKb[lo, d, :, 0:DH], k3[lo], f3[lo], ALU.mult))
                link(nc.vector.tensor_tensor(BKb[hi, d, :, DH:P], k3[hi], f3[hi], ALU.mult))
                link(nc.vector.tensor_tensor(KRb[lo, d, :, 0:DH], kk3[lo], f1[lo], ALU.mult))
                link(nc.vector.tensor_tensor(KRb[hi, d, :, DH:P], kk3[hi], f1[hi], ALU.mult))
                link(nc.vector.tensor_tensor(KRb[lo, d, TC // C:, DH:P], r3[lo], f2[lo, TC // C:], ALU.mult))
                link(nc.vector.tensor_tensor(KRb[hi, d, TC // C:, 0:DH], r3[hi], f2[hi, TC // C:], ALU.mult))
                at = C - 1 if d == 0 else 0
                nc.vector.tensor_copy(pc_all[:, p * 2 + d, :], f2[:, :, at]).then_inc(s_bk, 1)

            cumulate(0)
            dve.wait_ge(s_ae, 6 * p + 3)
            link(nc.vector.reciprocal(t2, t2))
            link(nc.vector.scalar_tensor_tensor(kk, kS, pp[:, K_K:K_K + 1], t2, ALU.mult, ALU.mult))
            dve.wait_ge(s_pe, 3 * p + 5)
            shift(rraw, 1, T, rS, 0, C0_R, MP_R, MN_R).then_inc(s_sh, 1)
            dve.wait_ge(s_sh, 3 * p + 2)
            nc.vector.scalar_tensor_tensor(rk, rS, pp[:, R_K:R_K + 1], kS[:, TC:TT], ALU.mult, ALU.mult).then_inc(s_bn, 1)
            dve.wait_ge(s_pe, 3 * p + 6)
            if not first:
                dve.wait_ge(s_vs, 2 * p)
            link(shift(vraw, CO, TC, vS, 0, C0_V, MP_V, MN_V))
            shift(vraw, XO, T, vS, TC, C0_V, MP_V, MN_V).then_inc(s_sh, 1)
            products(0)
            dve.wait_ge(s_ax, 7 * p + 7)
            dve.wait_ge(s_sh, 3 * p + 3)
            nc.vector.tensor_tensor(bonus[:, p, :], psum[2][:, 0:T], vS[:, TC:TT], ALU.mult).then_inc(s_bd, 1)
            cumulate(1)
            products(1)
            return n_dv[0]

        n = pair(0, True)
        assert n == PAIR_STEPS, n
        with dve.Fori(1, PAIRS) as p:
            pair(p, False)

        def rows(a):
            return a.rearrange("p (n c) -> p n c", c=GRID)

        with dve.Fori(0, PAIRS) as q:
            nc.vector.tensor_copy(pp[:, 0:NPAR], par[:, q, :]).then_inc(s_pp, 1)
            dve.wait_ge(s_pp, q + 6 * PAIRS + 1)
            dve.wait_ge(s_pe, q + 3 * PAIRS + 4)
            dve.wait_ge(s_pj, 3 * q + 3 * PAIRS + 5)
            nc.vector.tensor_tensor(t2[:, 0:T], t1[:, 0:T], psum[2][:, 0:T], ALU.mult).then_inc(s_cv, 1)
            dve.wait_ge(s_cv, q * 4 + 5)
            nc.vector.tensor_scalar(cs[:, 0:T], t2[:, 0:T], pp[:, CV1:CV1 + 1], None, ALU.mult).then_inc(s_cv, 1)
            dve.wait_ge(s_cv, q * 4 + 6)
            z, o = rows(t2[:, 0:T]), rows(cs[:, 0:T])
            nc.vector.scalar_tensor_tensor(o[:, :, 1:], z[:, :, :-1], pp[:, CV0:CV0 + 1], o[:, :, 1:],
                                           ALU.mult, ALU.add).then_inc(s_cv, 1)
            dve.wait_ge(s_cv, q * 4 + 7)
            nc.vector.scalar_tensor_tensor(o[:, :, :-1], z[:, :, 1:], pp[:, CV2:CV2 + 1], o[:, :, :-1],
                                           ALU.mult, ALU.add).then_inc(s_cv, 1)
            dve.wait_ge(s_cv, q * 4 + 8)
            dve.wait_ge(s_pj, 3 * q + 3 * PAIRS + 6)
            nc.vector.tensor_tensor(yconv[:, q, :], psum[3][:, 0:T], cs[:, 0:T], ALU.mult).then_inc(s_done3, 1)
        for stage in LATER["vector"]:
            stage(dve)

    @block.tensor
    def _(pe):
        pe.wait_ge(s_const, 7)
        pe.wait_ge(s_prow, 16 * 20)
        nc.tensor.transpose(psum[4][:, 0:24], prow[0:24, :], ident[0:24, 0:24]).then_inc(s_ptr, 1)
        nc.tensor.transpose(psum[5][:, 0:4 * NPAR], prow2[0:4 * NPAR, :], ident[0:4 * NPAR, 0:4 * NPAR]).then_inc(s_ptr, 1)
        pe.wait_ge(s_silu, 2)
        for i in range(8):
            pe.wait_ge(s_wm[i % 3], 16 * (i // 3 + 1))
            w = [wm, wm2, wm3][i % 3]
            for h in range(2):
                j = 2 * i + h
                for k in range(KT):
                    m = nc.tensor.matmul(psum[6][:, 2 * j:2 * j + 2], w[:, k, P * h:P * h + P], silu_col[:, k, :],
                                         start=k == 0, stop=k == KT - 1)
            m.then_inc(s_mod, 1)
        for t in range(NTC + NT):
            pe.wait_ge(s_xs, t + 1)
            for h in range(2):
                if t >= 2:
                    pe.wait_ge(s_hT, 2 * (t - 2) + h + 1)
                for k in range(4 * h, 4 * h + 4):
                    m = nc.tensor.transpose(psum[2 * (t % 2) + h][:, P * (k % 4):P * (k % 4) + P],
                                            xs[:, t % 2, P * k:P * k + P], ident)
                m.then_inc(s_tr, 1)

        def project(j, bx, bc, loads):
            pe.wait_ge(s_w[j], loads)
            for k in range(KT):
                m = nc.tensor.matmul(psum[bx][:, 0:T], wring[:, j, k, :], hT[:, k, TC:TT], start=k == 0, stop=k == KT - 1)
                if bc is not None:
                    m = nc.tensor.matmul(psum[bc][:, 0:TC], wring[:, j, k, :], hT[:, k, 0:TC], start=k == 0, stop=k == KT - 1)
            m.then_inc(s_pj, 1)

        pe.wait_ge(s_hT, 12)
        project(0, 0, 1, 16)
        project(1, 2, 3, 16)
        project(2, 4, None, 16)

        def low_rank(d, which):
            src = [lo_w, lo_a][which]
            sl = slice(DH * d, DH * d + DH)
            nc.tensor.matmul(psum[5][:, 0:T], lora[sl, 0, which, :], src[sl, TC:TT], start=True, stop=True)
            nc.tensor.matmul(psum[6][:, 0:TC], lora[sl, 0, which, :], src[sl, 0:TC], start=True, stop=True).then_inc(s_ax, 1)

        def pair(p, first):
            pe.wait_ge(s_pe, 3 * p + 3)
            project(0, 0, 1, 16 * p + 32)
            if not first:
                pe.wait_ge(s_bd, p)
            project(1, 2, None, 16 * p + 32)
            pe.wait_ge(s_lora, 80 * p + 80)
            if not first:
                pe.wait_ge(s_ae, 6 * p)
            low_rank(0, 0)
            pe.wait_ge(s_ae, 6 * p + 1)
            low_rank(0, 1)
            pe.wait_ge(s_ae, 6 * p + 2)
            pe.wait_ge(s_kk, p + 1)
            nc.tensor.matmul(psum[5][:, 0:T], head_ones, sqk[:, TC:TT], start=True, stop=True)
            nc.tensor.matmul(psum[6][:, 0:TC], head_ones, sqk[:, 0:TC], start=True, stop=True).then_inc(s_ax, 1)
            project(2, 3, 4, 16 * p + 32)
            pe.wait_ge(s_ae, 6 * p + 3)
            low_rank(1, 0)
            nc.tensor.matmul(psum[7][:, 0:T], gw, lo_g, start=True, stop=True).then_inc(s_ax, 1)
            pe.wait_ge(s_ae, 6 * p + 4)
            low_rank(1, 1)
            pe.wait_ge(s_bn, p + 1)
            nc.tensor.matmul(psum[2][:, 0:T], head_ones, rk, start=True, stop=True).then_inc(s_ax, 1)

        pair(0, True)
        with pe.Fori(1, PAIRS) as p:
            pair(p, False)
        pe.wait_ge(s_pe, 3 * PAIRS + 3)
        pe.wait_ge(s_bd, PAIRS)
        credit(pe, s_done3, 1)
        with pe.Fori(0, PAIRS) as q:
            pe.wait_ge(s_done3, q + 1)
            project(0, 0, None, q * 16 + 16 * (PAIRS + 2))
            project(1, 2, None, q * 16 + 16 * (PAIRS + 2))
            project(2, 3, None, q * 16 + 16 * (PAIRS + 2))
        for stage in LATER["tensor"]:
            stage(pe)


_INS = ['x', 'c', 'ctx', 'c_ctx', 'w_mod', 'b_mod', 'norm_gains', 'w_in', 'w_out', 'conv_w', 'tshift_mu',
        'decay_w0', 'decay_w2', 'iclr_a0', 'iclr_a2', 'gate_w2', 'k_k', 'k_a', 'r_k', 'lnx_g', 'lnx_b',
        'peer_wq', 'peer_subkeys', 'peer_u', 'peer_v']
_OUTS = [((1, 512, 1024), 'float32')]


def kernel(**inputs):
    import numpy as _np
    import concourse.bacc as _bacc
    from concourse import mybir as _mybir
    from concourse.bass_utils import run_bass_kernel_spmd as _run

    nc = _bacc.Bacc("TRN2", target_bir_lowering=False, num_devices=1)
    arrays, args = {}, []
    for name in _INS:
        a = _np.ascontiguousarray(inputs[name])
        if a.dtype.kind in "iu":
            a = a.astype(_np.int64)
        arrays[f"in_{name}_dram"] = a
        args.append(nc.dram_tensor(f"in_{name}_dram", a.shape, _mybir.dt.from_np(a.dtype), kind="ExternalInput").ap())
    for i, (shape, dtype) in enumerate(_OUTS):
        dt = _mybir.dt.from_np(_np.dtype(dtype))
        args.append(nc.dram_tensor(f"out_{i}_dram", shape, dt, kind="ExternalOutput").ap())
    layer(nc, *args)
    r = _run(nc, [arrays], core_ids=[0])
    got = tuple(r.results[0][f"out_{i}_dram"] for i in range(len(_OUTS)))
    return got[0]
```

```python
import concourse.bass as bass
from concourse import mybir
from contextlib import ExitStack

F32 = mybir.dt.float32
U32 = mybir.dt.uint32
ALU = mybir.AluOpType
ACT = mybir.ActivationFunctionType
AX = mybir.AxisListType

P = 128
D = 1024
KT = D // P
T = 512
TC = 256
TT = T + TC
NT = T // P
NTC = TC // P
GRID = 64
DH = 64
PAIRS = 4
C = 64
NCH = TT // C
NXC = T // C
NB = 4
D_IN = 3456
NORM_EPS = 1e-6
LNX_EPS = 64e-5
DECAY = 0.6065306597126334
HEADS = 8
KEYS = 128
TOPK = 16
DQ = 256
ROWS = [(0, 1, 16), (1, 1, 8), (2, 1, 5), (3, 1, 4), (4, 1, 3), (5, 3, 2), (8, 8, 1)]
PAIR_STEPS = 40
NCAND = sum(m * w for _, m, w in ROWS)

(MP_R, MP_K, MP_V, MN_R, MN_K, MN_V, W0_F, W0_B, A0_F, A0_B, K_K, K_A, R_K, LNX_G, LNX_B,
 CV0, CV1, CV2) = range(18)
NPAR = 18
(C0_R, C0_K, C0_V, OMKA) = range(18, 22)
NPP = 22

LINKS = 15
RING = 8


def layer(nc, x, c, ctx_in, c_ctx, w_mod, b_mod, norm_gains, w_in, w_out, conv_w, tshift_mu,
          decay_w0, decay_w2, iclr_a0, iclr_a2, gate_w2, k_k, k_a, r_k, lnx_g, lnx_b,
          peer_wq, peer_subkeys, peer_u, peer_v, out):
    with ExitStack() as stack:
        _layer(nc, stack, x, c, ctx_in, c_ctx, w_mod, b_mod, norm_gains, w_in, w_out, conv_w, tshift_mu,
               decay_w0, decay_w2, iclr_a0, iclr_a2, gate_w2, k_k, k_a, r_k, lnx_g, lnx_b,
               peer_wq, peer_subkeys, peer_u, peer_v, out)


def _layer(nc, stack, x, c, ctx_in, c_ctx, w_mod, b_mod, norm_gains, w_in, w_out, conv_w, tshift_mu,
           decay_w0, decay_w2, iclr_a0, iclr_a2, gate_w2, k_k, k_a, r_k, lnx_g, lnx_b,
           peer_wq, peer_subkeys, peer_u, peer_v, out):
    ARENA = 53120
    MOD = ARENA - 2048 - 7 * D
    arena = stack.enter_context(nc.sbuf_tensor("arena", [P, ARENA], F32))
    psum = [stack.enter_context(nc.psum_tensor(f"bank{i}", [P, 512], F32)) for i in range(8)]

    class Cut:

        def __init__(self, at, end=ARENA):
            self.at, self.end = at, end

        def __call__(self, *shape):
            n = 1
            for s in shape:
                n *= s
            a = arena[:, self.at:self.at + n]
            self.at += n
            assert self.at <= self.end, (self.at, self.end)
            if len(shape) == 2:
                a = a.rearrange("p (a b) -> p a b", b=shape[1])
            elif len(shape) == 3:
                a = a.rearrange("p (a b c) -> p a b c", b=shape[1], c=shape[2])
            elif len(shape) == 4:
                a = a.rearrange("p (a b c d) -> p a b c d", b=shape[1], c=shape[2], d=shape[3])
            return a

    def sem(name):
        return stack.enter_context(nc.semaphore(name))

    keep = Cut(0)
    ident = keep(P)
    xn = keep(NT, D)
    head_ones = keep(P)
    mix_diag = keep(P)
    par = keep(PAIRS + 1, NPAR)
    bias4 = keep(4)
    ybmod = keep(64)
    shsc = keep(16, 2)
    ng_col = keep(16)
    eps = keep(4)
    silu_col = keep(KT, 2)
    yconv = keep(PAIRS, T)
    bonus = keep(PAIRS, T)
    gate = keep(PAIRS, T)
    pc_all = keep(2 * PAIRS, NCH)
    KEEP_END = keep.at

    cut = Cut(KEEP_END)
    hT = cut(KT, TT)
    wring = cut(3, KT, P)
    s3 = cut.at
    ctxn = cut(NTC, D)
    wm = cut(8, KT, 2 * P)
    prow = cut(P)
    prow2 = cut(P)
    sq = cut(D)
    xs = cut(NTC + NT, D)
    modrow = cut(2 * D)
    pcolA = cut(P)
    pcolB = cut(P)
    cc = cut(2, KT)
    ccs = cut(2, KT)
    ssq = cut(8)
    rstd = cut(8)
    mod1 = cut(16, 2)
    tab = cut(KT, 2)
    assert cut.at <= ARENA - 2048

    cut = Cut(s3)
    lo_w = cut(TT)
    lo_a = cut(TT)
    lo_g = cut(T)
    lora = cut(2, 2, P)
    gw = cut(P)
    kraw = cut(TT + 4)
    vraw = cut(TT + 4)
    rraw = cut(T + 2)
    kS = cut(TT)
    vS = cut(TT)
    rS = cut(T)
    kk = cut(TT)
    sqk = cut(TT)
    sg = cut(TT)
    aa = cut(2, TT)
    cs = cut(TT)
    ex = cut(TT)
    inc = cut(TT)
    e1 = cut(TT)
    e2 = cut(TT)
    e3 = cut(TT)
    t1 = cut(TT)
    t2 = cut(TT)
    rk = cut(T)
    pp = cut(NPP)
    scan_keep = cut(TT)
    BKb = cut(2, NCH, P)
    KRb = cut(2, NCH, P)
    VSb = cut(NCH, P)
    CO, XO = 1, TC + 3

    cut = Cut(KEEP_END)
    BKs = cut(2, NB, P)
    VSs = cut(2, NB, P)
    BKT = cut(2, NB, P)
    NBD = cut(2, NB, P)
    MBD = cut(2, NB, P)
    ZZ = cut(2, NB, P)
    XX = cut(2, NB, P)
    AA = cut(2, NB, P)
    ysum = cut(PAIRS, NXC, DH)
    LE = cut(3, 2, NB * P)
    LO = cut(3, 2, NB * P)
    QQ = cut(3, 2, NB * P)
    KVP = cut(3, 2, NB * P)
    SV = cut(3, 2, NB * P)
    RB = cut(2, P)
    TMPS = cut(2, P)
    Yb = cut(NXC, 2, 2, DH)
    KRx = cut(2, NB, 2, P)
    assert cut.at <= MOD
    cut = Cut(ARENA - 2048)
    msk_e = cut(2, P)
    msk_o = cut(2, P)
    lvl = cut(2, 6, P)
    cut = Cut(MOD, ARENA - 2048)
    wmr = cut(KT, 256)
    silb = cut(KT, P)
    rows = cut(4, D)
    g1row, sh2row, a2row, g2row = (rows[:, i, :] for i in range(4))

    cut = Cut(KEEP_END + 8192)
    H2N = cut(NT, D)
    SC = arena[:, KEEP_END:KEEP_END + (NT + 1) * 2048].rearrange("p (t h k) -> p t h k", h=2 * HEADS, k=KEYS)
    brow = arena[:, KEEP_END:KEEP_END + 7 * D]
    ysq = H2N.rearrange("p a b -> p (a b)")[:, 2048:4096].rearrange("p (a x v) -> p a x v", x=NXC, v=DH)
    assert cut.at == KEEP_END + 8192 + 4096
    h2T = cut(KT, T)
    YT = h2T.rearrange("p a b -> p (a b)").rearrange("p (i c) -> p i c", c=P)
    U = cut(RING, D)
    V = cut(RING, D)
    wo = U
    wqA = V.rearrange("p s (k n) -> p s k n", k=KT)
    late = cut.at
    tmp5 = cut(D)
    st5 = cut(96)
    yrw = arena[:, ARENA - 2048:].rearrange("p (a b) -> p a b", b=T)
    sh5 = arena[:, KEEP_END:KEEP_END + D]
    h2cur = arena[:, ARENA - 2048:ARENA - 1024]
    ot = arena[:, ARENA - 1024:]
    cut = Cut(cut.at, MOD + 6 * D)
    diag = cut(4, P)
    SCs = cut(2, 2, KEYS)
    mr = cut(2, KEYS)
    oh = cut(TOPK, NCAND)
    v16 = cut(2, TOPK)
    i16 = cut(2, TOPK)
    i16f = cut(2, TOPK)
    cand = cut(64)
    cid = cut(64)
    cmr = cut(64)
    iot = cut(64)
    top = cut(TOPK)
    pos = cut(TOPK)
    posf = cut(TOPK)
    exf = cut(TOPK)
    idx = cut(4, TOPK)
    ntop = cut(2)
    prob = cut(TOPK)
    psum_ = cut(2)
    gsm = cut(2, TOPK)
    acts = cut(2, TOPK)
    gel = cut(2, TOPK)
    wts = cut(2, TOPK)
    fst = cut(8)
    fsq = gate.rearrange("p a b -> p (a b)")[:, 0:512]
    wq2 = yconv.rearrange("p a b -> p (a b)").rearrange("p (s k n) -> p s k n", s=2, k=KT)
    skn = gate.rearrange("p a b -> p (a b)").rearrange("p (s n) -> p s n", n=P)
    skT = bonus.rearrange("p a b -> p (a b)").rearrange("p (s n) -> p s n", n=P)
    qT = arena[:, KEEP_END + 2048:KEEP_END + 3072].rearrange("p (s n) -> p s n", n=T)
    qB = gate.rearrange("p a b -> p (a b)")[:, 1024:1024 + 6 * P].rearrange("p (s n) -> p s n", n=3 * P)

    def v3(a):
        return a.rearrange("p (i c) -> p i c", c=P)

    bk_dram = nc.dram_tensor("bk_scratch", [2 * PAIRS, P, NCH * P], F32, kind="Internal").ap()
    kr_dram = nc.dram_tensor("kr_scratch", [2 * PAIRS, P, NCH * P], F32, kind="Internal").ap()
    vs_dram = nc.dram_tensor("vs_scratch", [PAIRS, P, NCH * P], F32, kind="Internal").ap()

    s_c = sem("cond_loaded")
    s_prow = sem("param_rows_loaded")
    s_x = [sem(f"latents_loaded{i}") for i in range(NT)]
    s_ctx = sem("context_loaded")
    s_wm = [sem(f"wmod_loaded{i}") for i in range(8)]
    s_const = sem("constants_made")
    s_silu = sem("silu_made")
    s_ptr = sem("params_transposed")
    s_pcol = sem("param_columns_made")
    s_mod = sem("mod_products")
    s_mrow = sem("mod_rows_moved")
    s_modc = sem("mod_columns_made")
    s_ssq = sem("square_sums")
    s_rstd = sem("rstd_made")
    s_dv = sem("vector_steps")
    s_xs = sem("normed_rows")
    s_tr = sem("rows_transposed")
    s_hT = sem("hT_lower_half")
    s_hU = sem("hT_upper_half")
    s_w = [sem(f"win_loaded{i}") for i in range(3)]
    s_pj = sem("projections_made")
    s_pe = sem("projections_evacuated")
    s_lora = sem("lora_loaded")
    s_ax = sem("aux_products")
    s_ae = sem("aux_evacuated")
    s_sh = sem("shifted")
    s_kk = sem("kk_ready")
    s_cum = sem("decay_sums")
    s_e = sem("decay_factors")
    s_bk = sem("pair_dir_ready")
    s_vs = sem("vs_ready")
    s_spill = sem("spilled")
    s_pz = sem("pads_zeroed")
    s_pp, s_b4 = sem("pair_params"), sem("pair_biases")
    s_bn = sem("bonus_product_in")
    s_cv = sem("conv_steps")
    s_bd = sem("bonus_made")
    s_done3 = sem("stage3_vector_done")
    s_mask = sem("masks_made")
    s_bkl = [sem(f"bk_loaded{d}") for d in range(2)]
    s_vsl = [sem(f"vs_loaded{d}") for d in range(2)]
    s_krl = [sem(f"kr_loaded{i}") for i in range(6)]
    s_nz = sem("n_zeroed")
    s_mk = [sem(f"chunk_products{d}") for d in range(2)]
    s_ac = [sem(f"chunk_scalar_moves{d}") for d in range(2)]
    s_vc = [sem(f"chunk_vector_moves{d}") for d in range(2)]
    s_zt = [sem(f"inverse_products{d}") for d in range(2)]
    s_pl = [sem(f"inverse_started{d}") for d in range(2)]
    s_c1 = [sem(f"state_read{d}") for d in range(2)]
    s_rb = [sem(f"state_read_split{d}") for d in range(2)]
    s_y1 = [sem(f"y_from_state{d}") for d in range(2)]
    s_c2 = [sem(f"chunk_applied{d}") for d in range(2)]
    s_tm = [sem(f"state_decayed{d}") for d in range(2)]
    s_st = [sem(f"state_written{d}") for d in range(2)]
    s_y2 = [sem(f"y_from_chunk{d}") for d in range(2)]
    s_ys = sem("y_summed")
    s_br = sem("rows_loaded")
    s_wo = sem("wout_loaded")
    s_wr = sem("wmod_row_weights")
    s_sb = sem("silu_spread")
    s_mr = sem("modulation_rows")
    s_me = sem("modulation_rows_moved")
    s_row = sem("rows_finished")
    s_yz = sem("y_transpose_zeroed")
    s_m0 = sem("head_sums")
    s_hn = sem("head_norm_vector")
    s_ha = sem("head_norm_scalar")
    s_yt = sem("y_transposed")
    s_yv = sem("y_affine")
    s_yg = sem("y_gated")
    s_op = sem("mixer_output")
    s_n1 = sem("norm1_scalar")
    s_m1 = sem("norm1_vector")
    s_h2 = sem("h2_rows")
    s_h2t = sem("h2_transposed")
    s_h2e = sem("h2_columns")
    s_wq = [sem(f"wq_loaded{i}") for i in range(2)]
    s_sk = sem("subkeys_loaded")
    s_wa = [sem(f"wq_half_loaded{i}") for i in range(2)]
    s_skt = sem("subkeys_transposed")
    s_ske = sem("subkeys_moved")
    s_q = sem("queries")
    s_qe = sem("queries_moved")
    s_s = sem("scores")
    s_se = sem("scores_moved")
    s_qb = sem("late_queries")
    s_qbe = sem("late_queries_moved")
    s_sb6 = sem("late_scores")
    s_sbe = sem("late_scores_moved")
    s_io = sem("iota_made")
    s_scs = sem("scores_staged")
    s_lk = sem("topk_links")
    s_tk = sem("experts_chosen")
    s_ex = sem("probabilities_raised")
    s_gs = sem("probabilities")
    s_u = [sem(f"u_rows{i}") for i in range(RING)]
    s_v = [sem(f"v_rows{i}") for i in range(RING)]
    s_dot = sem("dots")
    s_ge = sem("gelus")
    s_wt = sem("expert_weights")
    s_dg = sem("weight_diagonals")
    s_mm = sem("experts_added")
    s_hc = sem("h2_current")
    s_fa = sem("final_scalar")
    s_fv = sem("final_vector")
    s_out = sem("output_stored")
    s_pass_sp, s_pass_dve, s_pass_pool = sem("sync_passed"), sem("vector_passed"), sem("pool_passed")

    block = stack.enter_context(nc.Block())

    x_v = x[0].rearrange("(t p) d -> t p d", p=P)
    ctx_v = ctx_in[0].rearrange("(t p) d -> t p d", p=P)
    wmod_v = w_mod[0].rearrange("(p k) n -> p k n", k=KT)
    win_v = w_in[0].rearrange("(k p) n -> p k n", p=P)

    def credit(engine, semaphore, n):
        engine.sem_inc(semaphore, n)

    def apart(engine, passed):
        engine.sem_inc(passed, 1)

    W1, W2 = [psum[0], psum[2]], [psum[1], psum[3]]
    C1, C2 = [psum[4], psum[6]], [psum[5], psum[7]]
    ORDER = [[0, 1, 2], [0, 2, 1]]
    ITEMS = [[0, 1, 2, 3], [3, 2, 1, 0]]
    LV = 5
    MK = {"bkT": 1, "vT": 2, "kv": 3, "ge": 4, "go": 5, "nT": 6}
    for l in range(LV):
        MK["a", l] = 7 + 3 * l
        if l < LV - 1:
            MK["z", l] = 8 + 3 * l
            MK["x", l] = 9 + 3 * l
    MK["x", LV - 1] = 8 + 3 * (LV - 1)
    MK["q"] = 9 + 3 * (LV - 1)
    NMK = MK["q"]
    AC = {"bkT": 1, "vT": 2, "m": 3, "q": 4}
    NAC = 4
    VC = {"kv": 1, "ge": 2, "go": 3}
    for l in range(LV):
        VC["a", l] = 4 + 3 * l
        if l < LV - 1:
            VC["z", l] = 5 + 3 * l
            VC["x", l] = 6 + 3 * l
    VC["x", LV - 1] = 5 + 3 * (LV - 1)
    NVC = VC["x", LV - 1]
    NPL = 2

    def bcast(m, rows, cols):
        w = cols.stop - cols.start
        return m[rows, cols].unsqueeze(1).broadcast_to([rows.stop - rows.start, NB, w])

    MOD_BLOCKS = [[0], [1], [2, 3]]

    LOW, HIGH, ALL = slice(0, DH), slice(DH, P), slice(0, P)

    def steps4(engine, do, tail):
        do(0, 0, None, True)
        do(0, 1, (0, 0), True)
        do(0, 2, (0, 1), True)
        with engine.Fori(1, PAIRS) as p:
            do(p, 0, (p - 1, 2), False)
            do(p, 1, (p, 0), False)
            do(p, 2, (p, 1), False)
        tail()

    def sync4(sp):
        sp.wait_ge(s_done3, PAIRS + 1)

        def do(p, b, chain, first):
            n = 3 * p + b
            for d in range(2):
                src = slice(ORDER[d][b] * NB * P, (ORDER[d][b] + 1) * NB * P)
                if not (first and b == 0):
                    sp.wait_ge(s_mk[d], NMK * (n - 1) + MK["go"])
                if not first:
                    apart(sp, s_pass_sp)
                    sp.wait_ge(s_c1[d], 12 * (p - 1) + 4 * b + 4)
                    apart(sp, s_pass_sp)
                sp.dma_start(BKs[:, d].rearrange("p a b -> p (a b)"), bk_dram[2 * p + d][:, src]).then_inc(s_bkl[d], 16)
                sp.dma_start(VSs[:, d].rearrange("p a b -> p (a b)"), vs_dram[p][:, src]).then_inc(s_vsl[d], 16)
                sp.dma_start(KRx[LOW, d, :, 0, :], kr_dram[2 * p + d][LOW, src].rearrange("p (i c) -> p i c", c=P)).then_inc(s_krl[2 * b + d], 16)
                sp.dma_start(KRx[HIGH, d, :, 1, :], kr_dram[2 * p + d][HIGH, src].rearrange("p (i c) -> p i c", c=P)).then_inc(s_krl[2 * b + d], 16)
                sp.dma_start(LE[LOW, b, d, :], kr_dram[2 * p + d][LOW, src]).then_inc(s_krl[2 * b + d], 16)
                sp.dma_start(LO[HIGH, b, d, :], kr_dram[2 * p + d][HIGH, src]).then_inc(s_krl[2 * b + d], 16)
            for j in MOD_BLOCKS[b]:
                if not (first and j == 0):
                    sp.wait_ge(s_mr, 4 * p + j)
                    apart(sp, s_pass_sp)
                sp.dma_start(wmr, wmod_v[:, :, bass.ds(p * D + (2 * D + 256 * j), 256)]).then_inc(s_wr, 16)
        steps4(sp, do, lambda: None)

    def pool_masks(pool):
        n = [0]

        def put(i):
            n[0] += 1
            i.then_inc(s_mask, 1)
            pool.wait_ge(s_mask, n[0])

        for d in range(2):
            put(nc.gpsimd.memset(msk_e[:, d], 1.0))
            put(nc.gpsimd.memset(msk_o[:, d], 1.0))
            for l in range(6):
                s = 1 << l
                v = lvl[:, d, l].rearrange("p (n h s) -> p n h s", h=2, s=s)
                put(nc.gpsimd.memset(v[:, :, d], 0.0))
                put(nc.gpsimd.memset(v[:, :, 1 - d], 1.0))
        for d in range(2):
            sg_ = 1 - 2 * d
            for tile, ops in ((msk_e, (ALU.is_gt, ALU.is_ge)), (msk_o, (ALU.is_ge, ALU.is_gt))):
                for h in range(2):
                    for rows in (LOW, HIGH):
                        a = tile[rows, d, DH * h:DH * h + DH]
                        put(nc.gpsimd.affine_select(out=a, in_=a, compare_op=ops[h], fill=0.0, base=0,
                                                    pattern=[[sg_, DH]], channel_multiplier=-sg_))
            for l in range(6):
                s = 1 << l
                v = lvl[:, d, l].rearrange("p (n w) -> p n w", w=2 * s)
                put(nc.gpsimd.affine_select(out=v, in_=v, compare_op=ALU.is_ge, fill=0.0, base=-d * s,
                                            pattern=[[-2 * s, P // (2 * s)], [0, 2 * s]], channel_multiplier=1))
        for d in range(2):
            for l in range(6):
                s = 1 << l
                v = lvl[:, d, l].rearrange("p (n w) -> p n w", w=2 * s)
                put(nc.gpsimd.affine_select(out=v, in_=v, compare_op=ALU.is_ge, fill=0.0, base=s - 1 + d * s,
                                            pattern=[[2 * s, P // (2 * s)], [0, 2 * s]], channel_multiplier=-1))
        return n[0]

    def pool4(pool):
        pool.wait_ge(s_done3, PAIRS + 1)
        pool.wait_ge(s_spill, 16 * 5 * PAIRS)
        for d in range(2):
            nc.gpsimd.memset(NBD[:, d], 0.0).then_inc(s_nz, 1)
        for d in range(2):
            for n, quarter in ((2 * d + 2, KRx[HIGH, d, :, 0, :]), (2 * d + 3, KRx[LOW, d, :, 1, :])):
                pool.wait_ge(s_nz, n)
                nc.gpsimd.memset(quarter, 0.0).then_inc(s_nz, 1)
        pool.wait_ge(s_nz, 6)
        nc.gpsimd.tensor_copy(silb, silu_col[:, :, 0:1].broadcast_to([P, KT, P])).then_inc(s_sb, 1)

        def do(p, b, chain, first):
            n = 3 * p + b
            for d in range(2):
                pool.wait_ge(s_vc[d], NVC * n + VC["go"])
                nc.gpsimd.tensor_tensor(ZZ[:, d], NBD[:, d], bcast(lvl[:, d, 0], ALL, ALL), ALU.mult).then_inc(s_zt[d], 1)
                pool.wait_ge(s_zt[d], 2 * n + 1)
                nc.gpsimd.tensor_tensor(ZZ[:, d], ZZ[:, d], bcast(ident, ALL, ALL), ALU.add).then_inc(s_pl[d], 1)
                pool.wait_ge(s_ac[d], NAC * n + AC["m"])
                nc.gpsimd.tensor_tensor(XX[:, d], MBD[:, d], bcast(lvl[:, 1 - d, 0], ALL, ALL), ALU.mult).then_inc(s_zt[d], 1)
                pool.wait_ge(s_zt[d], 2 * n + 2)
                nc.gpsimd.tensor_tensor(XX[:, d], XX[:, d], bcast(ident, ALL, ALL), ALU.add).then_inc(s_pl[d], 1)
        steps4(pool, do, lambda: None)

    def scalar4(act):
        def copies(cp, cb, i, which):
            for d in range(2):
                ci = ITEMS[d][i]
                xc = NB * ORDER[d][cb] + ci - TC // C
                src = [C1, C2][which][d]
                if which == 0:
                    act.wait_ge(s_rb[d], 12 * cp + 4 * cb + i + 1)
                elif (cb, i) == (2, 3):
                    act.wait_ge(s_c2[d], 12 * cp + 12)
                else:
                    act.wait_ge(s_st[d], 11 * cp + 4 * cb + i + 1)
                nc.scalar.activation(Yb[HIGH, xc, d, which, :], src[HIGH, 0:DH], ACT.Identity)
                nc.scalar.activation(Yb[LOW, xc, d, which, :], src[LOW, DH:P], ACT.Identity).then_inc([s_y1, s_y2][which][d], 1)

        def chain_part(chain, i, first):
            cp, cb = chain
            if cb == 0:
                return
            if i == 0 and cb == 1 and not first:
                act.wait_ge(s_ys, cp)
            copies(cp, cb, i, 0)
            copies(cp, cb, i, 1)

        def mod_row(p, j):
            act.wait_ge(s_mr, 4 * p + j + 1)
            nc.scalar.activation(rows[:, p, 256 * j:256 * j + 256], C1[j % 2][:, P:P + 256], ACT.Identity).then_inc(s_me, 1)

        def do(p, b, chain, first):
            n = 3 * p + b
            for d in range(2):
                act.wait_ge(s_mk[d], NMK * n + MK["bkT"])
                nc.scalar.activation(BKT[:, d], v3(W1[d][:, :]), ACT.Identity).then_inc(s_ac[d], 1)
            for d in range(2):
                act.wait_ge(s_mk[d], NMK * n + MK["vT"])
                if not first:
                    act.wait_ge(s_c1[d], 12 * (p - 1) + 4 * b + 4)
                    act.wait_ge(s_st[d], 11 * (p - 1) + min(4 * b + 4, 11))
                nc.scalar.activation(v3(SV[:, b, d]), v3(W2[d][:, :]), ACT.Identity).then_inc(s_ac[d], 1)
            for d in range(2):
                act.wait_ge(s_mk[d], NMK * n + MK["nT"])
                nc.scalar.activation(MBD[:, d], v3(W2[d][:, :]), ACT.Identity).then_inc(s_ac[d], 1)
            mod_row(p, b)
            for i in range(NB):
                if chain:
                    chain_part(chain, i, first)
                if b == 2 and i == 0:
                    mod_row(p, 3)
            for d in range(2):
                act.wait_ge(s_mk[d], NMK * n + MK["q"])
                if not first:
                    act.wait_ge(s_c2[d], 12 * (p - 1) + 4 * b + 4)
                nc.scalar.activation(v3(QQ[:, b, d]), v3(W2[d][:, :]), ACT.Identity).then_inc(s_ac[d], 1)

        def tail():
            for i in range(NB):
                chain_part((PAIRS - 1, 2), i, False)
        steps4(act, do, tail)

    def vector4(dve):
        def split(cp, cb, i):
            for d in range(2):
                dve.wait_ge(s_c1[d], 12 * cp + 4 * cb + i + 1)
                nc.vector.tensor_tensor(RB[:, d], C1[d][:, 0:P], mix_diag, ALU.mult).then_inc(s_rb[d], 1)
            if (cb, i) == (2, 3):
                return
            for d in range(2):
                ci = ITEMS[d][i]
                c = NB * ORDER[d][cb] + ci
                if not (cb == 0 and i == 0):
                    dve.wait_ge(s_st[d], 11 * cp + 4 * cb + i)
                nc.vector.scalar_tensor_tensor(TMPS[:, d], v3(SV[:, cb, d])[:, ci], pc_all[:, 2 * cp + d, c:c + 1],
                                               v3(KVP[:, cb, d])[:, ci], ALU.mult, ALU.add).then_inc(s_tm[d], 1)

        def advance(cp, cb, i):
            if (cb, i) == (2, 3):
                return
            nb, ni = (cb, i + 1) if i < 3 else (cb + 1, 0)
            for d in range(2):
                ci = ITEMS[d][i]
                c = NB * ORDER[d][cb] + ci
                dst = v3(SV[:, nb, d])[:, ITEMS[d][ni]]
                dve.wait_ge(s_c2[d], 12 * cp + 4 * cb + i + 1)
                dve.wait_ge(s_tm[d], 11 * cp + 4 * cb + i + 1)
                if ni == 0:
                    dve.wait_ge(s_vc[d], NVC * (3 * cp + nb) + VC["kv"])
                for rows, cols in ((LOW, slice(0, DH)), (HIGH, slice(DH, P))):
                    last = nc.vector.scalar_tensor_tensor(dst[rows, cols], C2[d][rows, cols],
                                                          pc_all[rows, 2 * cp + d, c:c + 1], TMPS[rows, d, cols],
                                                          ALU.mult, ALU.add)
                last.then_inc(s_st[d], 1)

        def total(cp):
            for d in range(2):
                dve.wait_ge(s_y1[d], 8 * cp + 8)
                dve.wait_ge(s_y2[d], 8 * cp + 8)
            nc.vector.tensor_reduce(ysum[:, cp], Yb.rearrange("p x d s v -> p x v d s"), AX.XY, ALU.add).then_inc(s_ys, 1)

        def do(p, b, chain, first):
            n = 3 * p + b
            if first and b == 0:
                dve.wait_ge(s_nz, 2)
                dve.wait_ge(s_mask, n_masks)
            for d in range(2):
                dve.wait_ge(s_mk[d], NMK * n + MK["kv"])
                pc = pc_all[:, 2 * p + d, NB * ORDER[d][b]:NB * ORDER[d][b] + NB]
                nc.vector.tensor_tensor(v3(KVP[:, b, d]), v3(W1[d][:, :]), pc.unsqueeze(2).broadcast_to([P, NB, P]),
                                        ALU.mult).then_inc(s_vc[d], 1)
            for d in range(2):
                g = v3(W2[d][:, :])
                dve.wait_ge(s_mk[d], NMK * n + MK["ge"])
                if not (first and b == 0):
                    dve.wait_ge(s_pl[d], NPL * n)
                nc.vector.tensor_tensor(NBD[LOW, d, :, 0:DH], g[LOW, :, 0:DH], bcast(msk_e[:, d], LOW, slice(0, DH)), ALU.mult)
                nc.vector.tensor_tensor(BKT[LOW, d, :, DH:P], g[LOW, :, DH:P], bcast(msk_e[:, d], LOW, slice(DH, P)), ALU.mult)
                nc.vector.tensor_tensor(v3(LE[:, b, d])[HIGH], g[HIGH], bcast(msk_e[:, d], HIGH, ALL), ALU.mult).then_inc(s_vc[d], 1)
            for d in range(2):
                g = v3(W1[d][:, :])
                dve.wait_ge(s_mk[d], NMK * n + MK["go"])
                nc.vector.tensor_tensor(v3(LO[:, b, d])[LOW], g[LOW], bcast(msk_o[:, d], LOW, ALL), ALU.mult)
                nc.vector.tensor_tensor(BKT[HIGH, d, :, 0:DH], g[HIGH, :, 0:DH], bcast(msk_o[:, d], HIGH, slice(0, DH)), ALU.mult)
                nc.vector.tensor_tensor(NBD[HIGH, d, :, DH:P], g[HIGH, :, DH:P], bcast(msk_o[:, d], HIGH, slice(DH, P)),
                                        ALU.mult).then_inc(s_vc[d], 1)
            for l in range(LV):
                for d in range(2):
                    dve.wait_ge(s_mk[d], NMK * n + MK["a", l])
                    nc.vector.tensor_tensor(AA[:, d], v3(W1[d][:, :]), bcast(lvl[:, d, l + 1], ALL, ALL), ALU.mult).then_inc(s_vc[d], 1)
                if chain and l < NB:
                    split(*chain, l)
                for d in range(2):
                    if l < LV - 1:
                        dve.wait_ge(s_mk[d], NMK * n + MK["z", l])
                        nc.vector.tensor_tensor(ZZ[:, d], v3(W2[d][:, :]), ZZ[:, d], ALU.add).then_inc(s_vc[d], 1)
                    dve.wait_ge(s_mk[d], NMK * n + MK["x", l])
                    nc.vector.tensor_tensor(XX[:, d], v3(W1[d][:, :]), XX[:, d], ALU.add).then_inc(s_vc[d], 1)
                if chain and l < NB:
                    advance(*chain, l)
            if chain and chain[1] == 2:
                total(chain[0])

        def tail():
            for i in range(NB):
                split(PAIRS - 1, 2, i)
                advance(PAIRS - 1, 2, i)
            total(PAIRS - 1)
        steps4(dve, do, tail)

    def tensor4(pe):
        def read_state(cp, cb, i, first):
            for d in range(2):
                ci = ITEMS[d][i]
                if not (cb == 0 and i == 0):
                    pe.wait_ge(s_st[d], 11 * cp + 4 * cb + i)
                yc = 8 * cp + max(4 * (cb - 1) + i, 0)
                if not (first and yc == 0):
                    pe.wait_ge(s_y1[d], yc)
                if not (first and cb == 0 and i == 0):
                    pe.wait_ge(s_rb[d], 12 * cp + 4 * cb + i)
                nc.tensor.matmul(C1[d][:, 0:DH], v3(LE[:, cb, d])[:, ci], v3(SV[:, cb, d])[:, ci, 0:DH], start=True, stop=True)
                nc.tensor.matmul(C1[d][:, DH:P], v3(LO[:, cb, d])[:, ci], v3(SV[:, cb, d])[:, ci, DH:P], start=True,
                                 stop=True).then_inc(s_c1[d], 1)

        def apply_chunk(cp, cb, i, first):
            for d in range(2):
                ci = ITEMS[d][i]
                pe.wait_ge(s_rb[d], 12 * cp + 4 * cb + i + 1)
                if i == 0:
                    pe.wait_ge(s_ac[d], NAC * (3 * cp + cb) + AC["q"])
                yc = 8 * cp + max(4 * (cb - 1) + i, 0)
                if not (first and yc == 0):
                    pe.wait_ge(s_y2[d], yc)
                nc.tensor.matmul(C2[d][:, 0:P], v3(QQ[:, cb, d])[:, ci], RB[:, d], start=True, stop=True).then_inc(s_c2[d], 1)

        def mod_row(p, j, first):
            if first and j == 0:
                pe.wait_ge(s_sb, 1)
            if not (first and j < 2):
                pe.wait_ge(s_me, 4 * p + j - 1)
            d = j % 2
            read = 4 * (3 * p + min(j, 2) - 1) + (j == 3)
            copied = [8 * p - 4, 8 * p, 8 * p, 8 * p + 1][j]
            if not first or read > 0:
                pe.wait_ge(s_rb[d], read)
            if not first or copied > 0:
                pe.wait_ge(s_y1[d], copied)
            pe.wait_ge(s_wr, 64 * p + 16 * j + 16)
            for k in range(KT):
                m = nc.tensor.matmul(C1[j % 2][:, P:P + 256], silb[:, k, :], wmr[:, k, :], start=k == 0, stop=k == KT - 1)
            m.then_inc(s_mr, 1)

        def four(f, s):
            for i in range(NB):
                m = f(i)
            m.then_inc(s, 1)

        def do(p, b, chain, first):
            n = 3 * p + b
            start = first and b == 0
            for d in range(2):
                pe.wait_ge(s_bkl[d], 16 * n + 16)
                if not start:
                    pe.wait_ge(s_vc[d], NVC * n)
                    pe.wait_ge(s_ac[d], NAC * n)
                four(lambda i: nc.tensor.transpose(W1[d][:, P * i:P * i + P], BKs[:, d, i], ident), s_mk[d])
                pe.wait_ge(s_vsl[d], 16 * n + 16)
                four(lambda i: nc.tensor.transpose(W2[d][:, P * i:P * i + P], VSs[:, d, i], ident), s_mk[d])
            for d in range(2):
                pe.wait_ge(s_ac[d], NAC * n + AC["vT"])
                four(lambda i: nc.tensor.matmul(W1[d][:, P * i:P * i + P], BKT[:, d, i], v3(SV[:, b, d])[:, i],
                                                start=True, stop=True), s_mk[d])
                pe.wait_ge(s_krl[2 * b + d], 64 * p + 64)
                if start and d == 0:
                    pe.wait_ge(s_nz, 6)
                four(lambda i: nc.tensor.matmul(W2[d][:, P * i:P * i + P], BKs[:, d, i], KRx[:, d, i, 0],
                                                start=True, stop=True), s_mk[d])
            for d in range(2):
                pe.wait_ge(s_vc[d], NVC * n + VC["kv"])
                four(lambda i: nc.tensor.matmul(W1[d][:, P * i:P * i + P], BKs[:, d, i], KRx[:, d, i, 1],
                                                start=True, stop=True), s_mk[d])
            mod_row(p, b, first)
            for d in range(2):
                pe.wait_ge(s_vc[d], NVC * n + VC["go"])
                four(lambda i: nc.tensor.transpose(W2[d][:, P * i:P * i + P], NBD[:, d, i], ident), s_mk[d])
            for l in range(LV):
                if b == 2 and l == 1:
                    mod_row(p, 3, first)
                for d in range(2):
                    if l == 0:
                        pe.wait_ge(s_pl[d], NPL * n + 2)
                        pe.wait_ge(s_ac[d], NAC * n + AC["m"])
                    else:
                        pe.wait_ge(s_vc[d], NVC * n + VC["x", l - 1])
                    four(lambda i: nc.tensor.matmul(W1[d][:, P * i:P * i + P], MBD[:, d, i], ZZ[:, d, i],
                                                    start=True, stop=True), s_mk[d])
                if chain and l < NB:
                    if l == 0:
                        pe.wait_ge(s_me, 4 * p + b + 1)
                    if b == 2 and l == 1:
                        pe.wait_ge(s_me, 4 * p + 4)
                    read_state(*chain, l, first)
                for d in range(2):
                    pe.wait_ge(s_vc[d], NVC * n + VC["a", l])
                    if l < LV - 1:
                        four(lambda i: nc.tensor.matmul(W2[d][:, P * i:P * i + P], XX[:, d, i], AA[:, d, i],
                                                        start=True, stop=True), s_mk[d])
                    four(lambda i: nc.tensor.matmul(W1[d][:, P * i:P * i + P], AA[:, d, i], XX[:, d, i],
                                                    start=True, stop=True), s_mk[d])
                if chain and l < NB:
                    apply_chunk(*chain, l, first)
            for d in range(2):
                pe.wait_ge(s_vc[d], NVC * n + VC["x", LV - 1])
                four(lambda i: nc.tensor.matmul(W2[d][:, P * i:P * i + P], XX[:, d, i], BKT[:, d, i],
                                                start=True, stop=True), s_mk[d])

        def tail():
            for i in range(NB):
                read_state(PAIRS - 1, 2, i, False)
                apply_chunk(PAIRS - 1, 2, i, False)
        steps4(pe, do, tail)

    wout_v = w_out[0].rearrange("(k p) n -> p k n", p=P)
    wq_v = peer_wq[0].rearrange("(k p) n -> p k n", p=P)
    skey_v = peer_subkeys[0].rearrange("h s k d -> k (h s) d")
    HS = 2 * HEADS

    def sync5(sp):
        sp.wait_ge(s_ys, PAIRS)
        sp.dma_start(brow[:, 0:4 * D], b_mod[0, 2 * D:6 * D].unsqueeze(0).broadcast_to([P, 4 * D])).then_inc(s_br, 16)
        sp.dma_start(brow[:, 4 * D:7 * D], norm_gains[0, 1:4].rearrange("g d -> (g d)").unsqueeze(0)
                     .broadcast_to([P, 3 * D])).then_inc(s_br, 16)
        sp.dma_start(wo, wout_v).then_inc(s_wo, 16)
        for i in range(8):
            sp.dma_start(wqA[:, i], wq_v[:, :, P * i:P * i + P]).then_inc(s_wa[i // 4], 16)
        sp.wait_ge(s_yg, 2 * PAIRS)
        sp.dma_start(skn, skey_v).then_inc(s_sk, 16)
        for i in range(8, HS):
            if i % 4 == 0:
                sp.wait_ge(s_q, i // 4 - 1)
            sp.dma_start(wqA[:, i % 8], wq_v[:, :, P * i:P * i + P]).then_inc(s_wa[i // 4 % 2], 16)
        sp.wait_ge(s_op, NT)
        for i in range(HS):
            if i >= 2:
                sp.wait_ge(s_qb, i - 1)
            sp.dma_start(wq2[:, i % 2], wq_v[:, :, P * i:P * i + P]).then_inc(s_wq[i % 2], 16)

    def pool5(pool):
        pool.wait_ge(s_ys, PAIRS)
        nc.gpsimd.memset(YT, 0.0).then_inc(s_yz, 1)

    def scalar5(act):
        y = ysum.rearrange("p a x v -> p (a x) v")
        act.wait_ge(s_hn, 2)
        nc.scalar.activation(ysq.rearrange("p a x v -> p (a x) v"), y, ACT.Square).then_inc(s_ha, 1)
        act.wait_ge(s_hn, 3)
        nc.scalar.activation(st5[:, 32:64], st5[:, 32:64], ACT.Sqrt, bias=eps[:, 2:3], scale=1.0 / DH).then_inc(s_ha, 1)
        for p in range(PAIRS):
            for b in range(2):
                act.wait_ge(s_yt, 2 * p + b + 1)
                bank = v3(psum[2 * p + b][:, :])
                for rows, cols in ((LOW, slice(DH, P)), (HIGH, slice(0, DH))):
                    o = yrw[rows, p, 256 * b:256 * b + 256].rearrange("p (i c) -> p i c", c=DH)
                    i = nc.scalar.activation(o, bank[rows, :, cols], ACT.Identity, bias=par[rows, p, LNX_B:LNX_B + 1],
                                             scale=par[rows, p, LNX_G:LNX_G + 1])
                i.then_inc(s_yv, 1)
        n = [0]

        def put(i):
            n[0] += 1
            i.then_inc(s_n1, 1)

        def columns(t):
            for h in range(2):
                act.wait_ge(s_h2t, 2 * t + h + 1)
                nc.scalar.activation(h2T[:, 4 * h:4 * h + 4, P * t:P * t + P], v3(psum[2 * t + h][:, :]),
                                     ACT.Identity).then_inc(s_h2e, 1)

        for t in range(NT):
            act.wait_ge(s_op, t + 1)
            for h in range(2):
                if n[0]:
                    act.wait_ge(s_n1, n[0])
                put(nc.scalar.activation(tmp5[:, 0:512], psum[2 * t + h][:, :], ACT.Square,
                                         accum_out=st5[:, 64 + 2 * t + h:65 + 2 * t + h]))
            if t >= 1:
                columns(t - 1)
            act.wait_ge(s_m1, 5 * t + 1)
            put(nc.scalar.activation(st5[:, 80 + t:81 + t], st5[:, 76 + t:77 + t], ACT.Sqrt, bias=eps[:, 0:1], scale=1.0 / D))
            act.wait_ge(s_m1, 5 * t + 4)
            act.wait_ge(s_n1, n[0])
            put(nc.scalar.activation(tmp5, xn[:, t, :], ACT.Square, accum_out=st5[:, 84 + t:85 + t]))
            act.wait_ge(s_n1, n[0])
            put(nc.scalar.activation(st5[:, 88 + t:89 + t], st5[:, 84 + t:85 + t], ACT.Sqrt, bias=eps[:, 0:1], scale=1.0 / D))
        act.wait_ge(s_row, 5)
        for b in range(4):
            act.wait_ge(s_skt, b + 1)
            nc.scalar.activation(skT[:, 4 * b:4 * b + 4], v3(psum[b][:, :]), ACT.Identity).then_inc(s_ske, 1)
        for b in range(4):
            act.wait_ge(s_q, b + 1)
            nc.scalar.activation(qT[:, b % 2], psum[4 + b % 2][:, :], ACT.Identity).then_inc(s_qe, 1)
            act.wait_ge(s_s, b + 1)
            nc.scalar.activation(SC[:, 0, 4 * b:4 * b + 4], v3(psum[b % 2][:, :]), ACT.Identity).then_inc(s_se, 1)
            if b == 0:
                act.wait_ge(s_se, 1)
                act.wait_ge(s_h2, 2 * NT)
                for h in range(2):
                    nc.scalar.activation(SCs[:, h], SC[:, 0, 2 * h:2 * h + 2, :], ACT.Identity).then_inc(s_scs, 1)
        columns(NT - 1)

    def vector5(dve):
        n = [0]

        def put(i):
            n[0] += 1
            i.then_inc(s_hn, 1)
            dve.wait_ge(s_hn, n[0])

        dve.wait_ge(s_ys, PAIRS)
        y = ysum.rearrange("p a x v -> p (a x) v")
        nc.vector.tensor_reduce(st5[:, 0:32], y, AX.X, ALU.add).then_inc(s_m0, 1)
        dve.wait_ge(s_m0, 1)
        put(nc.vector.tensor_scalar(st5[:, 0:32], st5[:, 0:32], 1.0 / DH, None, ALU.mult))
        put(nc.vector.tensor_tensor(y, y, st5[:, 0:32].unsqueeze(2).broadcast_to([P, 32, DH]), ALU.subtract))
        dve.wait_ge(s_ha, 1)
        put(nc.vector.tensor_reduce(st5[:, 32:64], ysq.rearrange("p a x v -> p (a x) v"), AX.X, ALU.add))
        dve.wait_ge(s_ha, 2)
        put(nc.vector.reciprocal(st5[:, 32:64], st5[:, 32:64]))
        dve.wait_ge(s_yz, 1)
        rs = st5[:, 32:64].unsqueeze(2).broadcast_to([P, 32, DH])
        nc.vector.tensor_tensor(YT[HIGH, :, 0:DH], y[HIGH], rs[HIGH], ALU.mult)
        put(nc.vector.tensor_tensor(YT[LOW, :, DH:P], y[LOW], rs[LOW], ALU.mult))
        for p in range(PAIRS):
            dve.wait_ge(s_yv, 2 * p + 2)
            nc.vector.tensor_tensor(yrw[:, p], yrw[:, p], bonus[:, p], ALU.add).then_inc(s_yg, 1)
            dve.wait_ge(s_yg, 2 * p + 1)
            nc.vector.tensor_tensor(yrw[:, p], yrw[:, p], gate[:, p], ALU.mult).then_inc(s_yg, 1)
        dve.wait_ge(s_br, 32)
        dve.wait_ge(s_me, 16)
        nc.vector.tensor_tensor(rows.rearrange("p a b -> p (a b)"), rows.rearrange("p a b -> p (a b)"), brow[:, 0:4 * D],
                                ALU.add).then_inc(s_row, 1)
        dve.wait_ge(s_row, 1)
        nc.vector.tensor_tensor(g1row, g1row, brow[:, 4 * D:5 * D], ALU.mult).then_inc(s_row, 1)
        nc.vector.scalar_tensor_tensor(a2row, a2row, 1.0, brow[:, 5 * D:6 * D], ALU.add, ALU.mult).then_inc(s_row, 1)
        nc.vector.tensor_tensor(g2row, g2row, brow[:, 6 * D:7 * D], ALU.mult).then_inc(s_row, 2)
        dve.wait_ge(s_row, 5)
        k = [0]

        def link(i):
            k[0] += 1
            i.then_inc(s_m1, 1)
            dve.wait_ge(s_m1, k[0])

        for t in range(NT):
            dve.wait_ge(s_n1, 5 * t + 2)
            link(nc.vector.tensor_tensor(st5[:, 76 + t:77 + t], st5[:, 64 + 2 * t:65 + 2 * t], st5[:, 65 + 2 * t:66 + 2 * t], ALU.add))
            dve.wait_ge(s_n1, 5 * t + 3)
            link(nc.vector.reciprocal(st5[:, 80 + t:81 + t], st5[:, 80 + t:81 + t]))
            for h in range(2):
                i = nc.vector.scalar_tensor_tensor(sh5[:, 512 * h:512 * h + 512], psum[2 * t + h][:, :],
                                                   st5[:, 80 + t:81 + t], g1row[:, 512 * h:512 * h + 512], ALU.mult, ALU.mult)
            link(i)
            link(nc.vector.tensor_tensor(xn[:, t, :], xn[:, t, :], sh5, ALU.add))
            dve.wait_ge(s_n1, 5 * t + 5)
            link(nc.vector.reciprocal(st5[:, 88 + t:89 + t], st5[:, 88 + t:89 + t]))
            nc.vector.scalar_tensor_tensor(H2N[:, t, :], xn[:, t, :], st5[:, 88 + t:89 + t], a2row, ALU.mult,
                                           ALU.mult).then_inc(s_h2, 1)
            dve.wait_ge(s_h2, 2 * t + 1)
            nc.vector.tensor_tensor(H2N[:, t, :], H2N[:, t, :], sh2row, ALU.add).then_inc(s_h2, 1)

    def tensor5(pe):
        pe.wait_ge(s_hn, 5)
        pe.wait_ge(s_me, 16)
        for b in range(8):
            for i in range(4):
                m = nc.tensor.transpose(psum[b][:, P * i:P * i + P], YT[:, 4 * b + i, :], ident)
            m.then_inc(s_yt, 1)
        def columns(t):
            pe.wait_ge(s_h2, 2 * t + 2)
            for h in range(2):
                for k in range(4):
                    m = nc.tensor.transpose(psum[2 * t + h][:, P * k:P * k + P],
                                            H2N[:, t, P * (4 * h + k):P * (4 * h + k) + P], ident)
                m.then_inc(s_h2t, 1)

        pe.wait_ge(s_wo, 16)
        pe.wait_ge(s_yg, 2 * PAIRS)
        for t in range(NT):
            for k in range(KT):
                a = (yconv if k < PAIRS else yrw)[:, k % PAIRS, P * t:P * t + P]
                for h in range(2):
                    m = nc.tensor.matmul(psum[2 * t + h][:, :], a, wo[:, k, 512 * h:512 * h + 512],
                                         start=k == 0, stop=k == KT - 1)
            m.then_inc(s_op, 1)
            if t:
                columns(t - 1)
        pe.wait_ge(s_sk, 16)
        pe.wait_ge(s_h2e, 4)
        for b in range(4):
            for i in range(4):
                m = nc.tensor.transpose(psum[b][:, P * i:P * i + P], skn[:, 4 * b + i], ident)
            m.then_inc(s_skt, 1)
        def queries(b):
            pe.wait_ge(s_wa[b % 2], 64 * (b // 2 + 1))
            if b >= 2:
                pe.wait_ge(s_qe, b - 1)
            else:
                pe.wait_ge(s_h2e, 6)
            for i in range(4):
                for k in range(KT):
                    m = nc.tensor.matmul(psum[4 + b % 2][:, P * i:P * i + P], wqA[:, 4 * (b % 2) + i, k, :], h2T[:, k, 0:P],
                                         start=k == 0, stop=k == KT - 1)
            m.then_inc(s_q, 1)

        def scores(b):
            pe.wait_ge(s_ske, 4)
            pe.wait_ge(s_qe, b + 1)
            if b >= 2:
                pe.wait_ge(s_se, b - 1)
            for i in range(4):
                m = nc.tensor.matmul(psum[b % 2][:, P * i:P * i + P], qT[:, b % 2, P * i:P * i + P], skT[:, 4 * b + i],
                                     start=True, stop=True)
            m.then_inc(s_s, 1)

        for b in range(4):
            queries(b)
            scores(b)
        columns(NT - 1)

    PO = [psum[6], psum[7]]
    NSL = TOPK
    out_v = out[0].rearrange("(t p) d -> t p d", p=P)

    def tiles6(engine, body, tail):
        body(0, True)
        with engine.Fori(1, NT) as t:
            body(t, False)
        tail()

    def sync6(sp):
        with sp.Fori(0, NT) as t:
            sp.wait_ge(s_fv, 4 * t + 8)
            sp.dma_start(out_v[t], ot).then_inc(s_out, 16)
        sp.wait_ge(s_out, 16 * NT + 16)

    def pool6(pool):
        pool.wait_ge(s_h2, 2 * NT)
        nc.gpsimd.iota(iot[:, 0:NCAND], pattern=[[1, NCAND]], base=0, channel_multiplier=0,
                       allow_small_or_imprecise_dtypes=True).then_inc(s_io, 1)

        def gather(kind, g, hi, j, first):
            ring, table, sems, used = [(U, peer_u[0], s_u, s_dot), (V, peer_v[0], s_v, s_mm)][kind]
            if not (first and hi == 0 and j < RING):
                pool.wait_ge(used, NSL * g + j + 1 - RING)
            apart(pool, s_pass_pool)
            pool.indirect_dma_start(ring[:, j % RING, :], None, table,
                                    bass.IndirectOffsetOnAxis(ap=idx[:, hi % 4, j:j + 1].bitcast(U32), axis=0)
                                    ).then_inc(sems[j % RING], 16)

        def body(t, first):
            for h in range(HEADS):
                g = t * HEADS + h
                pool.wait_ge(s_tk, g + 1)
                for j in range(NSL):
                    gather(0, g, h, j, first)
                    if h:
                        if first and h == 1 and j == 0:
                            pool.wait_ge(s_q, 4)
                        gather(1, g - 1, h - 1, j, first)
                    elif not first:
                        gather(1, g - 1, HEADS - 1, j, False)

        def tail():
            for j in range(NSL):
                gather(1, NT * HEADS - 1, HEADS - 1, j, False)
        tiles6(pool, body, tail)

    def scalar6(act):

        def stage_scores(t, h):
            g = t * HEADS + h
            nc.scalar.activation(SCs[:, h % 2], SC[:, t, 2 * h:2 * h + 2, :], ACT.Identity).then_inc(s_scs, 1)

        def diags(g, hp):
            for j in range(NSL):
                if not (isinstance(g, int) and g == 0 and j < 4):
                    act.wait_ge(s_mm, NSL * g + j - 3)
                nc.scalar.activation(diag[:, j % 4], ident, ACT.Identity, scale=wts[:, hp % 2, j:j + 1]).then_inc(s_dg, 1)

        def exps(g):
            act.wait_ge(s_tk, g + 1)
            if not (isinstance(g, int) and g == 0):
                act.wait_ge(s_gs, 2 * g)
            nc.scalar.activation(prob, top, ACT.Exp, bias=ntop[:, 0:1], accum_out=psum_[:, 0:1]).then_inc(s_ex, 1)

        def finish(t):
            act.wait_ge(s_mm, NSL * HEADS * (t + 1))
            act.wait_ge(s_fv, 4 * t + 4)
            nc.scalar.activation(fsq[:, 0:512], PO[0][:, :], ACT.Square, accum_out=fst[:, 0:1]).then_inc(s_fa, 1)
            act.wait_ge(s_fa, 3 * t + 1)
            nc.scalar.activation(fsq[:, 0:512], PO[1][:, :], ACT.Square, accum_out=fst[:, 1:2]).then_inc(s_fa, 1)
            act.wait_ge(s_fv, 4 * t + 5)
            nc.scalar.activation(fst[:, 3:4], fst[:, 2:3], ACT.Sqrt, bias=eps[:, 0:1], scale=1.0 / D).then_inc(s_fa, 1)

        exps(0)

        def late_scores(h):
            for a in range(2):
                act.wait_ge(s_qb, 2 * h + a + 1)
                nc.scalar.activation(qB[:, a], psum[2 + a][:, 0:3 * P], ACT.Identity).then_inc(s_qbe, 1)
            for a in range(2):
                act.wait_ge(s_sb6, 2 * h + a + 1)
                nc.scalar.activation(SC[:, 1:NT, 2 * h + a, :], v3(psum[a][:, 0:3 * P]), ACT.Identity).then_inc(s_sbe, 1)

        def body(t, first):
            for h in range(HEADS):
                g = t * HEADS + h
                if h == 0:
                    if not first:
                        act.wait_ge(s_dot, NSL * g)
                    nc.scalar.activation(h2cur, H2N[:, t, :], ACT.Identity).then_inc(s_hc, 1)
                if first:
                    late_scores(h)
                    if h == HEADS - 2:
                        act.wait_ge(s_sbe, 4)
                if h or not first:
                    act.wait_ge(s_wt, g)
                    diags(g - 1, (h - 1) % HEADS)
                act.wait_ge(s_tk, g + 1)
                if h < HEADS - 2:
                    stage_scores(t, h + 2)
                else:
                    stage_scores(t + 1, h + 2 - HEADS)
                exps(g + 1)
                act.wait_ge(s_dot, NSL * (g + 1))
                nc.scalar.activation(gel[:, h % 2], acts[:, h % 2], ACT.Gelu).then_inc(s_ge, 1)
                if h == 0 and not first:
                    finish(t - 1)

        def tail():
            g = NT * HEADS
            act.wait_ge(s_wt, g)
            diags(g - 1, HEADS - 1)
            finish(NT - 1)
        tiles6(act, body, tail)

    def vector6(dve):
        NL = LINKS

        def topk(g, hp, first):
            n = [0]

            def link(i):
                n[0] += 1
                i.then_inc(s_lk, 1)
                dve.wait_ge(s_lk, NL * g + n[0])
                apart(dve, s_pass_dve)

            dve.wait_ge(s_scs, g + 1)
            apart(dve, s_pass_dve)
            a = SCs[:, hp % 2]
            u16, p16 = i16.bitcast(U32), pos.bitcast(U32)
            for s in range(2):
                i = nc.vector.max(v16[:, s, 0:8], a[:, s])
            link(i)
            for s in range(2):
                nc.vector.max_index(u16[:, s, 0:8], v16[:, s, 0:8], a[:, s])
                i = nc.vector.match_replace(mr[:, s], v16[:, s, 0:8], a[:, s], -3.0e38)
            link(i)
            for s in range(2):
                i = nc.vector.max(v16[:, s, 8:16], mr[:, s])
            link(i)
            for s in range(2):
                i = nc.vector.max_index(u16[:, s, 8:16], v16[:, s, 8:16], mr[:, s])
            link(i)
            link(nc.vector.tensor_copy(i16f, u16))
            link(nc.vector.tensor_scalar(i16f[:, 0], i16f[:, 0], float(KEYS), None, ALU.mult))
            at = 0
            for r, m, w in ROWS:
                for src, dst, op in ((v16, cand, ALU.add), (i16f, cid, ALU.add)):
                    i = nc.vector.tensor_tensor(dst[:, at:at + m * w].rearrange("p (a b) -> p a b", b=w),
                                                src[:, 0, r:r + m].unsqueeze(2).broadcast_to([P, m, w]),
                                                src[:, 1, 0:w].unsqueeze(1).broadcast_to([P, m, w]), op)
                at += m * w
            link(i)
            if not first:
                dve.wait_ge(s_ex, g)
                apart(dve, s_pass_dve)
            link(nc.vector.max(top[:, 0:8], cand[:, 0:NCAND]))
            nc.vector.max_index(p16[:, 0:8], top[:, 0:8], cand[:, 0:NCAND])
            link(nc.vector.match_replace(cmr[:, 0:NCAND], top[:, 0:8], cand[:, 0:NCAND], -3.0e38))
            link(nc.vector.max(top[:, 8:16], cmr[:, 0:NCAND]))
            nc.vector.tensor_scalar(ntop[:, 0:1], top[:, 0:1], -1.0, None, ALU.mult)
            link(nc.vector.max_index(p16[:, 8:16], top[:, 8:16], cmr[:, 0:NCAND]))
            link(nc.vector.tensor_copy(posf, p16))
            link(nc.vector.tensor_tensor(oh, iot[:, 0:NCAND].unsqueeze(1).broadcast_to([P, TOPK, NCAND]),
                                         posf.unsqueeze(2).broadcast_to([P, TOPK, NCAND]), ALU.is_equal))
            link(nc.vector.tensor_tensor(oh, oh, cid[:, 0:NCAND].unsqueeze(1).broadcast_to([P, TOPK, NCAND]), ALU.mult))
            link(nc.vector.tensor_reduce(exf, oh, AX.X, ALU.add))
            assert n[0] == NL, n[0]
            nc.vector.tensor_copy(idx[:, hp % 4].bitcast(U32), exf).then_inc(s_tk, 1)

        def softmax(g, hp):
            dve.wait_ge(s_ex, g + 1)
            nc.vector.reciprocal(psum_[:, 1:2], psum_[:, 0:1]).then_inc(s_gs, 1)
            dve.wait_ge(s_gs, 2 * g + 1)
            nc.vector.tensor_scalar(gsm[:, hp % 2], prob, psum_[:, 1:2], None, ALU.mult).then_inc(s_gs, 1)

        def finish(t):
            dve.wait_ge(s_fa, 3 * t + 2)
            nc.vector.tensor_tensor(fst[:, 2:3], fst[:, 0:1], fst[:, 1:2], ALU.add).then_inc(s_fv, 1)
            dve.wait_ge(s_fa, 3 * t + 3)
            nc.vector.reciprocal(fst[:, 4:5], fst[:, 3:4]).then_inc(s_fv, 1)
            dve.wait_ge(s_fv, 4 * t + 6)
            dve.wait_ge(s_out, 16 * t + 16)
            for h in range(2):
                i = nc.vector.scalar_tensor_tensor(ot[:, 512 * h:512 * h + 512], PO[h][:, :], fst[:, 4:5],
                                                   g2row[:, 512 * h:512 * h + 512], ALU.mult, ALU.mult)
            i.then_inc(s_fv, 1)
            dve.wait_ge(s_fv, 4 * t + 7)
            nc.vector.tensor_tensor(ot, ot, xn[:, t, :], ALU.add).then_inc(s_fv, 1)

        credit(dve, s_fv, 4)
        credit(dve, s_out, 16)
        dve.wait_ge(s_io, 1)
        topk(0, 0, True)
        softmax(0, 0)

        def body(t, first):
            for h in range(HEADS):
                g = t * HEADS + h
                if h == 0:
                    dve.wait_ge(s_hc, t + 1)
                if h >= 3 or not first:
                    dve.wait_ge(s_mm, NSL * (g - 2))
                topk(g + 1, (h + 1) % HEADS, False)
                for j in range(NSL):
                    dve.wait_ge(s_u[j % RING], 32 * g + 16 * (j // RING) + 16)
                    nc.vector.tensor_tensor_reduce(U[:, j % RING, :], U[:, j % RING, :], h2cur, 1.0, 0.0, ALU.mult, ALU.add,
                                                   acts[:, h % 2, j:j + 1]).then_inc(s_dot, 1)
                softmax(g + 1, (h + 1) % HEADS)
                dve.wait_ge(s_ge, g + 1)
                if h >= 2 or not first:
                    dve.wait_ge(s_dg, NSL * (g - 1))
                nc.vector.tensor_tensor(wts[:, h % 2], gel[:, h % 2], gsm[:, h % 2], ALU.mult).then_inc(s_wt, 1)
                if h == 0 and not first:
                    finish(t - 1)

        tiles6(dve, body, lambda: finish(NT - 1))

    def tensor6(pe):
        def experts(g, hp, first):
            for j in range(NSL):
                pe.wait_ge(s_dg, NSL * g + j + 1)
                pe.wait_ge(s_v[j % RING], 32 * g + 16 * (j // RING) + 16)
                for h in range(2):
                    m = nc.tensor.matmul(PO[h][:, :], diag[:, j % 4], V[:, j % RING, 512 * h:512 * h + 512],
                                         start=hp == 0 and j == 0, stop=hp == HEADS - 1 and j == NSL - 1)
                m.then_inc(s_mm, 1)

        def late_scores(h):
            for a in range(2):
                i = 2 * h + a
                pe.wait_ge(s_wq[a], 16 * h + 16)
                if h:
                    pe.wait_ge(s_qbe, i - 1)
                for k in range(KT):
                    m = nc.tensor.matmul(psum[2 + a][:, 0:3 * P], wq2[:, a, k, :], h2T[:, k, P:T], start=k == 0, stop=k == KT - 1)
                m.then_inc(s_qb, 1)
            for a in range(2):
                i = 2 * h + a
                pe.wait_ge(s_qbe, i + 1)
                if h:
                    pe.wait_ge(s_sbe, i - 1)
                else:
                    pe.wait_ge(s_se, 4)
                for t in range(3):
                    m = nc.tensor.matmul(psum[a][:, P * t:P * t + P], qB[:, a, P * t:P * t + P], skT[:, i],
                                         start=True, stop=True)
                m.then_inc(s_sb6, 1)

        pe.wait_ge(s_h2e, 2 * NT)

        def body(t, first):
            for h in range(HEADS):
                g = t * HEADS + h
                if first:
                    late_scores(h)
                if h:
                    if h == 1 and not first:
                        pe.wait_ge(s_fv, 4 * t + 4)
                    experts(g - 1, h - 1, first)
                elif not first:
                    experts(g - 1, HEADS - 1, False)
        tiles6(pe, body, lambda: experts(NT * HEADS - 1, HEADS - 1, False))


    n_masks = 4 + 4 * 6 + 16 + 12 + 12
    LATER = {'sync': (sync4, sync5, sync6), 'pool': (pool4, pool5, pool6), 'scalar': (scalar4, scalar5, scalar6),
             'vector': (vector4, vector5, vector6), 'tensor': (tensor4, tensor5, tensor6)}

    @block.sync
    def _(sp):
        sp.dma_start(cc[:, 0, :], c[0].rearrange("(p k) -> p k", k=KT)).then_inc(s_c, 16)
        sp.dma_start(cc[:, 1, :], c_ctx.rearrange("(p k) -> p k", k=KT)).then_inc(s_c, 16)
        for i in range(8):
            sp.dma_start(wm[:, i], wmod_v[:, :, 256 * i:256 * i + 256]).then_inc(s_wm[i], 16)
            if i == 2:
                for t in range(NTC):
                    sp.dma_start(ctxn[:, t, :], ctx_v[t]).then_inc(s_ctx, 16)
            if i == 6:
                sp.dma_start(prow[0:16, :], b_mod[0, 0:2048].rearrange("(r q) -> r q", q=P)).then_inc(s_prow, 16)
                sp.dma_start(prow[16:24, :], norm_gains[0, 0].rearrange("(r q) -> r q", q=P)).then_inc(s_prow, 16)
                par_rows = [tshift_mu[0, 0, 0], tshift_mu[0, 0, 1], tshift_mu[0, 0, 2],
                        tshift_mu[0, 1, 0], tshift_mu[0, 1, 1], tshift_mu[0, 1, 2],
                        decay_w0[0, 0], decay_w0[0, 1], iclr_a0[0, 0], iclr_a0[0, 1],
                        k_k[0], k_a[0], r_k[0].rearrange("h n -> (h n)"), lnx_g[0], lnx_b[0],
                        conv_w[0, 0], conv_w[0, 1], conv_w[0, 2]]
                for n, row in enumerate(par_rows):
                    sp.dma_start(prow2[4 * n:4 * n + 4, :], row.rearrange("(r q) -> r q", q=P)).then_inc(s_prow, 16)
            if i >= 4:
                sp.dma_start(xn[:, i - 4, :], x_v[i - 4]).then_inc(s_x[i - 4], 16)
        for j, col in enumerate([25 * P, 26 * P, 24 * P]):
            sp.dma_start(wring[:, j], win_v[:, :, col:col + P]).then_inc(s_w[j], 16)
        sp.wait_ge(s_hT, 6)
        sp.wait_ge(s_hU, 6)

        def lora_loads(p):
            for d in range(2):
                sp.dma_start(lora[DH * d:DH * d + DH, d, 0, :],
                             decay_w2[0, d, :, bass.ds(p * P, P)]).then_inc(s_lora, 16)
                sp.dma_start(lora[DH * d:DH * d + DH, d, 1, :],
                             iclr_a2[0, d, :, bass.ds(p * P, P)]).then_inc(s_lora, 16)
            sp.dma_start(gw, gate_w2[0, :, bass.ds(p * P, P)]).then_inc(s_lora, 16)

        def pair_loads(p, first):
            for j, base in enumerate((16, 12, 20)):
                sp.wait_ge(s_pj, 3 * p + j + 1)
                sp.dma_start(wring[:, j], win_v[:, :, bass.ds(base * P + p * P, P)]).then_inc(s_w[j], 16)
            if not first:
                sp.wait_ge(s_ax, 7 * p)
                apart(sp, s_pass_sp)
            lora_loads(p)

        sp.wait_ge(s_pz, 1)
        pair_loads(0, True)
        with sp.Fori(1, PAIRS) as p:
            pair_loads(p, False)
        for j, base in enumerate((4, 8, 0)):
            sp.wait_ge(s_pj, 3 * PAIRS + j + 1)
            sp.dma_start(wring[:, j], win_v[:, :, base * P:base * P + P]).then_inc(s_w[j], 16)
        with sp.Fori(1, PAIRS) as q:
            for j, base in enumerate((4, 8, 0)):
                sp.wait_ge(s_pj, 3 * (q + PAIRS) + j + 1)
                apart(sp, s_pass_sp)
                sp.dma_start(wring[:, j], win_v[:, :, bass.ds(base * P + q * P, P)]).then_inc(s_w[j], 16)
        sp.wait_ge(s_spill, 16 * 5 * PAIRS)
        for stage in LATER["sync"]:
            stage(sp)

    @block.gpsimd
    def _(pool):
        n = [0]

        def put(i, done=s_const):
            n[0] += 1
            i.then_inc(done, 1)
            pool.wait_ge(done, n[0])

        put(nc.gpsimd.memset(ident, 0.0))
        put(nc.gpsimd.memset(head_ones, 0.0))
        put(nc.gpsimd.memset(eps[:, 0:1], NORM_EPS))
        put(nc.gpsimd.memset(eps[:, 1:2], 1e-12))
        put(nc.gpsimd.memset(eps[:, 2:3], LNX_EPS))
        put(nc.gpsimd.memset(eps[:, 3:4], 0.0))
        put(nc.gpsimd.memset(par[:, PAIRS], 0.0))
        put(nc.gpsimd.affine_select(out=ident, in_=ident, compare_op=ALU.not_equal, fill=1.0, base=0,
                                    pattern=[[-1, P]], channel_multiplier=1))
        put(nc.gpsimd.memset(head_ones[0:DH, 0:DH], 1.0))
        put(nc.gpsimd.memset(head_ones[DH:P, DH:P], 1.0))
        assert pool_masks(pool) == n_masks
        pool.wait_ge(s_hT, 6)
        pool.wait_ge(s_hU, 6)
        n[0] = 0
        for tile in (lora, kraw, vraw, rraw, VSb, KRb):
            put(nc.gpsimd.memset(tile, 0.0), s_pz)
        put(nc.gpsimd.memset(scan_keep, 1.0), s_pz)
        put(nc.gpsimd.memset(scan_keep.rearrange("p (n c) -> p n c", c=C)[:, :, 0:1], 0.0), s_pz)
        def spills(p):
            pool.wait_ge(s_vs, 2 * p + 2)
            apart(pool, s_pass_pool)
            pool.dma_start(vs_dram[p], VSb.rearrange("p a b -> p (a b)")).then_inc(s_spill, 16)
            for d in range(2):
                pool.wait_ge(s_bk, 2 * p + d + 1)
                apart(pool, s_pass_pool)
                pool.dma_start(bk_dram[2 * p + d], BKb[:, d].rearrange("p a b -> p (a b)")).then_inc(s_spill, 16)
                pool.dma_start(kr_dram[2 * p + d], KRb[:, d].rearrange("p a b -> p (a b)")).then_inc(s_spill, 16)

        spills(0)
        with pool.Fori(1, PAIRS) as p:
            spills(p)
        for stage in LATER["pool"]:
            stage(pool)

    @block.scalar
    def _(act):
        act.wait_ge(s_c, 32)
        nc.scalar.activation(ccs, cc, ACT.Sigmoid).then_inc(s_silu, 1)
        act.wait_ge(s_const, 6)
        for i in range(NTC + NT):
            if i < NTC:
                act.wait_ge(s_ctx, 16 * NTC)
                src = ctxn[:, i, :]
            else:
                act.wait_ge(s_x[i - NTC], 16)
                src = xn[:, i - NTC, :]
            if i:
                act.wait_ge(s_ssq, i)
            nc.scalar.activation(sq, src, ACT.Square, accum_out=ssq[:, i:i + 1]).then_inc(s_ssq, 1)
        act.wait_ge(s_ssq, NTC + NT)
        nc.scalar.activation(rstd[:, 0:6], ssq[:, 0:6], ACT.Sqrt, bias=eps[:, 0:1], scale=1.0 / D).then_inc(s_ssq, 1)
        for b in range(4):
            act.wait_ge(s_mod, 2 * b + 2)
            nc.scalar.activation(modrow[0:2, T * b:T * b + T], psum[b][0:2, :], ACT.Identity).then_inc(s_mrow, 1)
        act.wait_ge(s_modc, 3)
        for t in range(NTC + NT):
            which = 1 if t < NTC else 0
            act.wait_ge(s_tr, 2 * t + 1)
            for k in range(4):
                i = nc.scalar.activation(hT[:, k, P * t:P * t + P], psum[2 * (t % 3)][:, P * k:P * k + P],
                                         ACT.Identity, bias=shsc[:, k, which:which + 1],
                                         scale=tab[:, k, which:which + 1])
            i.then_inc(s_hT, 1)
        act.wait_ge(s_pj, 1)
        nc.scalar.activation(lo_w[:, TC:TT], psum[0][:, 0:T], ACT.Tanh)
        nc.scalar.activation(lo_w[:, 0:TC], psum[1][:, 0:TC], ACT.Tanh).then_inc(s_pe, 1)
        act.wait_ge(s_pj, 2)
        nc.scalar.activation(lo_a[:, TC:TT], psum[2][:, 0:T], ACT.Identity)
        nc.scalar.activation(lo_a[:, 0:TC], psum[3][:, 0:TC], ACT.Identity).then_inc(s_pe, 1)
        act.wait_ge(s_pj, 3)
        nc.scalar.activation(lo_g, psum[4][:, 0:T], ACT.Sigmoid).then_inc(s_pe, 1)

        def pair(p, first):
            def aux(d, which):
                act.wait_ge(s_ax, 7 * p + [[1, 2], [4, 6]][d][which])
                if which == 0 and (d or not first):
                    act.wait_ge(s_cum, 2 * p + d)
                if which == 1 and not first:
                    act.wait_ge(s_bk, 2 * p - 1 + d)
                dst, col = [sg, aa[:, d]][which], 2 * which + d
                bx, bc = (0, 1) if (d, which) == (1, 0) else (5, 6)
                nc.scalar.activation(dst[:, TC:TT], psum[bx][:, 0:T], ACT.Sigmoid, bias=bias4[:, col:col + 1])
                nc.scalar.activation(dst[:, 0:TC], psum[bc][:, 0:TC], ACT.Sigmoid,
                                     bias=bias4[:, col:col + 1]).then_inc(s_ae, 1)

            def factors(d):
                act.wait_ge(s_cum, 2 * p + d + 1)
                if d or not first:
                    act.wait_ge(s_bk, 2 * p + d)
                nc.scalar.activation(e1, ex, ACT.Exp, scale=-DECAY)
                nc.scalar.activation(e3, inc, ACT.Exp, scale=DECAY)
                nc.scalar.activation(e2, inc, ACT.Exp, scale=-DECAY).then_inc(s_e, 1)

            act.wait_ge(s_pj, 3 * p + 4)
            if first:
                act.wait_ge(s_pz, 8)
            else:
                act.wait_ge(s_sh, 3 * p)
            nc.scalar.activation(kraw[:, XO:XO + T], psum[0][:, 0:T], ACT.Identity)
            nc.scalar.activation(kraw[:, CO:CO + TC], psum[1][:, 0:TC], ACT.Identity).then_inc(s_pe, 1)
            act.wait_ge(s_b4, p + 1)
            aux(0, 0)
            act.wait_ge(s_pj, 3 * p + 5)
            nc.scalar.activation(rraw[:, 1:1 + T], psum[2][:, 0:T], ACT.Identity).then_inc(s_pe, 1)
            aux(0, 1)
            act.wait_ge(s_sh, 3 * p + 1)
            nc.scalar.activation(sqk, kS, ACT.Square, scale=pp[:, K_K:K_K + 1]).then_inc(s_kk, 1)
            act.wait_ge(s_pj, 3 * p + 6)
            nc.scalar.activation(vraw[:, XO:XO + T], psum[3][:, 0:T], ACT.Identity)
            nc.scalar.activation(vraw[:, CO:CO + TC], psum[4][:, 0:TC], ACT.Identity).then_inc(s_pe, 1)
            act.wait_ge(s_ax, 7 * p + 3)
            nc.scalar.activation(t2[:, TC:TT], psum[5][:, 0:T], ACT.Sqrt, bias=eps[:, 1:2])
            nc.scalar.activation(t2[:, 0:TC], psum[6][:, 0:TC], ACT.Sqrt, bias=eps[:, 1:2]).then_inc(s_ae, 1)
            aux(1, 0)
            factors(0)
            act.wait_ge(s_sh, 3 * p + 3)
            if not first:
                act.wait_ge(s_spill, 16 * 5 * p)
            v_c = vS.rearrange("p (n c) -> p n c", c=C)
            nc.scalar.activation(VSb[0:DH, :, DH:P], v_c[0:DH], ACT.Identity).then_inc(s_vs, 1)
            nc.scalar.activation(VSb[DH:P, :, 0:DH], v_c[DH:P], ACT.Identity).then_inc(s_vs, 1)
            act.wait_ge(s_ax, 7 * p + 5)
            nc.scalar.activation(gate[:, p, :], psum[2][:, 0:T], ACT.Identity).then_inc(s_ae, 1)
            aux(1, 1)
            factors(1)

        pair(0, True)
        with act.Fori(1, PAIRS) as p:
            pair(p, False)
        act.wait_ge(s_bk, 2 * PAIRS)
        credit(act, s_cv, 4)
        with act.Fori(0, PAIRS) as q:
            act.wait_ge(s_pj, 3 * q + 3 * PAIRS + 4)
            act.wait_ge(s_cv, q * 4 + 4)
            nc.scalar.activation(t1[:, 0:T], psum[0][:, 0:T], ACT.Identity).then_inc(s_pe, 1)
        for stage in LATER["scalar"]:
            stage(act)

    @block.vector
    def _(dve):
        n_dv = [0]

        dve.wait_ge(s_silu, 1)
        nc.vector.tensor_tensor(silu_col.rearrange("p k v -> p v k"), cc, ccs, ALU.mult).then_inc(s_silu, 1)
        dve.wait_ge(s_ptr, 1)
        nc.vector.tensor_copy(pcolA[:, 0:24], psum[4][:, 0:24]).then_inc(s_pcol, 1)
        dve.wait_ge(s_ptr, 2)
        nc.vector.tensor_copy(par[:, 0:PAIRS].rearrange("p r i -> p i r"),
                              psum[5][:, 0:4 * NPAR].rearrange("p (i r) -> p i r", r=PAIRS)).then_inc(s_pcol, 1)
        dve.wait_ge(s_const, 10)
        nc.vector.tensor_copy(mix_diag, head_ones).then_inc(s_pcol, 1)
        dve.wait_ge(s_ssq, NTC + NT + 1)
        nc.vector.reciprocal(rstd[:, 0:6], rstd[:, 0:6]).then_inc(s_rstd, 1)
        dve.wait_ge(s_rstd, 1)
        for t in range(NTC + NT):
            src = ctxn[:, t, :] if t < NTC else xn[:, t - NTC, :]
            nc.vector.tensor_scalar(xs[:, t, :], src, rstd[:, t:t + 1], None, ALU.mult).then_inc(s_xs, 1)
        dve.wait_ge(s_mod, 9)
        dve.wait_ge(s_pcol, 3)
        nc.vector.tensor_tensor(shsc, psum[6][:, 0:32].rearrange("p (a b) -> p a b", b=2),
                                pcolA[:, 0:16].unsqueeze(2).broadcast_to([P, 16, 2]), ALU.add).then_inc(s_modc, 1)
        dve.wait_ge(s_modc, 1)
        nc.vector.tensor_scalar(tab, shsc[:, 8:16], 1.0, None, ALU.add).then_inc(s_modc, 1)
        dve.wait_ge(s_modc, 2)
        nc.vector.tensor_tensor(tab, tab, pcolA[:, 16:24].unsqueeze(2).broadcast_to([P, 8, 2]),
                                ALU.mult).then_inc(s_modc, 1)
        dve.wait_ge(s_modc, 3)
        for t in range(NTC + NT):
            which = 1 if t < NTC else 0
            dve.wait_ge(s_tr, 2 * t + 2)
            for k in range(4, 8):
                i = nc.vector.tensor_scalar(hT[:, k, P * t:P * t + P], psum[2 * (t % 3) + 1][:, P * (k - 4):P * (k - 4) + P],
                                            tab[:, k, which:which + 1], shsc[:, k, which:which + 1], ALU.mult, ALU.add)
            i.then_inc(s_hU, 1)
        dve.wait_ge(s_pz, 8)
        nc.vector.tensor_copy(bias4, par[:, 0, W0_F:W0_F + 4]).then_inc(s_b4, 1)

        def chunks(a):
            return a.rearrange("p (n c) -> p n c", c=C)

        def pair(p, first):
            n_dv[0] = 0
            base = p * PAIR_STEPS

            def link(ins):
                n_dv[0] += 1
                ins.then_inc(s_dv, 1)
                dve.wait_ge(s_dv, base + n_dv[0])

            def shift(raw, off, cols, dst, dst0, c0, mp, mn):
                o = dst[:, dst0:dst0 + cols]
                link(nc.vector.tensor_scalar(o, raw[:, off:off + cols], pp[:, c0:c0 + 1], None, ALU.mult))
                link(nc.vector.scalar_tensor_tensor(o, raw[:, off - 1:off - 1 + cols], pp[:, mp:mp + 1], o, ALU.mult, ALU.add))
                return nc.vector.scalar_tensor_tensor(o, raw[:, off + 1:off + 1 + cols], pp[:, mn:mn + 1], o, ALU.mult, ALU.add)

            if not first:
                dve.wait_ge(s_ae, 6 * p)
            nc.vector.tensor_copy(pp[:, 0:NPAR], par[:, p, :]).then_inc(s_pp, 1)
            dve.wait_ge(s_pp, 6 * p + 1)
            nc.vector.tensor_scalar(pp[:, C0_R:C0_R + 3], pp[:, MP_R:MP_R + 3], -1.0, 1.0, ALU.mult, ALU.add).then_inc(s_pp, 1)
            nc.vector.tensor_scalar(pp[:, OMKA:OMKA + 1], pp[:, K_A:K_A + 1], -1.0, 1.0, ALU.mult, ALU.add).then_inc(s_pp, 1)
            dve.wait_ge(s_pp, 6 * p + 3)
            nc.vector.tensor_tensor(pp[:, C0_R:C0_R + 3], pp[:, C0_R:C0_R + 3], pp[:, MN_R:MN_R + 3], ALU.subtract).then_inc(s_pp, 3)
            dve.wait_ge(s_pp, 6 * p + 6)
            dve.wait_ge(s_pe, 3 * p + 4)
            link(shift(kraw, CO, TC, kS, 0, C0_K, MP_K, MN_K))
            shift(kraw, XO, T, kS, TC, C0_K, MP_K, MN_K).then_inc(s_sh, 1)

            def cumulate(d):
                dve.wait_ge(s_ae, 6 * p + [1, 4][d])
                if d or not first:
                    dve.wait_ge(s_e, 2 * p + d)
                link(nc.vector.tensor_tensor_scan(cs, scan_keep, sg, 0.0, ALU.mult, ALU.add))
                if d == 0:
                    link(nc.vector.tensor_copy(inc, cs))
                    nc.vector.tensor_tensor(ex, cs, sg, ALU.subtract).then_inc(s_cum, 1)
                else:
                    tot = chunks(cs)[:, :, C - 1:C].broadcast_to([P, NCH, C])
                    link(nc.vector.tensor_tensor(chunks(ex), tot, chunks(cs), ALU.subtract))
                    nc.vector.tensor_tensor(inc, ex, sg, ALU.add).then_inc(s_cum, 1)

            def products(d):
                dve.wait_ge(s_e, 2 * p + d + 1)
                dve.wait_ge(s_ae, 6 * p + [2, 6][d])
                if not first:
                    dve.wait_ge(s_spill, 16 * 5 * p)
                link(nc.vector.tensor_scalar(t1, aa[:, d], pp[:, K_A:K_A + 1], pp[:, OMKA:OMKA + 1], ALU.mult, ALU.add))
                link(nc.vector.tensor_tensor(t1, t1, kS, ALU.mult))
                k3 = chunks(t1)
                f1, f2, f3, kk3, r3 = chunks(e1), chunks(e2), chunks(e3), chunks(kk), chunks(rS)
                lo, hi = slice(0, DH), slice(DH, P)
                link(nc.vector.tensor_tensor(BKb[lo, d, :, DH:P], k3[lo], f3[lo], ALU.mult))
                link(nc.vector.tensor_tensor(BKb[hi, d, :, 0:DH], k3[hi], f3[hi], ALU.mult))
                link(nc.vector.scalar_tensor_tensor(t1, kk, -1.0, aa[:, d], ALU.mult, ALU.mult))
                link(nc.vector.tensor_tensor(BKb[lo, d, :, 0:DH], k3[lo], f3[lo], ALU.mult))
                link(nc.vector.tensor_tensor(BKb[hi, d, :, DH:P], k3[hi], f3[hi], ALU.mult))
                link(nc.vector.tensor_tensor(KRb[lo, d, :, 0:DH], kk3[lo], f1[lo], ALU.mult))
                link(nc.vector.tensor_tensor(KRb[hi, d, :, DH:P], kk3[hi], f1[hi], ALU.mult))
                link(nc.vector.tensor_tensor(KRb[lo, d, TC // C:, DH:P], r3[lo], f2[lo, TC // C:], ALU.mult))
                link(nc.vector.tensor_tensor(KRb[hi, d, TC // C:, 0:DH], r3[hi], f2[hi, TC // C:], ALU.mult))
                at = C - 1 if d == 0 else 0
                nc.vector.tensor_copy(pc_all[:, p * 2 + d, :], f2[:, :, at]).then_inc(s_bk, 1)

            cumulate(0)
            dve.wait_ge(s_pe, 3 * p + 5)
            shift(rraw, 1, T, rS, 0, C0_R, MP_R, MN_R).then_inc(s_sh, 1)
            dve.wait_ge(s_sh, 3 * p + 2)
            nc.vector.scalar_tensor_tensor(rk, rS, pp[:, R_K:R_K + 1], kS[:, TC:TT], ALU.mult, ALU.mult).then_inc(s_bn, 1)
            dve.wait_ge(s_pe, 3 * p + 6)
            if not first:
                dve.wait_ge(s_vs, 2 * p)
            link(shift(vraw, CO, TC, vS, 0, C0_V, MP_V, MN_V))
            shift(vraw, XO, T, vS, TC, C0_V, MP_V, MN_V).then_inc(s_sh, 1)
            dve.wait_ge(s_ae, 6 * p + 3)
            link(nc.vector.reciprocal(t2, t2))
            link(nc.vector.scalar_tensor_tensor(kk, kS, pp[:, K_K:K_K + 1], t2, ALU.mult, ALU.mult))
            products(0)
            dve.wait_ge(s_ax, 7 * p + 7)
            dve.wait_ge(s_sh, 3 * p + 3)
            nc.vector.tensor_tensor(bonus[:, p, :], psum[7][:, 0:T], vS[:, TC:TT], ALU.mult).then_inc(s_bd, 1)
            cumulate(1)
            dve.wait_ge(s_ae, 6 * p + 6)
            nc.vector.tensor_copy(bias4, par[:, p + 1, W0_F:W0_F + 4]).then_inc(s_b4, 1)
            products(1)
            return n_dv[0]

        n = pair(0, True)
        assert n == PAIR_STEPS, n
        with dve.Fori(1, PAIRS) as p:
            pair(p, False)

        def rows(a):
            return a.rearrange("p (n c) -> p n c", c=GRID)

        with dve.Fori(0, PAIRS) as q:
            nc.vector.tensor_copy(pp[:, 0:NPAR], par[:, q, :]).then_inc(s_pp, 1)
            dve.wait_ge(s_pp, q + 6 * PAIRS + 1)
            dve.wait_ge(s_pe, q + 3 * PAIRS + 4)
            dve.wait_ge(s_pj, 3 * q + 3 * PAIRS + 5)
            nc.vector.tensor_tensor(t2[:, 0:T], t1[:, 0:T], psum[2][:, 0:T], ALU.mult).then_inc(s_cv, 1)
            dve.wait_ge(s_cv, q * 4 + 5)
            nc.vector.tensor_scalar(cs[:, 0:T], t2[:, 0:T], pp[:, CV1:CV1 + 1], None, ALU.mult).then_inc(s_cv, 1)
            dve.wait_ge(s_cv, q * 4 + 6)
            z, o = rows(t2[:, 0:T]), rows(cs[:, 0:T])
            nc.vector.scalar_tensor_tensor(o[:, :, 1:], z[:, :, :-1], pp[:, CV0:CV0 + 1], o[:, :, 1:],
                                           ALU.mult, ALU.add).then_inc(s_cv, 1)
            dve.wait_ge(s_cv, q * 4 + 7)
            nc.vector.scalar_tensor_tensor(o[:, :, :-1], z[:, :, 1:], pp[:, CV2:CV2 + 1], o[:, :, :-1],
                                           ALU.mult, ALU.add).then_inc(s_cv, 1)
            dve.wait_ge(s_cv, q * 4 + 8)
            dve.wait_ge(s_pj, 3 * q + 3 * PAIRS + 6)
            nc.vector.tensor_tensor(yconv[:, q, :], psum[3][:, 0:T], cs[:, 0:T], ALU.mult).then_inc(s_done3, 1)
        for stage in LATER["vector"]:
            stage(dve)

    @block.tensor
    def _(pe):
        pe.wait_ge(s_const, 8)
        pe.wait_ge(s_silu, 2)
        for i in range(8):
            pe.wait_ge(s_wm[i], 16)
            for k in range(KT):
                m = nc.tensor.matmul(psum[i // 2][0:2, 256 * (i % 2):256 * (i % 2) + 256], silu_col[:, k, :], wm[:, i, k, :],
                                     start=k == 0, stop=k == KT - 1)
            m.then_inc(s_mod, 1)
        pe.wait_ge(s_prow, 16 * 20)
        nc.tensor.transpose(psum[4][:, 0:24], prow[0:24, :], ident[0:24, 0:24]).then_inc(s_ptr, 1)
        nc.tensor.transpose(psum[5][:, 0:4 * NPAR], prow2[0:4 * NPAR, :], ident[0:4 * NPAR, 0:4 * NPAR]).then_inc(s_ptr, 1)
        for j in range(16):
            pe.wait_ge(s_mrow, j // 4 + 1)
            m = nc.tensor.transpose(psum[6][:, 2 * j:2 * j + 2], modrow[0:2, P * j:P * j + P], ident[0:2, 0:2])
        m.then_inc(s_mod, 1)
        for t in range(NTC + NT):
            pe.wait_ge(s_xs, t + 1)
            for h in range(2):
                if t >= 3:
                    pe.wait_ge([s_hT, s_hU][h], t - 2)
                elif t == 2:
                    pe.wait_ge(s_pcol, 2)
                for k in range(4 * h, 4 * h + 4):
                    m = nc.tensor.transpose(psum[2 * (t % 3) + h][:, P * (k % 4):P * (k % 4) + P],
                                            xs[:, t, P * k:P * k + P], ident)
                m.then_inc(s_tr, 1)

        def project(j, bx, bc, loads):
            pe.wait_ge(s_w[j], loads)
            for k in range(KT):
                m = nc.tensor.matmul(psum[bx][:, 0:T], wring[:, j, k, :], hT[:, k, TC:TT], start=k == 0, stop=k == KT - 1)
                if bc is not None:
                    m = nc.tensor.matmul(psum[bc][:, 0:TC], wring[:, j, k, :], hT[:, k, 0:TC], start=k == 0, stop=k == KT - 1)
            m.then_inc(s_pj, 1)

        pe.wait_ge(s_hT, 6)
        pe.wait_ge(s_hU, 6)
        project(0, 0, 1, 16)
        project(1, 2, 3, 16)
        project(2, 4, None, 16)

        def low_rank(d, which, bx=5, bc=6):
            src = [lo_w, lo_a][which]
            nc.tensor.matmul(psum[bx][:, 0:T], lora[:, d, which, :], src[:, TC:TT], start=True, stop=True)
            nc.tensor.matmul(psum[bc][:, 0:TC], lora[:, d, which, :], src[:, 0:TC], start=True, stop=True).then_inc(s_ax, 1)

        def pair(p, first):
            pe.wait_ge(s_pe, 3 * p + 3)
            if not first:
                pe.wait_ge(s_ae, 6 * p - 2)
            project(0, 0, 1, 16 * p + 32)
            pe.wait_ge(s_lora, 80 * p + 80)
            if not first:
                pe.wait_ge(s_ae, 6 * p)
            low_rank(0, 0)
            if not first:
                pe.wait_ge(s_ae, 6 * p)
            project(1, 2, None, 16 * p + 32)
            pe.wait_ge(s_ae, 6 * p + 1)
            low_rank(0, 1)
            project(2, 3, 4, 16 * p + 32)
            pe.wait_ge(s_ae, 6 * p + 2)
            pe.wait_ge(s_kk, p + 1)
            nc.tensor.matmul(psum[5][:, 0:T], head_ones, sqk[:, TC:TT], start=True, stop=True)
            nc.tensor.matmul(psum[6][:, 0:TC], head_ones, sqk[:, 0:TC], start=True, stop=True).then_inc(s_ax, 1)
            pe.wait_ge(s_pe, 3 * p + 4)
            low_rank(1, 0, 0, 1)
            pe.wait_ge(s_pe, 3 * p + 5)
            nc.tensor.matmul(psum[2][:, 0:T], gw, lo_g, start=True, stop=True).then_inc(s_ax, 1)
            pe.wait_ge(s_ae, 6 * p + 3)
            low_rank(1, 1)
            pe.wait_ge(s_bn, p + 1)
            if not first:
                pe.wait_ge(s_bd, p)
            nc.tensor.matmul(psum[7][:, 0:T], head_ones, rk, start=True, stop=True).then_inc(s_ax, 1)

        pair(0, True)
        with pe.Fori(1, PAIRS) as p:
            pair(p, False)
        pe.wait_ge(s_pe, 3 * PAIRS + 3)
        pe.wait_ge(s_ae, 6 * PAIRS - 1)
        credit(pe, s_done3, 1)
        with pe.Fori(0, PAIRS) as q:
            pe.wait_ge(s_done3, q + 1)
            project(0, 0, None, q * 16 + 16 * (PAIRS + 2))
            project(1, 2, None, q * 16 + 16 * (PAIRS + 2))
            project(2, 3, None, q * 16 + 16 * (PAIRS + 2))
        for stage in LATER["tensor"]:
            stage(pe)


_INS = ['x', 'c', 'ctx', 'c_ctx', 'w_mod', 'b_mod', 'norm_gains', 'w_in', 'w_out', 'conv_w', 'tshift_mu',
        'decay_w0', 'decay_w2', 'iclr_a0', 'iclr_a2', 'gate_w2', 'k_k', 'k_a', 'r_k', 'lnx_g', 'lnx_b',
        'peer_wq', 'peer_subkeys', 'peer_u', 'peer_v']
_OUTS = [((1, 512, 1024), 'float32')]


def kernel(**inputs):
    import numpy as _np
    import concourse.bacc as _bacc
    from concourse import mybir as _mybir
    from concourse.bass_utils import run_bass_kernel_spmd as _run

    nc = _bacc.Bacc("TRN2", target_bir_lowering=False, num_devices=1)
    arrays, args = {}, []
    for name in _INS:
        a = _np.ascontiguousarray(inputs[name])
        if a.dtype.kind in "iu":
            a = a.astype(_np.int64)
        arrays[f"in_{name}_dram"] = a
        args.append(nc.dram_tensor(f"in_{name}_dram", a.shape, _mybir.dt.from_np(a.dtype), kind="ExternalInput").ap())
    for i, (shape, dtype) in enumerate(_OUTS):
        dt = _mybir.dt.from_np(_np.dtype(dtype))
        args.append(nc.dram_tensor(f"out_{i}_dram", shape, dt, kind="ExternalOutput").ap())
    layer(nc, *args)
    r = _run(nc, [arrays], core_ids=[0])
    got = tuple(r.results[0][f"out_{i}_dram"] for i in range(len(_OUTS)))
    return got[0]
```

```python
import concourse.bass as bass
from concourse import mybir
from contextlib import ExitStack

F32 = mybir.dt.float32
U32 = mybir.dt.uint32
ALU = mybir.AluOpType
ACT = mybir.ActivationFunctionType
AX = mybir.AxisListType

P = 128
D = 1024
KT = D // P
T = 512
TC = 256
TT = T + TC
NT = T // P
NTC = TC // P
GRID = 64
DH = 64
PAIRS = 4
C = 64
NCH = TT // C
NXC = T // C
NB = 4
NORM_EPS = 1e-6
LNX_EPS = 64e-5
DECAY = 0.6065306597126334
HEADS = 8
KEYS = 128
TOPK = 16
ROWS = [(0, 1, 16), (1, 1, 8), (2, 1, 5), (3, 1, 4), (4, 1, 3), (5, 3, 2), (8, 8, 1)]
PAIR_STEPS = 40
NCAND = sum(m * w for _, m, w in ROWS)

(MP_R, MP_K, MP_V, MN_R, MN_K, MN_V, W0_F, W0_B, A0_F, A0_B, K_K, K_A, R_K, LNX_G, LNX_B,
 CV0, CV1, CV2) = range(18)
NPAR = 18
(C0_R, C0_K, C0_V, OMKA) = range(18, 22)
NPP = 22

LINKS = 15
RING = 8


def layer(nc, x, c, ctx_in, c_ctx, w_mod, b_mod, norm_gains, w_in, w_out, conv_w, tshift_mu,
          decay_w0, decay_w2, iclr_a0, iclr_a2, gate_w2, k_k, k_a, r_k, lnx_g, lnx_b,
          peer_wq, peer_subkeys, peer_u, peer_v, out):
    with ExitStack() as stack:
        _layer(nc, stack, x, c, ctx_in, c_ctx, w_mod, b_mod, norm_gains, w_in, w_out, conv_w, tshift_mu,
               decay_w0, decay_w2, iclr_a0, iclr_a2, gate_w2, k_k, k_a, r_k, lnx_g, lnx_b,
               peer_wq, peer_subkeys, peer_u, peer_v, out)


def _layer(nc, stack, x, c, ctx_in, c_ctx, w_mod, b_mod, norm_gains, w_in, w_out, conv_w, tshift_mu,
           decay_w0, decay_w2, iclr_a0, iclr_a2, gate_w2, k_k, k_a, r_k, lnx_g, lnx_b,
           peer_wq, peer_subkeys, peer_u, peer_v, out):
    ARENA = 53120
    MOD = ARENA - 2048 - 7 * D
    arena = stack.enter_context(nc.sbuf_tensor("arena", [P, ARENA], F32))
    psum = [stack.enter_context(nc.psum_tensor(f"bank{i}", [P, 512], F32)) for i in range(8)]

    class Cut:

        def __init__(self, at, end=ARENA):
            self.at, self.end = at, end

        def __call__(self, *shape):
            n = 1
            for s in shape:
                n *= s
            a = arena[:, self.at:self.at + n]
            self.at += n
            assert self.at <= self.end, (self.at, self.end)
            if len(shape) == 2:
                a = a.rearrange("p (a b) -> p a b", b=shape[1])
            elif len(shape) == 3:
                a = a.rearrange("p (a b c) -> p a b c", b=shape[1], c=shape[2])
            elif len(shape) == 4:
                a = a.rearrange("p (a b c d) -> p a b c d", b=shape[1], c=shape[2], d=shape[3])
            return a

    def sem(name):
        return stack.enter_context(nc.semaphore(name))

    keep = Cut(0)
    ident = keep(P)
    xn = keep(NT, D)
    head_ones = keep(P)
    mix_diag = keep(P)
    par = keep(PAIRS + 1, NPAR)
    bias4 = keep(4)
    shsc = keep(16, 2)
    eps = keep(4)
    silu_col = keep(KT, 2)
    yconv = keep(PAIRS, T)
    bonus = keep(PAIRS, T)
    gate = keep(PAIRS, T)
    pc_all = keep(2 * PAIRS, NCH)
    KEEP_END = keep.at

    cut = Cut(KEEP_END)
    hT = cut(KT, TT)
    wring = cut(3, KT, P)
    s3 = cut.at
    ctxn = cut(NTC, D)
    wm = cut(8, KT, 2 * P)
    prow = cut(P)
    prow2 = cut(P)
    sq = cut(D)
    xs = cut(NTC + NT, D)
    modrow = cut(2 * D)
    pcolA = cut(P)
    cc = cut(2, KT)
    ccs = cut(2, KT)
    ssq = cut(8)
    rstd = cut(8)
    tab = cut(KT, 2)
    assert cut.at <= ARENA - 2048

    cut = Cut(s3)
    lo_w = cut(TT)
    lo_a = cut(TT)
    lo_g = cut(T)
    lora = cut(2, 2, P)
    gw = cut(P)
    kraw = cut(TT + 4)
    vraw = cut(TT + 4)
    rraw = cut(T + 2)
    k_sh = cut(TT)
    v_sh = cut(TT)
    r_sh = cut(T)
    kk = cut(TT)
    sqk = cut(TT)
    decay_sig = cut(TT)
    aa = cut(2, TT)
    cs = cut(TT)
    cum_before = cut(TT)
    cum_with = cut(TT)
    e1 = cut(TT)
    e2 = cut(TT)
    e3 = cut(TT)
    t1 = cut(TT)
    t2 = cut(TT)
    rk = cut(T)
    pp = cut(NPP)
    scan_keep = cut(TT)
    conv_in = [t1[:, 0:T], e1[:, 0:T]]
    CONV_BANKS = [(0, 2, 3), (5, 6, 7)]
    BKb = cut(2, NCH, P)
    KRb = cut(2, NCH, P)
    VSb = cut(NCH, P)
    CO, XO = 1, TC + 3

    cut = Cut(KEEP_END)
    BKs = cut(2, NB, P)
    VSs = cut(2, NB, P)
    BKT = cut(2, NB, P)
    NBD = cut(2, NB, P)
    MBD = cut(2, NB, P)
    ZZ = cut(2, NB, P)
    XX = cut(2, NB, P)
    AA = cut(2, NB, P)
    ysum = cut(PAIRS, NXC, DH)
    LE = cut(3, 2, NB * P)
    LO = cut(3, 2, NB * P)
    QQ = cut(3, 2, NB * P)
    KVP = cut(3, 2, NB * P)
    SV = cut(3, 2, NB * P)
    RB = cut(2, P)
    TMPS = cut(2, P)
    Yb = cut(NXC, 2, 2, DH)
    KRx = cut(2, NB, 2, P)
    assert cut.at <= MOD
    cut = Cut(ARENA - 2048)
    msk_e = cut(2, P)
    msk_o = cut(2, P)
    lvl = cut(2, 6, P)
    cut = Cut(MOD, ARENA - 2048)
    wmr = cut(KT, 256)
    silb = cut(KT, P)
    rows = cut(4, D)
    g1row, sh2row, a2row, g2row = (rows[:, i, :] for i in range(4))

    cut = Cut(KEEP_END + 8192)
    H2N = cut(NT, D)
    SC = arena[:, KEEP_END:KEEP_END + (NT + 1) * 2048].rearrange("p (t h k) -> p t h k", h=2 * HEADS, k=KEYS)
    brow = arena[:, KEEP_END:KEEP_END + 7 * D]
    ysq = H2N.rearrange("p a b -> p (a b)")[:, 2048:4096].rearrange("p (a x v) -> p a x v", x=NXC, v=DH)
    assert cut.at == KEEP_END + 8192 + 4096
    h2T = cut(KT, T)
    YT = h2T.rearrange("p a b -> p (a b)").rearrange("p (i c) -> p i c", c=P)
    u_ring = cut(RING, D)
    v_ring = cut(RING, D)
    wo = u_ring
    wqA = v_ring.rearrange("p s (k n) -> p s k n", k=KT)
    square_dump5 = cut(D)
    stats5 = cut(96)
    yrw = arena[:, ARENA - 2048:].rearrange("p (a b) -> p a b", b=T)
    normed5 = arena[:, KEEP_END:KEEP_END + D]
    h2cur = arena[:, ARENA - 2048:ARENA - 1024]
    out_tile = arena[:, ARENA - 1024:]
    cut = Cut(cut.at, MOD + 6 * D)
    diag = cut(4, P)
    SCs = cut(2, 2, KEYS)
    scores_left = cut(2, KEYS)
    one_hot = cut(TOPK, NCAND)
    v16 = cut(2, TOPK)
    i16 = cut(2, TOPK)
    i16f = cut(2, TOPK)
    cand = cut(64)
    cand_number = cut(64)
    cand_left = cut(64)
    iot = cut(64)
    top = cut(TOPK)
    pos = cut(TOPK)
    posf = cut(TOPK)
    expert_f32 = cut(TOPK)
    idx = cut(4, TOPK)
    neg_largest = cut(2)
    prob = cut(TOPK)
    exp_sum = cut(2)
    softmax_w = cut(2, TOPK)
    acts = cut(2, TOPK)
    gelu_dot = cut(2, TOPK)
    expert_w = cut(2, TOPK)
    final_stats = cut(8)
    square_dump = gate.rearrange("p a b -> p (a b)")[:, 0:512]
    wq2 = yconv.rearrange("p a b -> p (a b)").rearrange("p (s k n) -> p s k n", s=2, k=KT)
    skn = gate.rearrange("p a b -> p (a b)").rearrange("p (s n) -> p s n", n=P)
    skT = bonus.rearrange("p a b -> p (a b)").rearrange("p (s n) -> p s n", n=P)
    qT = arena[:, KEEP_END + 2048:KEEP_END + 3072].rearrange("p (s n) -> p s n", n=T)
    qB = gate.rearrange("p a b -> p (a b)")[:, 1024:1024 + 6 * P].rearrange("p (s n) -> p s n", n=3 * P)

    def v3(a):
        return a.rearrange("p (i c) -> p i c", c=P)

    bk_dram = nc.dram_tensor("bk_scratch", [2 * PAIRS, P, NCH * P], F32, kind="Internal").ap()
    kr_dram = nc.dram_tensor("kr_scratch", [2 * PAIRS, P, NCH * P], F32, kind="Internal").ap()
    vs_dram = nc.dram_tensor("vs_scratch", [PAIRS, P, NCH * P], F32, kind="Internal").ap()

    cond_loaded = sem("cond_loaded")
    param_rows_loaded = sem("param_rows_loaded")
    latents_loaded = [sem(f"latents_loaded{i}") for i in range(NT)]
    context_loaded = sem("context_loaded")
    wmod_loaded = [sem(f"wmod_loaded{i}") for i in range(8)]
    constants_made = sem("constants_made")
    silu_made = sem("silu_made")
    params_transposed = sem("params_transposed")
    param_columns_made = sem("param_columns_made")
    mod_products = sem("mod_products")
    mod_rows_moved = sem("mod_rows_moved")
    mod_columns_made = sem("mod_columns_made")
    square_sums = sem("square_sums")
    rstd_made = sem("rstd_made")
    vector_steps = sem("vector_steps")
    normed_rows = sem("normed_rows")
    rows_transposed = sem("rows_transposed")
    hT_lower = sem("hT_lower_half")
    hT_upper = sem("hT_upper_half")
    win_loaded = [sem(f"win_loaded{i}") for i in range(3)]
    projections_made = sem("projections_made")
    projections_evacuated = sem("projections_evacuated")
    lora_loaded = sem("lora_loaded")
    aux_products = sem("aux_products")
    aux_evacuated = sem("aux_evacuated")
    shifted = sem("shifted")
    kk_ready = sem("kk_ready")
    decay_sums = sem("decay_sums")
    decay_factors = sem("decay_factors")
    pair_dir_ready = sem("pair_dir_ready")
    vs_ready = sem("vs_ready")
    spilled_done = sem("spilled")
    pads_zeroed = sem("pads_zeroed")
    pair_params, pair_biases = sem("pair_params"), sem("pair_biases")
    bonus_product_in = sem("bonus_product_in")
    conv_steps = sem("conv_steps")
    bonus_made = sem("bonus_made")
    stage3_vector_done = sem("stage3_vector_done")
    masks_made = sem("masks_made")
    bk_loaded = [sem(f"bk_loaded{d}") for d in range(2)]
    vs_loaded = [sem(f"vs_loaded{d}") for d in range(2)]
    kr_loaded = [sem(f"kr_loaded{i}") for i in range(6)]
    n_zeroed = sem("n_zeroed")
    chunk_products = [sem(f"chunk_products{d}") for d in range(2)]
    chunk_scalar_moves = [sem(f"chunk_scalar_moves{d}") for d in range(2)]
    chunk_vector_moves = [sem(f"chunk_vector_moves{d}") for d in range(2)]
    inverse_products = [sem(f"inverse_products{d}") for d in range(2)]
    inverse_started = [sem(f"inverse_started{d}") for d in range(2)]
    state_read = [sem(f"state_read{d}") for d in range(2)]
    state_read_split = [sem(f"state_read_split{d}") for d in range(2)]
    y_from_state = [sem(f"y_from_state{d}") for d in range(2)]
    chunk_applied = [sem(f"chunk_applied{d}") for d in range(2)]
    state_decayed = [sem(f"state_decayed{d}") for d in range(2)]
    state_written = [sem(f"state_written{d}") for d in range(2)]
    y_from_chunk = [sem(f"y_from_chunk{d}") for d in range(2)]
    y_summed = sem("y_summed")
    rows_loaded = sem("rows_loaded")
    wout_loaded = [sem(f"wout_half_loaded{i}") for i in range(2)]
    wmod_row_weights = sem("wmod_row_weights")
    silu_spread = sem("silu_spread")
    modulation_rows = sem("modulation_rows")
    modulation_rows_moved = sem("modulation_rows_moved")
    rows_finished = sem("rows_finished")
    y_transpose_zeroed = sem("y_transpose_zeroed")
    head_sums = sem("head_sums")
    head_norm_vector = sem("head_norm_vector")
    head_norm_scalar = sem("head_norm_scalar")
    y_transposed = sem("y_transposed")
    y_affine = sem("y_affine")
    y_gated = sem("y_gated")
    mixer_output = sem("mixer_output")
    norm1_scalar = sem("norm1_scalar")
    norm1_vector = sem("norm1_vector")
    h2_rows = sem("h2_rows")
    h2_transposed = sem("h2_transposed")
    h2_columns = sem("h2_columns")
    wq_loaded = [sem(f"wq_loaded{i}") for i in range(2)]
    subkeys_loaded = sem("subkeys_loaded")
    wq_half_loaded = [sem(f"wq_half_loaded{i}") for i in range(2)]
    subkeys_transposed = sem("subkeys_transposed")
    subkeys_moved = sem("subkeys_moved")
    queries_done = sem("queries")
    queries_moved = sem("queries_moved")
    scores_done = sem("scores")
    scores_moved = sem("scores_moved")
    late_queries = sem("late_queries")
    late_queries_moved = sem("late_queries_moved")
    late_scores_done = sem("late_scores")
    late_scores_moved = sem("late_scores_moved")
    iota_made = sem("iota_made")
    scores_staged = sem("scores_staged")
    topk_links = sem("topk_links")
    experts_chosen = sem("experts_chosen")
    probabilities_raised = sem("probabilities_raised")
    probabilities = sem("probabilities")
    u_rows = [sem(f"u_rows{i}") for i in range(RING)]
    v_rows = [sem(f"v_rows{i}") for i in range(RING)]
    dots = sem("dots")
    gelus = sem("gelus")
    expert_weights = sem("expert_weights")
    weight_diagonals = sem("weight_diagonals")
    experts_added = sem("experts_added")
    h2_current = sem("h2_current")
    final_scalar = sem("final_scalar")
    final_vector = sem("final_vector")
    output_stored = sem("output_stored")
    passed = sem("waits_passed")

    block = stack.enter_context(nc.Block())

    x_v = x[0].rearrange("(t p) d -> t p d", p=P)
    ctx_v = ctx_in[0].rearrange("(t p) d -> t p d", p=P)
    wmod_v = w_mod[0].rearrange("(p k) n -> p k n", k=KT)
    win_v = w_in[0].rearrange("(k p) n -> p k n", p=P)

    def credit(engine, semaphore, n):
        engine.sem_inc(semaphore, n)

    def apart(engine):
        engine.sem_inc(passed, 1)

    W1, W2 = [psum[0], psum[2]], [psum[1], psum[3]]
    C1, C2 = [psum[4], psum[6]], [psum[5], psum[7]]
    ORDER = [[0, 1, 2], [0, 2, 1]]
    ITEMS = [[0, 1, 2, 3], [3, 2, 1, 0]]
    LV = 5
    MK = {"bkT": 1, "vT": 2, "kv": 3, "ge": 4, "go": 5, "nT": 6}
    for l in range(LV):
        MK["a", l] = 7 + 3 * l
        if l < LV - 1:
            MK["z", l] = 8 + 3 * l
            MK["x", l] = 9 + 3 * l
    MK["x", LV - 1] = 8 + 3 * (LV - 1)
    MK["q"] = 9 + 3 * (LV - 1)
    NMK = MK["q"]
    AC = {"bkT": 1, "vT": 2, "m": 3, "q": 4}
    NAC = 4
    VC = {"kv": 1, "ge": 2, "go": 3}
    for l in range(LV):
        VC["a", l] = 4 + 3 * l
        if l < LV - 1:
            VC["z", l] = 5 + 3 * l
            VC["x", l] = 6 + 3 * l
    VC["x", LV - 1] = 5 + 3 * (LV - 1)
    NVC = VC["x", LV - 1]
    NPL = 2

    def bcast(m, rows, cols):
        w = cols.stop - cols.start
        return m[rows, cols].unsqueeze(1).broadcast_to([rows.stop - rows.start, NB, w])

    MOD_BLOCKS = [[0], [1], [2, 3]]

    LOW, HIGH, ALL = slice(0, DH), slice(DH, P), slice(0, P)

    def steps4(engine, do, tail):
        do(0, 0, None, True)
        do(0, 1, (0, 0), True)
        do(0, 2, (0, 1), True)
        with engine.Fori(1, PAIRS) as p:
            do(p, 0, (p - 1, 2), False)
            do(p, 1, (p, 0), False)
            do(p, 2, (p, 1), False)
        tail()

    def sync4(sp):
        sp.wait_ge(stage3_vector_done, PAIRS + 2)

        def do(p, b, chain, first):
            n = 3 * p + b
            for d in range(2):
                src = slice(ORDER[d][b] * NB * P, (ORDER[d][b] + 1) * NB * P)
                if not (first and b == 0):
                    sp.wait_ge(chunk_products[d], NMK * (n - 1) + MK["go"])
                if not first:
                    apart(sp)
                    sp.wait_ge(state_read[d], 12 * (p - 1) + 4 * b + 4)
                    apart(sp)
                sp.dma_start(BKs[:, d].rearrange("p a b -> p (a b)"), bk_dram[2 * p + d][:, src]).then_inc(bk_loaded[d], 16)
                sp.dma_start(VSs[:, d].rearrange("p a b -> p (a b)"), vs_dram[p][:, src]).then_inc(vs_loaded[d], 16)
                sp.dma_start(KRx[LOW, d, :, 0, :], kr_dram[2 * p + d][LOW, src].rearrange("p (i c) -> p i c", c=P)).then_inc(kr_loaded[2 * b + d], 16)
                sp.dma_start(KRx[HIGH, d, :, 1, :], kr_dram[2 * p + d][HIGH, src].rearrange("p (i c) -> p i c", c=P)).then_inc(kr_loaded[2 * b + d], 16)
                sp.dma_start(LE[LOW, b, d, :], kr_dram[2 * p + d][LOW, src]).then_inc(kr_loaded[2 * b + d], 16)
                sp.dma_start(LO[HIGH, b, d, :], kr_dram[2 * p + d][HIGH, src]).then_inc(kr_loaded[2 * b + d], 16)
            for j in MOD_BLOCKS[b]:
                if not (first and j == 0):
                    sp.wait_ge(modulation_rows, 4 * p + j)
                    apart(sp)
                sp.dma_start(wmr, wmod_v[:, :, bass.ds(p * D + (2 * D + 256 * j), 256)]).then_inc(wmod_row_weights, 16)
        steps4(sp, do, lambda: None)

    def pool_masks(pool):
        n = [0]

        def put(i):
            n[0] += 1
            i.then_inc(masks_made, 1)
            pool.wait_ge(masks_made, n[0])

        for d in range(2):
            put(nc.gpsimd.memset(msk_e[:, d], 1.0))
            put(nc.gpsimd.memset(msk_o[:, d], 1.0))
            for l in range(6):
                s = 1 << l
                v = lvl[:, d, l].rearrange("p (n h s) -> p n h s", h=2, s=s)
                put(nc.gpsimd.memset(v[:, :, d], 0.0))
                put(nc.gpsimd.memset(v[:, :, 1 - d], 1.0))
        for d in range(2):
            sg_ = 1 - 2 * d
            for tile, ops in ((msk_e, (ALU.is_gt, ALU.is_ge)), (msk_o, (ALU.is_ge, ALU.is_gt))):
                for h in range(2):
                    for rows in (LOW, HIGH):
                        a = tile[rows, d, DH * h:DH * h + DH]
                        put(nc.gpsimd.affine_select(out=a, in_=a, compare_op=ops[h], fill=0.0, base=0,
                                                    pattern=[[sg_, DH]], channel_multiplier=-sg_))
            for l in range(6):
                s = 1 << l
                v = lvl[:, d, l].rearrange("p (n w) -> p n w", w=2 * s)
                put(nc.gpsimd.affine_select(out=v, in_=v, compare_op=ALU.is_ge, fill=0.0, base=-d * s,
                                            pattern=[[-2 * s, P // (2 * s)], [0, 2 * s]], channel_multiplier=1))
        for d in range(2):
            for l in range(6):
                s = 1 << l
                v = lvl[:, d, l].rearrange("p (n w) -> p n w", w=2 * s)
                put(nc.gpsimd.affine_select(out=v, in_=v, compare_op=ALU.is_ge, fill=0.0, base=s - 1 + d * s,
                                            pattern=[[2 * s, P // (2 * s)], [0, 2 * s]], channel_multiplier=-1))
        return n[0]

    def pool4(pool):
        pool.wait_ge(stage3_vector_done, PAIRS + 2)
        pool.wait_ge(spilled_done, 16 * 5 * PAIRS)
        for d in range(2):
            nc.gpsimd.memset(NBD[:, d], 0.0).then_inc(n_zeroed, 1)
        for d in range(2):
            for n, quarter in ((2 * d + 2, KRx[HIGH, d, :, 0, :]), (2 * d + 3, KRx[LOW, d, :, 1, :])):
                pool.wait_ge(n_zeroed, n)
                nc.gpsimd.memset(quarter, 0.0).then_inc(n_zeroed, 1)
        pool.wait_ge(n_zeroed, 6)
        nc.gpsimd.tensor_copy(silb, silu_col[:, :, 0:1].broadcast_to([P, KT, P])).then_inc(silu_spread, 1)

    def scalar4(act):
        def copies(cp, cb, i, which):
            for d in range(2):
                ci = ITEMS[d][i]
                xc = NB * ORDER[d][cb] + ci - TC // C
                src = [C1, C2][which][d]
                if which == 0:
                    act.wait_ge(state_read_split[d], 12 * cp + 4 * cb + i + 1)
                elif (cb, i) == (2, 3):
                    act.wait_ge(chunk_applied[d], 12 * cp + 12)
                else:
                    act.wait_ge(state_written[d], 11 * cp + 4 * cb + i + 1)
                nc.scalar.activation(Yb[HIGH, xc, d, which, :], src[HIGH, 0:DH], ACT.Identity)
                nc.scalar.activation(Yb[LOW, xc, d, which, :], src[LOW, DH:P], ACT.Identity).then_inc([y_from_state, y_from_chunk][which][d], 1)

        def chain_part(chain, i, first):
            cp, cb = chain
            if cb == 0:
                return
            if i == 0 and cb == 1 and not first:
                act.wait_ge(y_summed, cp)
            copies(cp, cb, i, 0)
            copies(cp, cb, i, 1)

        def mod_row(p, j):
            act.wait_ge(modulation_rows, 4 * p + j + 1)
            nc.scalar.activation(rows[:, p, 256 * j:256 * j + 256], C1[j % 2][:, P:P + 256], ACT.Identity).then_inc(modulation_rows_moved, 1)

        def do(p, b, chain, first):
            n = 3 * p + b
            for d in range(2):
                act.wait_ge(chunk_products[d], NMK * n + MK["bkT"])
                nc.scalar.activation(BKT[:, d], v3(W1[d][:, :]), ACT.Identity).then_inc(chunk_scalar_moves[d], 1)
            for d in range(2):
                act.wait_ge(chunk_products[d], NMK * n + MK["vT"])
                if not first:
                    act.wait_ge(state_read[d], 12 * (p - 1) + 4 * b + 4)
                    act.wait_ge(state_written[d], 11 * (p - 1) + min(4 * b + 4, 11))
                nc.scalar.activation(v3(SV[:, b, d]), v3(W2[d][:, :]), ACT.Identity).then_inc(chunk_scalar_moves[d], 1)
            for d in range(2):
                act.wait_ge(chunk_products[d], NMK * n + MK["nT"])
                nc.scalar.activation(MBD[:, d], v3(W2[d][:, :]), ACT.Identity).then_inc(chunk_scalar_moves[d], 1)
            mod_row(p, b)
            for i in range(NB):
                if chain:
                    chain_part(chain, i, first)
                if b == 2 and i == 0:
                    mod_row(p, 3)
            for d in range(2):
                act.wait_ge(chunk_products[d], NMK * n + MK["q"])
                if not first:
                    act.wait_ge(chunk_applied[d], 12 * (p - 1) + 4 * b + 4)
                nc.scalar.activation(v3(QQ[:, b, d]), v3(W2[d][:, :]), ACT.Identity).then_inc(chunk_scalar_moves[d], 1)

        def tail():
            for i in range(NB):
                chain_part((PAIRS - 1, 2), i, False)
        steps4(act, do, tail)

    def vector4(dve):
        def split(cp, cb, i):
            for d in range(2):
                dve.wait_ge(state_read[d], 12 * cp + 4 * cb + i + 1)
                nc.vector.tensor_tensor(RB[:, d], C1[d][:, 0:P], mix_diag, ALU.mult).then_inc(state_read_split[d], 1)
            if (cb, i) == (2, 3):
                return
            for d in range(2):
                ci = ITEMS[d][i]
                c = NB * ORDER[d][cb] + ci
                if not (cb == 0 and i == 0):
                    dve.wait_ge(state_written[d], 11 * cp + 4 * cb + i)
                nc.vector.scalar_tensor_tensor(TMPS[:, d], v3(SV[:, cb, d])[:, ci], pc_all[:, 2 * cp + d, c:c + 1],
                                               v3(KVP[:, cb, d])[:, ci], ALU.mult, ALU.add).then_inc(state_decayed[d], 1)

        def advance(cp, cb, i):
            if (cb, i) == (2, 3):
                return
            nb, ni = (cb, i + 1) if i < 3 else (cb + 1, 0)
            for d in range(2):
                ci = ITEMS[d][i]
                c = NB * ORDER[d][cb] + ci
                dst = v3(SV[:, nb, d])[:, ITEMS[d][ni]]
                dve.wait_ge(chunk_applied[d], 12 * cp + 4 * cb + i + 1)
                dve.wait_ge(state_decayed[d], 11 * cp + 4 * cb + i + 1)
                if ni == 0:
                    dve.wait_ge(chunk_vector_moves[d], NVC * (3 * cp + nb) + VC["kv"])
                for rows, cols in ((LOW, slice(0, DH)), (HIGH, slice(DH, P))):
                    last = nc.vector.scalar_tensor_tensor(dst[rows, cols], C2[d][rows, cols],
                                                          pc_all[rows, 2 * cp + d, c:c + 1], TMPS[rows, d, cols],
                                                          ALU.mult, ALU.add)
                last.then_inc(state_written[d], 1)

        def total(cp):
            for d in range(2):
                dve.wait_ge(y_from_state[d], 8 * cp + 8)
                dve.wait_ge(y_from_chunk[d], 8 * cp + 8)
            nc.vector.tensor_reduce(ysum[:, cp], Yb.rearrange("p x d s v -> p x v d s"), AX.XY, ALU.add).then_inc(y_summed, 1)

        def do(p, b, chain, first):
            n = 3 * p + b
            if first and b == 0:
                dve.wait_ge(n_zeroed, 2)
                dve.wait_ge(masks_made, n_masks)
            for d in range(2):
                dve.wait_ge(chunk_products[d], NMK * n + MK["kv"])
                pc = pc_all[:, 2 * p + d, NB * ORDER[d][b]:NB * ORDER[d][b] + NB]
                nc.vector.tensor_tensor(v3(KVP[:, b, d]), v3(W1[d][:, :]), pc.unsqueeze(2).broadcast_to([P, NB, P]),
                                        ALU.mult).then_inc(chunk_vector_moves[d], 1)
            for d in range(2):
                g = v3(W2[d][:, :])
                dve.wait_ge(chunk_products[d], NMK * n + MK["ge"])
                nc.vector.tensor_tensor(NBD[LOW, d, :, 0:DH], g[LOW, :, 0:DH], bcast(msk_e[:, d], LOW, slice(0, DH)), ALU.mult)
                nc.vector.tensor_tensor(BKT[LOW, d, :, DH:P], g[LOW, :, DH:P], bcast(msk_e[:, d], LOW, slice(DH, P)), ALU.mult)
                nc.vector.tensor_tensor(v3(LE[:, b, d])[HIGH], g[HIGH], bcast(msk_e[:, d], HIGH, ALL), ALU.mult).then_inc(chunk_vector_moves[d], 1)
            for d in range(2):
                g = v3(W1[d][:, :])
                dve.wait_ge(chunk_products[d], NMK * n + MK["go"])
                nc.vector.tensor_tensor(v3(LO[:, b, d])[LOW], g[LOW], bcast(msk_o[:, d], LOW, ALL), ALU.mult)
                nc.vector.tensor_tensor(BKT[HIGH, d, :, 0:DH], g[HIGH, :, 0:DH], bcast(msk_o[:, d], HIGH, slice(0, DH)), ALU.mult)
                nc.vector.tensor_tensor(NBD[HIGH, d, :, DH:P], g[HIGH, :, DH:P], bcast(msk_o[:, d], HIGH, slice(DH, P)),
                                        ALU.mult).then_inc(chunk_vector_moves[d], 1)
            for d in range(2):
                dve.wait_ge(chunk_vector_moves[d], NVC * n + VC["go"])
                nc.vector.tensor_tensor(ZZ[:, d], NBD[:, d], bcast(lvl[:, d, 0], ALL, ALL), ALU.mult).then_inc(inverse_products[d], 1)
            for d in range(2):
                dve.wait_ge(inverse_products[d], 2 * n + 1)
                nc.vector.tensor_tensor(ZZ[:, d], ZZ[:, d], bcast(ident, ALL, ALL), ALU.add).then_inc(inverse_started[d], 1)
            for d in range(2):
                dve.wait_ge(chunk_scalar_moves[d], NAC * n + AC["m"])
                nc.vector.tensor_tensor(XX[:, d], MBD[:, d], bcast(lvl[:, 1 - d, 0], ALL, ALL), ALU.mult).then_inc(inverse_products[d], 1)
            for d in range(2):
                dve.wait_ge(inverse_products[d], 2 * n + 2)
                nc.vector.tensor_tensor(XX[:, d], XX[:, d], bcast(ident, ALL, ALL), ALU.add).then_inc(inverse_started[d], 1)
            for l in range(LV):
                for d in range(2):
                    dve.wait_ge(chunk_products[d], NMK * n + MK["a", l])
                    nc.vector.tensor_tensor(AA[:, d], v3(W1[d][:, :]), bcast(lvl[:, d, l + 1], ALL, ALL), ALU.mult).then_inc(chunk_vector_moves[d], 1)
                if chain and l < NB:
                    split(*chain, l)
                for d in range(2):
                    if l < LV - 1:
                        dve.wait_ge(chunk_products[d], NMK * n + MK["z", l])
                        nc.vector.tensor_tensor(ZZ[:, d], v3(W2[d][:, :]), ZZ[:, d], ALU.add).then_inc(chunk_vector_moves[d], 1)
                    dve.wait_ge(chunk_products[d], NMK * n + MK["x", l])
                    nc.vector.tensor_tensor(XX[:, d], v3(W1[d][:, :]), XX[:, d], ALU.add).then_inc(chunk_vector_moves[d], 1)
                if chain and l < NB:
                    advance(*chain, l)
            if chain and chain[1] == 2:
                total(chain[0])

        def tail():
            for i in range(NB):
                split(PAIRS - 1, 2, i)
                advance(PAIRS - 1, 2, i)
            total(PAIRS - 1)
        steps4(dve, do, tail)

    def tensor4(pe):
        def read_state(cp, cb, i, first):
            for d in range(2):
                ci = ITEMS[d][i]
                if not (cb == 0 and i == 0):
                    pe.wait_ge(state_written[d], 11 * cp + 4 * cb + i)
                yc = 8 * cp + max(4 * (cb - 1) + i, 0)
                if not (first and yc == 0):
                    pe.wait_ge(y_from_state[d], yc)
                if not (first and cb == 0 and i == 0):
                    pe.wait_ge(state_read_split[d], 12 * cp + 4 * cb + i)
                nc.tensor.matmul(C1[d][:, 0:DH], v3(LE[:, cb, d])[:, ci], v3(SV[:, cb, d])[:, ci, 0:DH], start=True, stop=True)
                nc.tensor.matmul(C1[d][:, DH:P], v3(LO[:, cb, d])[:, ci], v3(SV[:, cb, d])[:, ci, DH:P], start=True,
                                 stop=True).then_inc(state_read[d], 1)

        def apply_chunk(cp, cb, i, first):
            for d in range(2):
                ci = ITEMS[d][i]
                pe.wait_ge(state_read_split[d], 12 * cp + 4 * cb + i + 1)
                if i == 0:
                    pe.wait_ge(chunk_scalar_moves[d], NAC * (3 * cp + cb) + AC["q"])
                yc = 8 * cp + max(4 * (cb - 1) + i, 0)
                if not (first and yc == 0):
                    pe.wait_ge(y_from_chunk[d], yc)
                nc.tensor.matmul(C2[d][:, 0:P], v3(QQ[:, cb, d])[:, ci], RB[:, d], start=True, stop=True).then_inc(chunk_applied[d], 1)

        def mod_row(p, j, first):
            if first and j == 0:
                pe.wait_ge(silu_spread, 1)
            if not (first and j < 2):
                pe.wait_ge(modulation_rows_moved, 4 * p + j - 1)
            d = j % 2
            read = 4 * (3 * p + min(j, 2) - 1) + (j == 3)
            copied = [8 * p - 4, 8 * p, 8 * p, 8 * p + 1][j]
            if not first or read > 0:
                pe.wait_ge(state_read_split[d], read)
            if not first or copied > 0:
                pe.wait_ge(y_from_state[d], copied)
            pe.wait_ge(wmod_row_weights, 64 * p + 16 * j + 16)
            for k in range(KT):
                m = nc.tensor.matmul(C1[j % 2][:, P:P + 256], silb[:, k, :], wmr[:, k, :], start=k == 0, stop=k == KT - 1)
            m.then_inc(modulation_rows, 1)

        def four(f, s):
            for i in range(NB):
                m = f(i)
            m.then_inc(s, 1)

        def do(p, b, chain, first):
            n = 3 * p + b
            start = first and b == 0
            for d in range(2):
                pe.wait_ge(bk_loaded[d], 16 * n + 16)
                if not start:
                    pe.wait_ge(chunk_vector_moves[d], NVC * n)
                    pe.wait_ge(chunk_scalar_moves[d], NAC * n)
                four(lambda i: nc.tensor.transpose(W1[d][:, P * i:P * i + P], BKs[:, d, i], ident), chunk_products[d])
                pe.wait_ge(vs_loaded[d], 16 * n + 16)
                four(lambda i: nc.tensor.transpose(W2[d][:, P * i:P * i + P], VSs[:, d, i], ident), chunk_products[d])
            for d in range(2):
                pe.wait_ge(chunk_scalar_moves[d], NAC * n + AC["vT"])
                four(lambda i: nc.tensor.matmul(W1[d][:, P * i:P * i + P], BKT[:, d, i], v3(SV[:, b, d])[:, i],
                                                start=True, stop=True), chunk_products[d])
                pe.wait_ge(kr_loaded[2 * b + d], 64 * p + 64)
                if start and d == 0:
                    pe.wait_ge(n_zeroed, 6)
                four(lambda i: nc.tensor.matmul(W2[d][:, P * i:P * i + P], BKs[:, d, i], KRx[:, d, i, 0],
                                                start=True, stop=True), chunk_products[d])
            for d in range(2):
                pe.wait_ge(chunk_vector_moves[d], NVC * n + VC["kv"])
                four(lambda i: nc.tensor.matmul(W1[d][:, P * i:P * i + P], BKs[:, d, i], KRx[:, d, i, 1],
                                                start=True, stop=True), chunk_products[d])
            mod_row(p, b, first)
            for d in range(2):
                pe.wait_ge(chunk_vector_moves[d], NVC * n + VC["go"])
                four(lambda i: nc.tensor.transpose(W2[d][:, P * i:P * i + P], NBD[:, d, i], ident), chunk_products[d])
            for l in range(LV):
                if b == 2 and l == 1:
                    mod_row(p, 3, first)
                for d in range(2):
                    if l == 0:
                        pe.wait_ge(inverse_started[d], NPL * n + 1)
                        pe.wait_ge(chunk_scalar_moves[d], NAC * n + AC["m"])
                    else:
                        pe.wait_ge(chunk_vector_moves[d], NVC * n + VC["x", l - 1])
                    four(lambda i: nc.tensor.matmul(W1[d][:, P * i:P * i + P], MBD[:, d, i], ZZ[:, d, i],
                                                    start=True, stop=True), chunk_products[d])
                if chain and l < NB:
                    if l == 0:
                        pe.wait_ge(modulation_rows_moved, 4 * p + b + 1)
                    if b == 2 and l == 1:
                        pe.wait_ge(modulation_rows_moved, 4 * p + 4)
                    read_state(*chain, l, first)
                for d in range(2):
                    pe.wait_ge(chunk_vector_moves[d], NVC * n + VC["a", l])
                    if l == 0:
                        pe.wait_ge(inverse_started[d], NPL * n + 2)
                    if l < LV - 1:
                        four(lambda i: nc.tensor.matmul(W2[d][:, P * i:P * i + P], XX[:, d, i], AA[:, d, i],
                                                        start=True, stop=True), chunk_products[d])
                    four(lambda i: nc.tensor.matmul(W1[d][:, P * i:P * i + P], AA[:, d, i], XX[:, d, i],
                                                    start=True, stop=True), chunk_products[d])
                if chain and l < NB:
                    apply_chunk(*chain, l, first)
            for d in range(2):
                pe.wait_ge(chunk_vector_moves[d], NVC * n + VC["x", LV - 1])
                four(lambda i: nc.tensor.matmul(W2[d][:, P * i:P * i + P], XX[:, d, i], BKT[:, d, i],
                                                start=True, stop=True), chunk_products[d])

        def tail():
            for i in range(NB):
                read_state(PAIRS - 1, 2, i, False)
                apply_chunk(PAIRS - 1, 2, i, False)
        steps4(pe, do, tail)

    wout_v = w_out[0].rearrange("(k p) n -> p k n", p=P)
    wq_v = peer_wq[0].rearrange("(k p) n -> p k n", p=P)
    skey_v = peer_subkeys[0].rearrange("h s k d -> k (h s) d")
    HS = 2 * HEADS

    def sync5(sp):
        sp.wait_ge(y_summed, PAIRS)
        for i in range(2):
            sp.dma_start(wo[:, 4 * i:4 * i + 4], wout_v[:, 4 * i:4 * i + 4]).then_inc(wout_loaded[i], 16)
        sp.dma_start(brow[:, 0:4 * D], b_mod[0, 2 * D:6 * D].unsqueeze(0).broadcast_to([P, 4 * D])).then_inc(rows_loaded, 16)
        sp.dma_start(brow[:, 4 * D:7 * D], norm_gains[0, 1:4].rearrange("g d -> (g d)").unsqueeze(0)
                     .broadcast_to([P, 3 * D])).then_inc(rows_loaded, 16)
        for i in range(8):
            sp.dma_start(wqA[:, i], wq_v[:, :, P * i:P * i + P]).then_inc(wq_half_loaded[i // 4], 16)
        sp.wait_ge(y_gated, 2 * PAIRS)
        sp.dma_start(skn, skey_v).then_inc(subkeys_loaded, 16)
        for i in range(8, HS):
            if i % 4 == 0:
                sp.wait_ge(queries_done, i // 4 - 1)
            sp.dma_start(wqA[:, i % 8], wq_v[:, :, P * i:P * i + P]).then_inc(wq_half_loaded[i // 4 % 2], 16)
        sp.wait_ge(mixer_output, NT)
        for i in range(HS):
            if i >= 2:
                sp.wait_ge(late_queries, i - 1)
            sp.dma_start(wq2[:, i % 2], wq_v[:, :, P * i:P * i + P]).then_inc(wq_loaded[i % 2], 16)

    def pool5(pool):
        pool.wait_ge(y_summed, PAIRS)
        nc.gpsimd.memset(YT, 0.0).then_inc(y_transpose_zeroed, 1)

    def scalar5(act):
        y = ysum.rearrange("p a x v -> p (a x) v")
        act.wait_ge(head_norm_vector, 2)
        nc.scalar.activation(ysq.rearrange("p a x v -> p (a x) v"), y, ACT.Square).then_inc(head_norm_scalar, 1)
        act.wait_ge(head_norm_vector, 3)
        nc.scalar.activation(stats5[:, 32:64], stats5[:, 32:64], ACT.Sqrt, bias=eps[:, 2:3], scale=1.0 / DH).then_inc(head_norm_scalar, 1)
        for p in range(PAIRS):
            for b in range(2):
                act.wait_ge(y_transposed, 2 * p + b + 1)
                bank = v3(psum[4 + (2 * p + b) % 4][:, :])
                for rows, cols in ((LOW, slice(DH, P)), (HIGH, slice(0, DH))):
                    o = yrw[rows, p, 256 * b:256 * b + 256].rearrange("p (i c) -> p i c", c=DH)
                    i = nc.scalar.activation(o, bank[rows, :, cols], ACT.Identity, bias=par[rows, p, LNX_B:LNX_B + 1],
                                             scale=par[rows, p, LNX_G:LNX_G + 1])
                i.then_inc(y_affine, 1)
        n = [0]

        def put(i):
            n[0] += 1
            i.then_inc(norm1_scalar, 1)

        def columns(t):
            for h in range(2):
                act.wait_ge(h2_transposed, 2 * t + h + 1)
                nc.scalar.activation(h2T[:, 4 * h:4 * h + 4, P * t:P * t + P], v3(psum[2 * t + h][:, :]),
                                     ACT.Identity).then_inc(h2_columns, 1)

        for t in range(NT):
            act.wait_ge(mixer_output, t + 1)
            for h in range(2):
                if n[0]:
                    act.wait_ge(norm1_scalar, n[0])
                put(nc.scalar.activation(square_dump5[:, 0:512], psum[2 * t + h][:, :], ACT.Square,
                                         accum_out=stats5[:, 64 + 2 * t + h:65 + 2 * t + h]))
            if t >= 1:
                columns(t - 1)
            act.wait_ge(norm1_vector, 5 * t + 1)
            put(nc.scalar.activation(stats5[:, 80 + t:81 + t], stats5[:, 76 + t:77 + t], ACT.Sqrt, bias=eps[:, 0:1], scale=1.0 / D))
            act.wait_ge(norm1_vector, 5 * t + 4)
            act.wait_ge(norm1_scalar, n[0])
            put(nc.scalar.activation(square_dump5, xn[:, t, :], ACT.Square, accum_out=stats5[:, 84 + t:85 + t]))
            act.wait_ge(norm1_scalar, n[0])
            put(nc.scalar.activation(stats5[:, 88 + t:89 + t], stats5[:, 84 + t:85 + t], ACT.Sqrt, bias=eps[:, 0:1], scale=1.0 / D))
        act.wait_ge(rows_finished, 5)
        for b in range(4):
            act.wait_ge(subkeys_transposed, b + 1)
            nc.scalar.activation(skT[:, 4 * b:4 * b + 4], v3(psum[b][:, :]), ACT.Identity).then_inc(subkeys_moved, 1)
        for b in range(4):
            act.wait_ge(queries_done, b + 1)
            nc.scalar.activation(qT[:, b % 2], psum[4 + b % 2][:, :], ACT.Identity).then_inc(queries_moved, 1)
            act.wait_ge(scores_done, b + 1)
            nc.scalar.activation(SC[:, 0, 4 * b:4 * b + 4], v3(psum[b % 2][:, :]), ACT.Identity).then_inc(scores_moved, 1)
            if b == 0:
                act.wait_ge(scores_moved, 1)
                act.wait_ge(h2_rows, 2 * NT)
                for h in range(2):
                    nc.scalar.activation(SCs[:, h], SC[:, 0, 2 * h:2 * h + 2, :], ACT.Identity).then_inc(scores_staged, 1)
            if b == 1:
                nc.scalar.activation(h2cur, H2N[:, 0, :], ACT.Identity).then_inc(h2_current, 1)
                act.wait_ge(experts_chosen, 1)
                nc.scalar.activation(prob, top, ACT.Exp, bias=neg_largest[:, 0:1], accum_out=exp_sum[:, 0:1]).then_inc(probabilities_raised, 1)
        columns(NT - 1)

    def vector5(dve):
        n = [0]

        def put(i):
            n[0] += 1
            i.then_inc(head_norm_vector, 1)
            dve.wait_ge(head_norm_vector, n[0])

        dve.wait_ge(y_summed, PAIRS)
        y = ysum.rearrange("p a x v -> p (a x) v")
        nc.vector.tensor_reduce(stats5[:, 0:32], y, AX.X, ALU.add).then_inc(head_sums, 1)
        dve.wait_ge(head_sums, 1)
        put(nc.vector.tensor_scalar(stats5[:, 0:32], stats5[:, 0:32], 1.0 / DH, None, ALU.mult))
        put(nc.vector.tensor_tensor(y, y, stats5[:, 0:32].unsqueeze(2).broadcast_to([P, 32, DH]), ALU.subtract))
        dve.wait_ge(head_norm_scalar, 1)
        put(nc.vector.tensor_reduce(stats5[:, 32:64], ysq.rearrange("p a x v -> p (a x) v"), AX.X, ALU.add))
        dve.wait_ge(head_norm_scalar, 2)
        put(nc.vector.reciprocal(stats5[:, 32:64], stats5[:, 32:64]))
        dve.wait_ge(y_transpose_zeroed, 1)
        rs = stats5[:, 32:64].unsqueeze(2).broadcast_to([P, 32, DH])
        nc.vector.tensor_tensor(YT[HIGH, :, 0:DH], y[HIGH], rs[HIGH], ALU.mult)
        put(nc.vector.tensor_tensor(YT[LOW, :, DH:P], y[LOW], rs[LOW], ALU.mult))
        for p in range(PAIRS):
            dve.wait_ge(y_affine, 2 * p + 2)
            nc.vector.tensor_tensor(yrw[:, p], yrw[:, p], bonus[:, p], ALU.add).then_inc(y_gated, 1)
            dve.wait_ge(y_gated, 2 * p + 1)
            nc.vector.tensor_tensor(yrw[:, p], yrw[:, p], gate[:, p], ALU.mult).then_inc(y_gated, 1)
        dve.wait_ge(rows_loaded, 32)
        dve.wait_ge(modulation_rows_moved, 16)
        nc.vector.tensor_tensor(rows.rearrange("p a b -> p (a b)"), rows.rearrange("p a b -> p (a b)"), brow[:, 0:4 * D],
                                ALU.add).then_inc(rows_finished, 1)
        dve.wait_ge(rows_finished, 1)
        nc.vector.tensor_tensor(g1row, g1row, brow[:, 4 * D:5 * D], ALU.mult).then_inc(rows_finished, 1)
        nc.vector.scalar_tensor_tensor(a2row, a2row, 1.0, brow[:, 5 * D:6 * D], ALU.add, ALU.mult).then_inc(rows_finished, 1)
        nc.vector.tensor_tensor(g2row, g2row, brow[:, 6 * D:7 * D], ALU.mult).then_inc(rows_finished, 2)
        dve.wait_ge(rows_finished, 5)
        k = [0]

        def link(i):
            k[0] += 1
            i.then_inc(norm1_vector, 1)
            dve.wait_ge(norm1_vector, k[0])

        for t in range(NT):
            dve.wait_ge(norm1_scalar, 5 * t + 2)
            link(nc.vector.tensor_tensor(stats5[:, 76 + t:77 + t], stats5[:, 64 + 2 * t:65 + 2 * t], stats5[:, 65 + 2 * t:66 + 2 * t], ALU.add))
            dve.wait_ge(norm1_scalar, 5 * t + 3)
            link(nc.vector.reciprocal(stats5[:, 80 + t:81 + t], stats5[:, 80 + t:81 + t]))
            for h in range(2):
                i = nc.vector.scalar_tensor_tensor(normed5[:, 512 * h:512 * h + 512], psum[2 * t + h][:, :],
                                                   stats5[:, 80 + t:81 + t], g1row[:, 512 * h:512 * h + 512], ALU.mult, ALU.mult)
            link(i)
            link(nc.vector.tensor_tensor(xn[:, t, :], xn[:, t, :], normed5, ALU.add))
            dve.wait_ge(norm1_scalar, 5 * t + 5)
            link(nc.vector.reciprocal(stats5[:, 88 + t:89 + t], stats5[:, 88 + t:89 + t]))
            nc.vector.scalar_tensor_tensor(H2N[:, t, :], xn[:, t, :], stats5[:, 88 + t:89 + t], a2row, ALU.mult,
                                           ALU.mult).then_inc(h2_rows, 1)
            dve.wait_ge(h2_rows, 2 * t + 1)
            nc.vector.tensor_tensor(H2N[:, t, :], H2N[:, t, :], sh2row, ALU.add).then_inc(h2_rows, 1)

    def tensor5(pe):
        def project_out(t, ks):
            for k in ks:
                a = (yconv if k < PAIRS else yrw)[:, k % PAIRS, P * t:P * t + P]
                for h in range(2):
                    m = nc.tensor.matmul(psum[2 * t + h][:, :], a, wo[:, k, 512 * h:512 * h + 512],
                                         start=k == 0, stop=k == KT - 1)
            return m

        for d in range(2):
            pe.wait_ge(chunk_vector_moves[d], NVC * 3 * PAIRS)
            pe.wait_ge(chunk_scalar_moves[d], NAC * 3 * PAIRS)
        pe.wait_ge(wout_loaded[0], 16)
        project_out(0, range(4))
        pe.wait_ge(head_norm_vector, 5)
        pe.wait_ge(modulation_rows_moved, 16)
        for b in range(8):
            if b >= 4:
                pe.wait_ge(y_affine, b - 3)
            for i in range(4):
                m = nc.tensor.transpose(psum[4 + b % 4][:, P * i:P * i + P], YT[:, 4 * b + i, :], ident)
            m.then_inc(y_transposed, 1)
        project_out(1, range(4))

        def columns(t):
            pe.wait_ge(h2_rows, 2 * t + 2)
            for h in range(2):
                for k in range(4):
                    m = nc.tensor.transpose(psum[2 * t + h][:, P * k:P * k + P],
                                            H2N[:, t, P * (4 * h + k):P * (4 * h + k) + P], ident)
                m.then_inc(h2_transposed, 1)

        pe.wait_ge(wout_loaded[1], 16)
        pe.wait_ge(y_gated, 2 * PAIRS)
        for t in range(NT):
            project_out(t, range(4 if t < 2 else 0, KT)).then_inc(mixer_output, 1)
            if t:
                columns(t - 1)
        pe.wait_ge(subkeys_loaded, 16)
        pe.wait_ge(h2_columns, 4)
        for b in range(4):
            for i in range(4):
                m = nc.tensor.transpose(psum[b][:, P * i:P * i + P], skn[:, 4 * b + i], ident)
            m.then_inc(subkeys_transposed, 1)
        def queries(b):
            pe.wait_ge(wq_half_loaded[b % 2], 64 * (b // 2 + 1))
            if b >= 2:
                pe.wait_ge(queries_moved, b - 1)
            else:
                pe.wait_ge(h2_columns, 6)
            for i in range(4):
                for k in range(KT):
                    m = nc.tensor.matmul(psum[4 + b % 2][:, P * i:P * i + P], wqA[:, 4 * (b % 2) + i, k, :], h2T[:, k, 0:P],
                                         start=k == 0, stop=k == KT - 1)
            m.then_inc(queries_done, 1)

        def scores(b):
            pe.wait_ge(subkeys_moved, 4)
            pe.wait_ge(queries_moved, b + 1)
            if b >= 2:
                pe.wait_ge(scores_moved, b - 1)
            for i in range(4):
                m = nc.tensor.matmul(psum[b % 2][:, P * i:P * i + P], qT[:, b % 2, P * i:P * i + P], skT[:, 4 * b + i],
                                     start=True, stop=True)
            m.then_inc(scores_done, 1)

        for b in range(4):
            queries(b)
            scores(b)
        columns(NT - 1)

    PO = [psum[6], psum[7]]
    NSL = TOPK
    out_v = out[0].rearrange("(t p) d -> t p d", p=P)

    def tiles6(engine, body, tail):
        body(0, True)
        with engine.Fori(1, NT) as t:
            body(t, False)
        tail()

    def sync6(sp):
        with sp.Fori(0, NT) as t:
            sp.wait_ge(final_vector, 4 * t + 8)
            sp.dma_start(out_v[t], out_tile).then_inc(output_stored, 16)
        sp.wait_ge(output_stored, 16 * NT + 16)

    def pool6(pool):
        pool.wait_ge(h2_rows, 2 * NT)
        nc.gpsimd.iota(iot[:, 0:NCAND], pattern=[[1, NCAND]], base=0, channel_multiplier=0,
                       allow_small_or_imprecise_dtypes=True).then_inc(iota_made, 1)

        def gather(kind, g, hi, j, first):
            ring, table, sems, used = [(u_ring, peer_u[0], u_rows, dots), (v_ring, peer_v[0], v_rows, experts_added)][kind]
            if not (first and hi == 0 and j < RING):
                pool.wait_ge(used, NSL * g + j + 1 - RING)
            apart(pool)
            pool.indirect_dma_start(ring[:, j % RING, :], None, table,
                                    bass.IndirectOffsetOnAxis(ap=idx[:, hi % 4, j:j + 1].bitcast(U32), axis=0)
                                    ).then_inc(sems[j % RING], 16)

        def body(t, first):
            for h in range(HEADS):
                g = t * HEADS + h
                pool.wait_ge(experts_chosen, g + 1)
                for j in range(NSL):
                    gather(0, g, h, j, first)
                    if h:
                        if first and h == 1 and j == 0:
                            pool.wait_ge(queries_done, 4)
                        gather(1, g - 1, h - 1, j, first)
                    elif not first:
                        gather(1, g - 1, HEADS - 1, j, False)

        def tail():
            for j in range(NSL):
                gather(1, NT * HEADS - 1, HEADS - 1, j, False)
        tiles6(pool, body, tail)

    def scalar6(act):

        def stage_scores(t, h):
            g = t * HEADS + h
            nc.scalar.activation(SCs[:, h % 2], SC[:, t, 2 * h:2 * h + 2, :], ACT.Identity).then_inc(scores_staged, 1)

        def diags(g, hp):
            for j in range(NSL):
                if not (isinstance(g, int) and g == 0 and j < 4):
                    act.wait_ge(experts_added, NSL * g + j - 3)
                nc.scalar.activation(diag[:, j % 4], ident, ACT.Identity, scale=expert_w[:, hp % 2, j:j + 1]).then_inc(weight_diagonals, 1)

        def exps(g):
            act.wait_ge(experts_chosen, g + 1)
            act.wait_ge(probabilities, 2 * g)
            nc.scalar.activation(prob, top, ACT.Exp, bias=neg_largest[:, 0:1], accum_out=exp_sum[:, 0:1]).then_inc(probabilities_raised, 1)

        def finish(t):
            act.wait_ge(experts_added, NSL * HEADS * (t + 1))
            act.wait_ge(final_vector, 4 * t + 4)
            nc.scalar.activation(square_dump[:, 0:512], PO[0][:, :], ACT.Square, accum_out=final_stats[:, 0:1]).then_inc(final_scalar, 1)
            act.wait_ge(final_scalar, 3 * t + 1)
            nc.scalar.activation(square_dump[:, 0:512], PO[1][:, :], ACT.Square, accum_out=final_stats[:, 1:2]).then_inc(final_scalar, 1)
            act.wait_ge(final_vector, 4 * t + 5)
            nc.scalar.activation(final_stats[:, 3:4], final_stats[:, 2:3], ACT.Sqrt, bias=eps[:, 0:1], scale=1.0 / D).then_inc(final_scalar, 1)


        def late_scores(h):
            for a in range(2):
                act.wait_ge(late_queries, 2 * h + a + 1)
                nc.scalar.activation(qB[:, a], psum[2 + a][:, 0:3 * P], ACT.Identity).then_inc(late_queries_moved, 1)
            for a in range(2):
                act.wait_ge(late_scores_done, 2 * h + a + 1)
                nc.scalar.activation(SC[:, 1:NT, 2 * h + a, :], v3(psum[a][:, 0:3 * P]), ACT.Identity).then_inc(late_scores_moved, 1)

        def body(t, first):
            for h in range(HEADS):
                g = t * HEADS + h
                if h == 0 and not first:
                    act.wait_ge(dots, NSL * g)
                    nc.scalar.activation(h2cur, H2N[:, t, :], ACT.Identity).then_inc(h2_current, 1)
                if first:
                    late_scores(h)
                    if h == HEADS - 2:
                        act.wait_ge(late_scores_moved, 4)
                if h or not first:
                    act.wait_ge(expert_weights, g)
                    diags(g - 1, (h - 1) % HEADS)
                act.wait_ge(experts_chosen, g + 1)
                if h < HEADS - 2:
                    stage_scores(t, h + 2)
                else:
                    stage_scores(t + 1, h + 2 - HEADS)
                exps(g + 1)
                act.wait_ge(dots, NSL * (g + 1))
                nc.scalar.activation(gelu_dot[:, h % 2], acts[:, h % 2], ACT.Gelu).then_inc(gelus, 1)
                if h == 0 and not first:
                    finish(t - 1)

        def tail():
            g = NT * HEADS
            act.wait_ge(expert_weights, g)
            diags(g - 1, HEADS - 1)
            finish(NT - 1)
        tiles6(act, body, tail)

    def vector6(dve):
        NL = LINKS

        def topk(g, hp, first):
            n = [0]

            def link(i):
                n[0] += 1
                i.then_inc(topk_links, 1)
                dve.wait_ge(topk_links, NL * g + n[0])
                apart(dve)

            dve.wait_ge(scores_staged, g + 1)
            apart(dve)
            a = SCs[:, hp % 2]
            u16, p16 = i16.bitcast(U32), pos.bitcast(U32)
            for s in range(2):
                i = nc.vector.max(v16[:, s, 0:8], a[:, s])
            link(i)
            for s in range(2):
                nc.vector.max_index(u16[:, s, 0:8], v16[:, s, 0:8], a[:, s])
                i = nc.vector.match_replace(scores_left[:, s], v16[:, s, 0:8], a[:, s], -3.0e38)
            link(i)
            for s in range(2):
                i = nc.vector.max(v16[:, s, 8:16], scores_left[:, s])
            link(i)
            for s in range(2):
                i = nc.vector.max_index(u16[:, s, 8:16], v16[:, s, 8:16], scores_left[:, s])
            link(i)
            link(nc.vector.tensor_copy(i16f, u16))
            link(nc.vector.tensor_scalar(i16f[:, 0], i16f[:, 0], float(KEYS), None, ALU.mult))
            at = 0
            for r, m, w in ROWS:
                for src, dst, op in ((v16, cand, ALU.add), (i16f, cand_number, ALU.add)):
                    i = nc.vector.tensor_tensor(dst[:, at:at + m * w].rearrange("p (a b) -> p a b", b=w),
                                                src[:, 0, r:r + m].unsqueeze(2).broadcast_to([P, m, w]),
                                                src[:, 1, 0:w].unsqueeze(1).broadcast_to([P, m, w]), op)
                at += m * w
            link(i)
            if not first:
                dve.wait_ge(probabilities_raised, g)
                apart(dve)
            link(nc.vector.max(top[:, 0:8], cand[:, 0:NCAND]))
            nc.vector.max_index(p16[:, 0:8], top[:, 0:8], cand[:, 0:NCAND])
            link(nc.vector.match_replace(cand_left[:, 0:NCAND], top[:, 0:8], cand[:, 0:NCAND], -3.0e38))
            link(nc.vector.max(top[:, 8:16], cand_left[:, 0:NCAND]))
            nc.vector.tensor_scalar(neg_largest[:, 0:1], top[:, 0:1], -1.0, None, ALU.mult)
            link(nc.vector.max_index(p16[:, 8:16], top[:, 8:16], cand_left[:, 0:NCAND]))
            link(nc.vector.tensor_copy(posf, p16))
            link(nc.vector.tensor_tensor(one_hot, iot[:, 0:NCAND].unsqueeze(1).broadcast_to([P, TOPK, NCAND]),
                                         posf.unsqueeze(2).broadcast_to([P, TOPK, NCAND]), ALU.is_equal))
            link(nc.vector.tensor_tensor(one_hot, one_hot, cand_number[:, 0:NCAND].unsqueeze(1).broadcast_to([P, TOPK, NCAND]), ALU.mult))
            link(nc.vector.tensor_reduce(expert_f32, one_hot, AX.X, ALU.add))
            assert n[0] == NL, n[0]
            nc.vector.tensor_copy(idx[:, hp % 4].bitcast(U32), expert_f32).then_inc(experts_chosen, 1)

        def softmax(g, hp):
            dve.wait_ge(probabilities_raised, g + 1)
            nc.vector.reciprocal(exp_sum[:, 1:2], exp_sum[:, 0:1]).then_inc(probabilities, 1)
            dve.wait_ge(probabilities, 2 * g + 1)
            nc.vector.tensor_scalar(softmax_w[:, hp % 2], prob, exp_sum[:, 1:2], None, ALU.mult).then_inc(probabilities, 1)

        def finish(t):
            dve.wait_ge(final_scalar, 3 * t + 2)
            nc.vector.tensor_tensor(final_stats[:, 2:3], final_stats[:, 0:1], final_stats[:, 1:2], ALU.add).then_inc(final_vector, 1)
            dve.wait_ge(final_scalar, 3 * t + 3)
            nc.vector.reciprocal(final_stats[:, 4:5], final_stats[:, 3:4]).then_inc(final_vector, 1)
            dve.wait_ge(final_vector, 4 * t + 6)
            dve.wait_ge(output_stored, 16 * t + 16)
            for h in range(2):
                i = nc.vector.scalar_tensor_tensor(out_tile[:, 512 * h:512 * h + 512], PO[h][:, :], final_stats[:, 4:5],
                                                   g2row[:, 512 * h:512 * h + 512], ALU.mult, ALU.mult)
            i.then_inc(final_vector, 1)
            dve.wait_ge(final_vector, 4 * t + 7)
            nc.vector.tensor_tensor(out_tile, out_tile, xn[:, t, :], ALU.add).then_inc(final_vector, 1)

        credit(dve, final_vector, 4)
        credit(dve, output_stored, 16)
        dve.wait_ge(iota_made, 1)
        topk(0, 0, True)
        softmax(0, 0)

        def body(t, first):
            for h in range(HEADS):
                g = t * HEADS + h
                if h == 0:
                    dve.wait_ge(h2_current, t + 1)
                if h >= 3 or not first:
                    dve.wait_ge(experts_added, NSL * (g - 2))
                topk(g + 1, (h + 1) % HEADS, False)
                for j in range(NSL):
                    dve.wait_ge(u_rows[j % RING], 32 * g + 16 * (j // RING) + 16)
                    nc.vector.tensor_tensor_reduce(u_ring[:, j % RING, :], u_ring[:, j % RING, :], h2cur, 1.0, 0.0, ALU.mult, ALU.add,
                                                   acts[:, h % 2, j:j + 1]).then_inc(dots, 1)
                softmax(g + 1, (h + 1) % HEADS)
                dve.wait_ge(gelus, g + 1)
                if h >= 2 or not first:
                    dve.wait_ge(weight_diagonals, NSL * (g - 1))
                nc.vector.tensor_tensor(expert_w[:, h % 2], gelu_dot[:, h % 2], softmax_w[:, h % 2], ALU.mult).then_inc(expert_weights, 1)
                if h == 0 and not first:
                    finish(t - 1)

        tiles6(dve, body, lambda: finish(NT - 1))

    def tensor6(pe):
        def experts(g, hp, first):
            for j in range(NSL):
                pe.wait_ge(weight_diagonals, NSL * g + j + 1)
                pe.wait_ge(v_rows[j % RING], 32 * g + 16 * (j // RING) + 16)
                for h in range(2):
                    m = nc.tensor.matmul(PO[h][:, :], diag[:, j % 4], v_ring[:, j % RING, 512 * h:512 * h + 512],
                                         start=hp == 0 and j == 0, stop=hp == HEADS - 1 and j == NSL - 1)
                m.then_inc(experts_added, 1)

        def late_scores(h):
            for a in range(2):
                i = 2 * h + a
                pe.wait_ge(wq_loaded[a], 16 * h + 16)
                if h:
                    pe.wait_ge(late_queries_moved, i - 1)
                for k in range(KT):
                    m = nc.tensor.matmul(psum[2 + a][:, 0:3 * P], wq2[:, a, k, :], h2T[:, k, P:T], start=k == 0, stop=k == KT - 1)
                m.then_inc(late_queries, 1)
            for a in range(2):
                i = 2 * h + a
                pe.wait_ge(late_queries_moved, i + 1)
                if h:
                    pe.wait_ge(late_scores_moved, i - 1)
                else:
                    pe.wait_ge(scores_moved, 4)
                for t in range(3):
                    m = nc.tensor.matmul(psum[a][:, P * t:P * t + P], qB[:, a, P * t:P * t + P], skT[:, i],
                                         start=True, stop=True)
                m.then_inc(late_scores_done, 1)

        pe.wait_ge(h2_columns, 2 * NT)

        def body(t, first):
            for h in range(HEADS):
                g = t * HEADS + h
                if first:
                    late_scores(h)
                if h:
                    if h == 1 and not first:
                        pe.wait_ge(final_vector, 4 * t + 4)
                    experts(g - 1, h - 1, first)
                elif not first:
                    experts(g - 1, HEADS - 1, False)
        tiles6(pe, body, lambda: experts(NT * HEADS - 1, HEADS - 1, False))


    n_masks = 4 + 4 * 6 + 16 + 12 + 12
    later_stages = {'sync': (sync4, sync5, sync6), 'pool': (pool4, pool5, pool6), 'scalar': (scalar4, scalar5, scalar6),
             'vector': (vector4, vector5, vector6), 'tensor': (tensor4, tensor5, tensor6)}

    @block.sync
    def _(sp):
        sp.dma_start(cc[:, 0, :], c[0].rearrange("(p k) -> p k", k=KT)).then_inc(cond_loaded, 16)
        sp.dma_start(cc[:, 1, :], c_ctx.rearrange("(p k) -> p k", k=KT)).then_inc(cond_loaded, 16)
        for i in range(8):
            sp.dma_start(wm[:, i], wmod_v[:, :, 256 * i:256 * i + 256]).then_inc(wmod_loaded[i], 16)
            if i == 2:
                for t in range(NTC):
                    sp.dma_start(ctxn[:, t, :], ctx_v[t]).then_inc(context_loaded, 16)
            if i == 6:
                sp.dma_start(prow[0:16, :], b_mod[0, 0:2048].rearrange("(r q) -> r q", q=P)).then_inc(param_rows_loaded, 16)
                sp.dma_start(prow[16:24, :], norm_gains[0, 0].rearrange("(r q) -> r q", q=P)).then_inc(param_rows_loaded, 16)
                par_rows = [tshift_mu[0, 0, 0], tshift_mu[0, 0, 1], tshift_mu[0, 0, 2],
                        tshift_mu[0, 1, 0], tshift_mu[0, 1, 1], tshift_mu[0, 1, 2],
                        decay_w0[0, 0], decay_w0[0, 1], iclr_a0[0, 0], iclr_a0[0, 1],
                        k_k[0], k_a[0], r_k[0].rearrange("h n -> (h n)"), lnx_g[0], lnx_b[0],
                        conv_w[0, 0], conv_w[0, 1], conv_w[0, 2]]
                for n, row in enumerate(par_rows):
                    sp.dma_start(prow2[4 * n:4 * n + 4, :], row.rearrange("(r q) -> r q", q=P)).then_inc(param_rows_loaded, 16)
            if i >= 4:
                sp.dma_start(xn[:, i - 4, :], x_v[i - 4]).then_inc(latents_loaded[i - 4], 16)
        for j, col in enumerate([25 * P, 26 * P, 24 * P]):
            sp.dma_start(wring[:, j], win_v[:, :, col:col + P]).then_inc(win_loaded[j], 16)
        sp.wait_ge(hT_lower, 6)
        sp.wait_ge(hT_upper, 6)

        def lora_loads(p):
            for d in range(2):
                sp.dma_start(lora[DH * d:DH * d + DH, d, 0, :],
                             decay_w2[0, d, :, bass.ds(p * P, P)]).then_inc(lora_loaded, 16)
                sp.dma_start(lora[DH * d:DH * d + DH, d, 1, :],
                             iclr_a2[0, d, :, bass.ds(p * P, P)]).then_inc(lora_loaded, 16)
            sp.dma_start(gw, gate_w2[0, :, bass.ds(p * P, P)]).then_inc(lora_loaded, 16)

        def pair_loads(p, first):
            for j, base in enumerate((16, 12, 20)):
                sp.wait_ge(projections_made, 3 * p + j + 1)
                sp.dma_start(wring[:, j], win_v[:, :, bass.ds(base * P + p * P, P)]).then_inc(win_loaded[j], 16)
            if not first:
                sp.wait_ge(aux_products, 7 * p)
                apart(sp)
            lora_loads(p)

        sp.wait_ge(pads_zeroed, 1)
        pair_loads(0, True)
        with sp.Fori(1, PAIRS) as p:
            pair_loads(p, False)
        for j, base in enumerate((4, 8, 0)):
            sp.wait_ge(projections_made, 3 * PAIRS + j + 1)
            sp.dma_start(wring[:, j], win_v[:, :, base * P:base * P + P]).then_inc(win_loaded[j], 16)
        with sp.Fori(1, PAIRS) as q:
            for j, base in enumerate((4, 8, 0)):
                sp.wait_ge(projections_made, 3 * (q + PAIRS) + j + 1)
                apart(sp)
                sp.dma_start(wring[:, j], win_v[:, :, bass.ds(base * P + q * P, P)]).then_inc(win_loaded[j], 16)
        sp.wait_ge(spilled_done, 16 * 5 * PAIRS)
        for stage in later_stages["sync"]:
            stage(sp)

    @block.gpsimd
    def _(pool):
        n = [0]

        def put(i, done=constants_made):
            n[0] += 1
            i.then_inc(done, 1)
            pool.wait_ge(done, n[0])

        put(nc.gpsimd.memset(ident, 0.0))
        put(nc.gpsimd.memset(head_ones, 0.0))
        put(nc.gpsimd.memset(eps[:, 0:1], NORM_EPS))
        put(nc.gpsimd.memset(eps[:, 1:2], 1e-12))
        put(nc.gpsimd.memset(eps[:, 2:3], LNX_EPS))
        put(nc.gpsimd.memset(eps[:, 3:4], 0.0))
        put(nc.gpsimd.memset(par[:, PAIRS], 0.0))
        put(nc.gpsimd.affine_select(out=ident, in_=ident, compare_op=ALU.not_equal, fill=1.0, base=0,
                                    pattern=[[-1, P]], channel_multiplier=1))
        put(nc.gpsimd.memset(head_ones[0:DH, 0:DH], 1.0))
        put(nc.gpsimd.memset(head_ones[DH:P, DH:P], 1.0))
        assert pool_masks(pool) == n_masks
        pool.wait_ge(hT_lower, 6)
        pool.wait_ge(hT_upper, 6)
        n[0] = 0
        for tile in (lora, kraw, vraw, rraw, VSb, KRb):
            put(nc.gpsimd.memset(tile, 0.0), pads_zeroed)
        put(nc.gpsimd.memset(scan_keep, 1.0), pads_zeroed)
        put(nc.gpsimd.memset(scan_keep.rearrange("p (n c) -> p n c", c=C)[:, :, 0:1], 0.0), pads_zeroed)
        def spills(p):
            pool.wait_ge(vs_ready, 2 * p + 2)
            apart(pool)
            pool.dma_start(vs_dram[p], VSb.rearrange("p a b -> p (a b)")).then_inc(spilled_done, 16)
            for d in range(2):
                pool.wait_ge(pair_dir_ready, 2 * p + d + 1)
                apart(pool)
                pool.dma_start(bk_dram[2 * p + d], BKb[:, d].rearrange("p a b -> p (a b)")).then_inc(spilled_done, 16)
                pool.dma_start(kr_dram[2 * p + d], KRb[:, d].rearrange("p a b -> p (a b)")).then_inc(spilled_done, 16)

        spills(0)
        with pool.Fori(1, PAIRS) as p:
            spills(p)
        for stage in later_stages["pool"]:
            stage(pool)

    @block.scalar
    def _(act):
        act.wait_ge(cond_loaded, 32)
        nc.scalar.activation(ccs, cc, ACT.Sigmoid).then_inc(silu_made, 1)
        act.wait_ge(constants_made, 6)
        for i in range(NTC + NT):
            if i < NTC:
                act.wait_ge(context_loaded, 16 * NTC)
                src = ctxn[:, i, :]
            else:
                act.wait_ge(latents_loaded[i - NTC], 16)
                src = xn[:, i - NTC, :]
            if i:
                act.wait_ge(square_sums, i)
            nc.scalar.activation(sq, src, ACT.Square, accum_out=ssq[:, i:i + 1]).then_inc(square_sums, 1)
        act.wait_ge(square_sums, NTC + NT)
        nc.scalar.activation(rstd[:, 0:6], ssq[:, 0:6], ACT.Sqrt, bias=eps[:, 0:1], scale=1.0 / D).then_inc(square_sums, 1)
        for b in range(4):
            act.wait_ge(mod_products, 2 * b + 2)
            nc.scalar.activation(modrow[0:2, T * b:T * b + T], psum[b][0:2, :], ACT.Identity).then_inc(mod_rows_moved, 1)
        act.wait_ge(mod_columns_made, 3)
        for t in range(NTC + NT):
            which = 1 if t < NTC else 0
            act.wait_ge(rows_transposed, 2 * t + 1)
            for k in range(4):
                i = nc.scalar.activation(hT[:, k, P * t:P * t + P], psum[2 * (t % 3)][:, P * k:P * k + P],
                                         ACT.Identity, bias=shsc[:, k, which:which + 1],
                                         scale=tab[:, k, which:which + 1])
            i.then_inc(hT_lower, 1)
        act.wait_ge(projections_made, 1)
        nc.scalar.activation(lo_w[:, TC:TT], psum[0][:, 0:T], ACT.Tanh)
        nc.scalar.activation(lo_w[:, 0:TC], psum[1][:, 0:TC], ACT.Tanh).then_inc(projections_evacuated, 1)
        act.wait_ge(projections_made, 2)
        nc.scalar.activation(lo_a[:, TC:TT], psum[2][:, 0:T], ACT.Identity)
        nc.scalar.activation(lo_a[:, 0:TC], psum[3][:, 0:TC], ACT.Identity).then_inc(projections_evacuated, 1)
        act.wait_ge(projections_made, 3)
        nc.scalar.activation(lo_g, psum[4][:, 0:T], ACT.Sigmoid).then_inc(projections_evacuated, 1)

        def pair(p, first):
            def aux(d, which):
                act.wait_ge(aux_products, 7 * p + [[1, 2], [4, 6]][d][which])
                if which == 0 and (d or not first):
                    act.wait_ge(decay_sums, 2 * p + d)
                if which == 1 and not first:
                    act.wait_ge(pair_dir_ready, 2 * p - 1 + d)
                dst, col = [decay_sig, aa[:, d]][which], 2 * which + d
                bx, bc = (0, 1) if (d, which) == (1, 0) else (5, 6)
                nc.scalar.activation(dst[:, TC:TT], psum[bx][:, 0:T], ACT.Sigmoid, bias=bias4[:, col:col + 1])
                nc.scalar.activation(dst[:, 0:TC], psum[bc][:, 0:TC], ACT.Sigmoid,
                                     bias=bias4[:, col:col + 1]).then_inc(aux_evacuated, 1)

            def factors(d):
                act.wait_ge(decay_sums, 2 * p + d + 1)
                if d or not first:
                    act.wait_ge(pair_dir_ready, 2 * p + d)
                nc.scalar.activation(e1, cum_before, ACT.Exp, scale=-DECAY)
                nc.scalar.activation(e3, cum_with, ACT.Exp, scale=DECAY)
                nc.scalar.activation(e2, cum_with, ACT.Exp, scale=-DECAY).then_inc(decay_factors, 1)

            act.wait_ge(projections_made, 3 * p + 4)
            if first:
                act.wait_ge(pads_zeroed, 8)
            else:
                act.wait_ge(shifted, 3 * p)
            nc.scalar.activation(kraw[:, XO:XO + T], psum[0][:, 0:T], ACT.Identity)
            nc.scalar.activation(kraw[:, CO:CO + TC], psum[1][:, 0:TC], ACT.Identity).then_inc(projections_evacuated, 1)
            act.wait_ge(pair_biases, p + 1)
            aux(0, 0)
            act.wait_ge(projections_made, 3 * p + 5)
            nc.scalar.activation(rraw[:, 1:1 + T], psum[2][:, 0:T], ACT.Identity).then_inc(projections_evacuated, 1)
            aux(0, 1)
            act.wait_ge(shifted, 3 * p + 1)
            nc.scalar.activation(sqk, k_sh, ACT.Square, scale=pp[:, K_K:K_K + 1]).then_inc(kk_ready, 1)
            act.wait_ge(projections_made, 3 * p + 6)
            nc.scalar.activation(vraw[:, XO:XO + T], psum[3][:, 0:T], ACT.Identity)
            nc.scalar.activation(vraw[:, CO:CO + TC], psum[4][:, 0:TC], ACT.Identity).then_inc(projections_evacuated, 1)
            act.wait_ge(aux_products, 7 * p + 3)
            nc.scalar.activation(t2[:, TC:TT], psum[5][:, 0:T], ACT.Sqrt, bias=eps[:, 1:2])
            nc.scalar.activation(t2[:, 0:TC], psum[6][:, 0:TC], ACT.Sqrt, bias=eps[:, 1:2]).then_inc(aux_evacuated, 1)
            aux(1, 0)
            factors(0)
            act.wait_ge(shifted, 3 * p + 3)
            if not first:
                act.wait_ge(spilled_done, 16 * 5 * p)
            v_c = v_sh.rearrange("p (n c) -> p n c", c=C)
            nc.scalar.activation(VSb[0:DH, :, DH:P], v_c[0:DH], ACT.Identity).then_inc(vs_ready, 1)
            nc.scalar.activation(VSb[DH:P, :, 0:DH], v_c[DH:P], ACT.Identity).then_inc(vs_ready, 1)
            act.wait_ge(aux_products, 7 * p + 5)
            nc.scalar.activation(gate[:, p, :], psum[2][:, 0:T], ACT.Identity).then_inc(aux_evacuated, 1)
            aux(1, 1)
            factors(1)

        pair(0, True)
        with act.Fori(1, PAIRS) as p:
            pair(p, False)
        act.wait_ge(pair_dir_ready, 2 * PAIRS)
        credit(act, conv_steps, 8)
        with act.Fori(0, PAIRS // 2) as qq:
            for e in range(2):
                q = 2 * qq + e
                act.wait_ge(projections_made, 3 * q + 3 * PAIRS + 4)
                act.wait_ge(conv_steps, 4 * q + 4)
                nc.scalar.activation(conv_in[e], psum[CONV_BANKS[e][0]][:, 0:T], ACT.Identity).then_inc(projections_evacuated, 1)
        for stage in later_stages["scalar"]:
            stage(act)

    @block.vector
    def _(dve):
        n_dv = [0]

        dve.wait_ge(silu_made, 1)
        nc.vector.tensor_tensor(silu_col.rearrange("p k v -> p v k"), cc, ccs, ALU.mult).then_inc(silu_made, 1)
        dve.wait_ge(params_transposed, 1)
        nc.vector.tensor_copy(pcolA[:, 0:24], psum[4][:, 0:24]).then_inc(param_columns_made, 1)
        dve.wait_ge(params_transposed, 2)
        nc.vector.tensor_copy(par[:, 0:PAIRS].rearrange("p r i -> p i r"),
                              psum[5][:, 0:4 * NPAR].rearrange("p (i r) -> p i r", r=PAIRS)).then_inc(param_columns_made, 1)
        dve.wait_ge(constants_made, 10)
        nc.vector.tensor_copy(mix_diag, head_ones).then_inc(param_columns_made, 1)
        dve.wait_ge(square_sums, NTC + NT + 1)
        nc.vector.reciprocal(rstd[:, 0:6], rstd[:, 0:6]).then_inc(rstd_made, 1)
        dve.wait_ge(rstd_made, 1)
        for t in range(NTC + NT):
            src = ctxn[:, t, :] if t < NTC else xn[:, t - NTC, :]
            nc.vector.tensor_scalar(xs[:, t, :], src, rstd[:, t:t + 1], None, ALU.mult).then_inc(normed_rows, 1)
        dve.wait_ge(mod_products, 9)
        dve.wait_ge(param_columns_made, 3)
        nc.vector.tensor_tensor(shsc, psum[6][:, 0:32].rearrange("p (a b) -> p a b", b=2),
                                pcolA[:, 0:16].unsqueeze(2).broadcast_to([P, 16, 2]), ALU.add).then_inc(mod_columns_made, 1)
        dve.wait_ge(mod_columns_made, 1)
        nc.vector.tensor_scalar(tab, shsc[:, 8:16], 1.0, None, ALU.add).then_inc(mod_columns_made, 1)
        dve.wait_ge(mod_columns_made, 2)
        nc.vector.tensor_tensor(tab, tab, pcolA[:, 16:24].unsqueeze(2).broadcast_to([P, 8, 2]),
                                ALU.mult).then_inc(mod_columns_made, 1)
        dve.wait_ge(mod_columns_made, 3)
        for t in range(NTC + NT):
            which = 1 if t < NTC else 0
            dve.wait_ge(rows_transposed, 2 * t + 2)
            for k in range(4, 8):
                i = nc.vector.tensor_scalar(hT[:, k, P * t:P * t + P], psum[2 * (t % 3) + 1][:, P * (k - 4):P * (k - 4) + P],
                                            tab[:, k, which:which + 1], shsc[:, k, which:which + 1], ALU.mult, ALU.add)
            i.then_inc(hT_upper, 1)
        dve.wait_ge(pads_zeroed, 8)
        nc.vector.tensor_copy(bias4, par[:, 0, W0_F:W0_F + 4]).then_inc(pair_biases, 1)

        def chunks(a):
            return a.rearrange("p (n c) -> p n c", c=C)

        def pair(p, first):
            n_dv[0] = 0
            base = p * PAIR_STEPS

            def link(ins):
                n_dv[0] += 1
                ins.then_inc(vector_steps, 1)
                dve.wait_ge(vector_steps, base + n_dv[0])

            def shift(raw, off, cols, dst, dst0, c0, mp, mn):
                o = dst[:, dst0:dst0 + cols]
                link(nc.vector.tensor_scalar(o, raw[:, off:off + cols], pp[:, c0:c0 + 1], None, ALU.mult))
                link(nc.vector.scalar_tensor_tensor(o, raw[:, off - 1:off - 1 + cols], pp[:, mp:mp + 1], o, ALU.mult, ALU.add))
                return nc.vector.scalar_tensor_tensor(o, raw[:, off + 1:off + 1 + cols], pp[:, mn:mn + 1], o, ALU.mult, ALU.add)

            if not first:
                dve.wait_ge(aux_evacuated, 6 * p)
            nc.vector.tensor_copy(pp[:, 0:NPAR], par[:, p, :]).then_inc(pair_params, 1)
            dve.wait_ge(pair_params, 6 * p + 1)
            nc.vector.tensor_scalar(pp[:, C0_R:C0_R + 3], pp[:, MP_R:MP_R + 3], -1.0, 1.0, ALU.mult, ALU.add).then_inc(pair_params, 1)
            nc.vector.tensor_scalar(pp[:, OMKA:OMKA + 1], pp[:, K_A:K_A + 1], -1.0, 1.0, ALU.mult, ALU.add).then_inc(pair_params, 1)
            dve.wait_ge(pair_params, 6 * p + 3)
            nc.vector.tensor_tensor(pp[:, C0_R:C0_R + 3], pp[:, C0_R:C0_R + 3], pp[:, MN_R:MN_R + 3], ALU.subtract).then_inc(pair_params, 3)
            dve.wait_ge(pair_params, 6 * p + 6)
            dve.wait_ge(projections_evacuated, 3 * p + 4)
            link(shift(kraw, CO, TC, k_sh, 0, C0_K, MP_K, MN_K))
            shift(kraw, XO, T, k_sh, TC, C0_K, MP_K, MN_K).then_inc(shifted, 1)

            def cumulate(d):
                dve.wait_ge(aux_evacuated, 6 * p + [1, 4][d])
                if d or not first:
                    dve.wait_ge(decay_factors, 2 * p + d)
                link(nc.vector.tensor_tensor_scan(cs, scan_keep, decay_sig, 0.0, ALU.mult, ALU.add))
                if d == 0:
                    link(nc.vector.tensor_copy(cum_with, cs))
                    nc.vector.tensor_tensor(cum_before, cs, decay_sig, ALU.subtract).then_inc(decay_sums, 1)
                else:
                    tot = chunks(cs)[:, :, C - 1:C].broadcast_to([P, NCH, C])
                    link(nc.vector.tensor_tensor(chunks(cum_before), tot, chunks(cs), ALU.subtract))
                    nc.vector.tensor_tensor(cum_with, cum_before, decay_sig, ALU.add).then_inc(decay_sums, 1)

            def products(d):
                dve.wait_ge(decay_factors, 2 * p + d + 1)
                dve.wait_ge(aux_evacuated, 6 * p + [2, 6][d])
                if not first:
                    dve.wait_ge(spilled_done, 16 * 5 * p)
                link(nc.vector.tensor_scalar(t1, aa[:, d], pp[:, K_A:K_A + 1], pp[:, OMKA:OMKA + 1], ALU.mult, ALU.add))
                link(nc.vector.tensor_tensor(t1, t1, k_sh, ALU.mult))
                k3 = chunks(t1)
                f1, f2, f3, kk3, r3 = chunks(e1), chunks(e2), chunks(e3), chunks(kk), chunks(r_sh)
                lo, hi = slice(0, DH), slice(DH, P)
                link(nc.vector.tensor_tensor(BKb[lo, d, :, DH:P], k3[lo], f3[lo], ALU.mult))
                link(nc.vector.tensor_tensor(BKb[hi, d, :, 0:DH], k3[hi], f3[hi], ALU.mult))
                link(nc.vector.scalar_tensor_tensor(t1, kk, -1.0, aa[:, d], ALU.mult, ALU.mult))
                link(nc.vector.tensor_tensor(BKb[lo, d, :, 0:DH], k3[lo], f3[lo], ALU.mult))
                link(nc.vector.tensor_tensor(BKb[hi, d, :, DH:P], k3[hi], f3[hi], ALU.mult))
                link(nc.vector.tensor_tensor(KRb[lo, d, :, 0:DH], kk3[lo], f1[lo], ALU.mult))
                link(nc.vector.tensor_tensor(KRb[hi, d, :, DH:P], kk3[hi], f1[hi], ALU.mult))
                link(nc.vector.tensor_tensor(KRb[lo, d, TC // C:, DH:P], r3[lo], f2[lo, TC // C:], ALU.mult))
                link(nc.vector.tensor_tensor(KRb[hi, d, TC // C:, 0:DH], r3[hi], f2[hi, TC // C:], ALU.mult))
                at = C - 1 if d == 0 else 0
                nc.vector.tensor_copy(pc_all[:, p * 2 + d, :], f2[:, :, at]).then_inc(pair_dir_ready, 1)

            cumulate(0)
            dve.wait_ge(projections_evacuated, 3 * p + 5)
            shift(rraw, 1, T, r_sh, 0, C0_R, MP_R, MN_R).then_inc(shifted, 1)
            dve.wait_ge(shifted, 3 * p + 2)
            nc.vector.scalar_tensor_tensor(rk, r_sh, pp[:, R_K:R_K + 1], k_sh[:, TC:TT], ALU.mult, ALU.mult).then_inc(bonus_product_in, 1)
            dve.wait_ge(projections_evacuated, 3 * p + 6)
            if not first:
                dve.wait_ge(vs_ready, 2 * p)
            link(shift(vraw, CO, TC, v_sh, 0, C0_V, MP_V, MN_V))
            shift(vraw, XO, T, v_sh, TC, C0_V, MP_V, MN_V).then_inc(shifted, 1)
            dve.wait_ge(aux_evacuated, 6 * p + 3)
            link(nc.vector.reciprocal(t2, t2))
            link(nc.vector.scalar_tensor_tensor(kk, k_sh, pp[:, K_K:K_K + 1], t2, ALU.mult, ALU.mult))
            products(0)
            dve.wait_ge(aux_products, 7 * p + 7)
            dve.wait_ge(shifted, 3 * p + 3)
            nc.vector.tensor_tensor(bonus[:, p, :], psum[7][:, 0:T], v_sh[:, TC:TT], ALU.mult).then_inc(bonus_made, 1)
            cumulate(1)
            dve.wait_ge(aux_evacuated, 6 * p + 6)
            nc.vector.tensor_copy(bias4, par[:, p + 1, W0_F:W0_F + 4]).then_inc(pair_biases, 1)
            products(1)
            return n_dv[0]

        n = pair(0, True)
        assert n == PAIR_STEPS, n
        with dve.Fori(1, PAIRS) as p:
            pair(p, False)

        def rows_of(a):
            return a.rearrange("p (n c) -> p n c", c=GRID)

        with dve.Fori(0, PAIRS // 2) as qq:
            for e in range(2):
                q = 2 * qq + e
                banks = CONV_BANKS[e]
                nc.vector.tensor_copy(pp[:, 0:NPAR], par[:, q, :]).then_inc(pair_params, 1)
                dve.wait_ge(pair_params, q + 6 * PAIRS + 1)
                dve.wait_ge(projections_evacuated, q + 3 * PAIRS + 4)
                dve.wait_ge(projections_made, 3 * q + 3 * PAIRS + 5)
                nc.vector.tensor_tensor(t2[:, 0:T], conv_in[e], psum[banks[1]][:, 0:T], ALU.mult).then_inc(conv_steps, 1)
                dve.wait_ge(conv_steps, 4 * q + 9)
                nc.vector.tensor_scalar(cs[:, 0:T], t2[:, 0:T], pp[:, CV1:CV1 + 1], None, ALU.mult).then_inc(conv_steps, 1)
                dve.wait_ge(conv_steps, 4 * q + 10)
                z, o = rows_of(t2[:, 0:T]), rows_of(cs[:, 0:T])
                nc.vector.scalar_tensor_tensor(o[:, :, 1:], z[:, :, :-1], pp[:, CV0:CV0 + 1], o[:, :, 1:],
                                               ALU.mult, ALU.add).then_inc(conv_steps, 1)
                dve.wait_ge(conv_steps, 4 * q + 11)
                nc.vector.scalar_tensor_tensor(o[:, :, :-1], z[:, :, 1:], pp[:, CV2:CV2 + 1], o[:, :, :-1],
                                               ALU.mult, ALU.add).then_inc(conv_steps, 1)
                dve.wait_ge(conv_steps, 4 * q + 12)
                dve.wait_ge(projections_made, 3 * q + 3 * PAIRS + 6)
                nc.vector.tensor_tensor(yconv[:, q, :], psum[banks[2]][:, 0:T], cs[:, 0:T], ALU.mult).then_inc(stage3_vector_done, 1)
        for stage in later_stages["vector"]:
            stage(dve)

    @block.tensor
    def _(pe):
        pe.wait_ge(constants_made, 8)
        pe.wait_ge(silu_made, 2)
        for i in range(8):
            pe.wait_ge(wmod_loaded[i], 16)
            for k in range(KT):
                m = nc.tensor.matmul(psum[i // 2][0:2, 256 * (i % 2):256 * (i % 2) + 256], silu_col[:, k, :], wm[:, i, k, :],
                                     start=k == 0, stop=k == KT - 1)
            m.then_inc(mod_products, 1)
        pe.wait_ge(param_rows_loaded, 16 * 20)
        nc.tensor.transpose(psum[4][:, 0:24], prow[0:24, :], ident[0:24, 0:24]).then_inc(params_transposed, 1)
        nc.tensor.transpose(psum[5][:, 0:4 * NPAR], prow2[0:4 * NPAR, :], ident[0:4 * NPAR, 0:4 * NPAR]).then_inc(params_transposed, 1)
        for j in range(16):
            pe.wait_ge(mod_rows_moved, j // 4 + 1)
            m = nc.tensor.transpose(psum[6][:, 2 * j:2 * j + 2], modrow[0:2, P * j:P * j + P], ident[0:2, 0:2])
        m.then_inc(mod_products, 1)
        for t in range(NTC + NT):
            pe.wait_ge(normed_rows, t + 1)
            for h in range(2):
                if t >= 3:
                    pe.wait_ge([hT_lower, hT_upper][h], t - 2)
                elif t == 2:
                    pe.wait_ge(param_columns_made, 2)
                for k in range(4 * h, 4 * h + 4):
                    m = nc.tensor.transpose(psum[2 * (t % 3) + h][:, P * (k % 4):P * (k % 4) + P],
                                            xs[:, t, P * k:P * k + P], ident)
                m.then_inc(rows_transposed, 1)

        def project(j, bx, bc, loads):
            pe.wait_ge(win_loaded[j], loads)
            for k in range(KT):
                m = nc.tensor.matmul(psum[bx][:, 0:T], wring[:, j, k, :], hT[:, k, TC:TT], start=k == 0, stop=k == KT - 1)
                if bc is not None:
                    m = nc.tensor.matmul(psum[bc][:, 0:TC], wring[:, j, k, :], hT[:, k, 0:TC], start=k == 0, stop=k == KT - 1)
            m.then_inc(projections_made, 1)

        pe.wait_ge(hT_lower, 6)
        pe.wait_ge(hT_upper, 6)
        project(0, 0, 1, 16)
        project(1, 2, 3, 16)
        project(2, 4, None, 16)

        def low_rank(d, which, bx=5, bc=6):
            src = [lo_w, lo_a][which]
            nc.tensor.matmul(psum[bx][:, 0:T], lora[:, d, which, :], src[:, TC:TT], start=True, stop=True)
            nc.tensor.matmul(psum[bc][:, 0:TC], lora[:, d, which, :], src[:, 0:TC], start=True, stop=True).then_inc(aux_products, 1)

        def pair(p, first):
            pe.wait_ge(projections_evacuated, 3 * p + 3)
            if not first:
                pe.wait_ge(aux_evacuated, 6 * p - 2)
            project(0, 0, 1, 16 * p + 32)
            pe.wait_ge(lora_loaded, 80 * p + 80)
            if not first:
                pe.wait_ge(aux_evacuated, 6 * p)
            low_rank(0, 0)
            if not first:
                pe.wait_ge(aux_evacuated, 6 * p)
            project(1, 2, None, 16 * p + 32)
            pe.wait_ge(aux_evacuated, 6 * p + 1)
            low_rank(0, 1)
            project(2, 3, 4, 16 * p + 32)
            pe.wait_ge(aux_evacuated, 6 * p + 2)
            pe.wait_ge(kk_ready, p + 1)
            nc.tensor.matmul(psum[5][:, 0:T], head_ones, sqk[:, TC:TT], start=True, stop=True)
            nc.tensor.matmul(psum[6][:, 0:TC], head_ones, sqk[:, 0:TC], start=True, stop=True).then_inc(aux_products, 1)
            pe.wait_ge(projections_evacuated, 3 * p + 4)
            low_rank(1, 0, 0, 1)
            pe.wait_ge(projections_evacuated, 3 * p + 5)
            nc.tensor.matmul(psum[2][:, 0:T], gw, lo_g, start=True, stop=True).then_inc(aux_products, 1)
            pe.wait_ge(aux_evacuated, 6 * p + 3)
            low_rank(1, 1)
            pe.wait_ge(bonus_product_in, p + 1)
            if not first:
                pe.wait_ge(bonus_made, p)
            nc.tensor.matmul(psum[7][:, 0:T], head_ones, rk, start=True, stop=True).then_inc(aux_products, 1)

        pair(0, True)
        with pe.Fori(1, PAIRS) as p:
            pair(p, False)
        pe.wait_ge(projections_evacuated, 3 * PAIRS + 3)
        pe.wait_ge(aux_evacuated, 6 * PAIRS - 1)
        credit(pe, stage3_vector_done, 2)
        with pe.Fori(0, PAIRS // 2) as qq:
            for e in range(2):
                q = 2 * qq + e
                pe.wait_ge(stage3_vector_done, q + 1)
                if e:
                    pe.wait_ge(aux_evacuated, 6 * PAIRS)
                    pe.wait_ge(bonus_made, PAIRS)
                for j in range(3):
                    project(j, CONV_BANKS[e][j], None, q * 16 + 16 * (PAIRS + 2))
        for stage in later_stages["tensor"]:
            stage(pe)


_INS = ['x', 'c', 'ctx', 'c_ctx', 'w_mod', 'b_mod', 'norm_gains', 'w_in', 'w_out', 'conv_w', 'tshift_mu',
        'decay_w0', 'decay_w2', 'iclr_a0', 'iclr_a2', 'gate_w2', 'k_k', 'k_a', 'r_k', 'lnx_g', 'lnx_b',
        'peer_wq', 'peer_subkeys', 'peer_u', 'peer_v']
_OUTS = [((1, 512, 1024), 'float32')]


def kernel(**inputs):
    import numpy as _np
    import concourse.bacc as _bacc
    from concourse import mybir as _mybir
    from concourse.bass_utils import run_bass_kernel_spmd as _run

    nc = _bacc.Bacc("TRN2", target_bir_lowering=False, num_devices=1)
    arrays, args = {}, []
    for name in _INS:
        a = _np.ascontiguousarray(inputs[name])
        if a.dtype.kind in "iu":
            a = a.astype(_np.int64)
        arrays[f"in_{name}_dram"] = a
        args.append(nc.dram_tensor(f"in_{name}_dram", a.shape, _mybir.dt.from_np(a.dtype), kind="ExternalInput").ap())
    for i, (shape, dtype) in enumerate(_OUTS):
        dt = _mybir.dt.from_np(_np.dtype(dtype))
        args.append(nc.dram_tensor(f"out_{i}_dram", shape, dt, kind="ExternalOutput").ap())
    layer(nc, *args)
    r = _run(nc, [arrays], core_ids=[0])
    got = tuple(r.results[0][f"out_{i}_dram"] for i in range(len(_OUTS)))
    return got[0]
```
